# Optimizing a Trainium2 kernel written in Bass

```python
import jax, jax.numpy as jnp
from jax import lax
import numpy as np

D_MODEL = 1024
BATCH = 1
SEQ = 512
DEPTH = 1

SC_WIDTH = 512
SC_GROUPS = 4
SC_KERNEL = 3
DN_HEADS = 8
DN_DK = 64
DN_DV = 64
DN_KEY = DN_HEADS * DN_DK
DN_VAL = DN_HEADS * DN_DV
DN_CONV = 4
DN_CHUNK = 64
PEER_HEADS = 8
PEER_NKEYS = 128
PEER_EXPERTS = PEER_NKEYS * PEER_NKEYS
PEER_QDIM = 256
PEER_HALF = PEER_QDIM // 2
PEER_TOPK = 16
PEER_BLOCK = 128
NORM_EPS = 1e-6

IN_SIZES = (SC_WIDTH, SC_WIDTH, SC_WIDTH, DN_KEY, DN_KEY, DN_VAL, DN_VAL,
            DN_HEADS, DN_HEADS, D_MODEL, D_MODEL)
IN_COLS = 3 * SC_WIDTH + 2 * DN_KEY + 2 * DN_VAL + 2 * DN_HEADS + 2 * D_MODEL

kernel_name = "hybrid_conv_deltanet_peer_block"

def rmsnorm(x, w):
    xf = x.astype(jnp.float32)
    y = xf * lax.rsqrt(jnp.mean(xf * xf, axis=-1, keepdims=True) + NORM_EPS)
    return (y * w.astype(jnp.float32)).astype(x.dtype)

def l2norm(x):
    return x * lax.rsqrt(jnp.sum(x * x, axis=-1, keepdims=True) + NORM_EPS)

def split_cols(t, sizes):
    outs, start = [], 0
    for s in sizes:
        outs.append(t[..., start:start + s])
        start += s
    return outs

def causal_dwconv(x, w):
    K = w.shape[0]
    T = x.shape[1]
    xp = jnp.pad(x, ((0, 0), (K - 1, 0), (0, 0)))
    acc = xp[:, 0:T] * w[0]
    for k in range(1, K):
        acc = acc + xp[:, k:k + T] * w[k]
    return acc

def gated_delta_rule(q, k, v, g, beta):
    B, T, H, dk = q.shape
    dv = v.shape[-1]
    C = DN_CHUNK
    n = T // C

    def to_chunks(t):
        return jnp.moveaxis(t.reshape((B, n, C) + t.shape[2:]), 3, 1)

    qc, kc, vc, gc, bc = (to_chunks(t) for t in (q, k, v, g, beta))
    G = jnp.cumsum(gc, axis=-1)
    incl = jnp.tril(jnp.ones((C, C), dtype=bool))
    strict = jnp.tril(jnp.ones((C, C), dtype=bool), -1)
    diff = G[..., :, None] - G[..., None, :]
    decay = jnp.where(incl, jnp.exp(jnp.where(incl, diff, 0.0)), 0.0)
    kb = kc * bc[..., None]
    vb = vc * bc[..., None]
    L = jnp.einsum('bhnid,bhnjd->bhnij', kb, kc) * jnp.where(strict, decay, 0.0)
    eye = jnp.eye(C, dtype=L.dtype)
    rhs = jnp.concatenate([vb, kb * jnp.exp(G)[..., None]], axis=-1)
    sol = lax.linalg.triangular_solve(eye + L, rhs, left_side=True, lower=True,
                                      unit_diagonal=True)
    u, w = sol[..., :dv], sol[..., dv:]
    a_qk = jnp.einsum('bhnid,bhnjd->bhnij', qc, kc) * decay
    qg = qc * jnp.exp(G)[..., None]
    kdec = kc * jnp.exp(G[..., -1:] - G)[..., None]
    glast = jnp.exp(G[..., -1])

    xs = tuple(jnp.moveaxis(t, 2, 0) for t in (u, w, qg, a_qk, kdec, glast))

    def step(S, inp):
        u_n, w_n, qg_n, a_n, kd_n, gl_n = inp
        v_new = u_n - jnp.einsum('bhck,bhkv->bhcv', w_n, S)
        o = jnp.einsum('bhck,bhkv->bhcv', qg_n, S) + jnp.einsum('bhij,bhjv->bhiv', a_n, v_new)
        S = S * gl_n[..., None, None] + jnp.einsum('bhck,bhcv->bhkv', kd_n, v_new)
        return S, o

    S0 = jnp.zeros((B, H, dk, dv), dtype=q.dtype)
    _, o = lax.scan(step, S0, xs)
    return o.transpose(1, 0, 3, 2, 4).reshape(B, T, H, dv)

def token_mixer(h, w_in, sc_conv_w, dn_conv_w, dn_a_log, dn_dt_bias, dn_out_norm,
                w_sc_out, w_dn_out, w_mix_out):
    B, T, _ = h.shape
    proj = h @ w_in
    (sc_b, sc_c, sc_x, dn_q, dn_k, dn_v, dn_z, dn_a, dn_b,
     gate_sc, gate_dn) = split_cols(proj, IN_SIZES)

    br_sc = (sc_b * causal_dwconv(sc_c * sc_x, sc_conv_w)) @ w_sc_out

    qkv = jax.nn.silu(causal_dwconv(jnp.concatenate([dn_q, dn_k, dn_v], axis=-1), dn_conv_w))
    q, k, v = split_cols(qkv.astype(jnp.float32), (DN_KEY, DN_KEY, DN_VAL))
    q = l2norm(q.reshape(B, T, DN_HEADS, DN_DK)) * (DN_DK ** -0.5)
    k = l2norm(k.reshape(B, T, DN_HEADS, DN_DK))
    v = v.reshape(B, T, DN_HEADS, DN_DV)
    beta = jax.nn.sigmoid(dn_b.astype(jnp.float32))
    g = -jnp.exp(dn_a_log.astype(jnp.float32)) * jax.nn.softplus(
        dn_a.astype(jnp.float32) + dn_dt_bias.astype(jnp.float32))
    o = gated_delta_rule(q, k, v, g, beta)
    z = dn_z.astype(jnp.float32).reshape(B, T, DN_HEADS, DN_DV)
    o = (rmsnorm(o, dn_out_norm) * jax.nn.silu(z)).astype(h.dtype).reshape(B, T, DN_VAL)
    br_dn = o @ w_dn_out

    merged = jax.nn.sigmoid(gate_sc) * br_sc + jax.nn.sigmoid(gate_dn) * br_dn
    return merged @ w_mix_out

def peer(h, w_q, sub_keys, u_tab, v_tab):
    B, T, D = h.shape
    K = PEER_TOPK
    q = (h @ w_q).reshape(B, T, PEER_HEADS, 2, PEER_HALF)
    s = jnp.einsum('bthpd,hpnd->bthpn', q, sub_keys).astype(jnp.float32)
    v1, i1 = lax.top_k(s[..., 0, :], K)
    v2, i2 = lax.top_k(s[..., 1, :], K)
    cand = (v1[..., :, None] + v2[..., None, :]).reshape(B, T, PEER_HEADS, K * K)
    cidx = (i1[..., :, None] * PEER_NKEYS + i2[..., None, :]).reshape(B, T, PEER_HEADS, K * K)
    top_s, pos = lax.top_k(cand, K)
    eidx = jnp.take_along_axis(cidx, pos, axis=-1)
    gates = jax.nn.softmax(top_s, axis=-1)
    E = PEER_HEADS * K
    eidx = eidx.reshape(B, T, E)
    gates = gates.reshape(B, T, E).astype(h.dtype)
    nb = T // PEER_BLOCK

    def blk(t):
        return jnp.moveaxis(t.reshape((B, nb, PEER_BLOCK) + t.shape[2:]), 1, 0)

    def expert_block(args):
        hb, ib, gb = args
        u = jnp.take(u_tab, ib, axis=0)
        act = jax.nn.gelu(jnp.einsum('btd,bted->bte', hb, u), approximate=False)
        vv = jnp.take(v_tab, ib, axis=0)
        return jnp.einsum('bte,bted->btd', gb * act, vv)

    out = lax.map(expert_block, (blk(h), blk(eidx), blk(gates)))
    return jnp.moveaxis(out, 0, 1).reshape(B, T, D)

def setup_inputs(seed: int = 0) -> dict:
    key = jax.random.key(seed)
    ks = jax.random.split(key, 24)
    D = D_MODEL
    nrm = jax.random.normal
    f32 = jnp.float32
    dt = jnp.exp(jax.random.uniform(ks[9], (DEPTH, DN_HEADS), f32,
                                    np.log(1e-3).astype(np.float32), np.log(1e-1).astype(np.float32)))
    return {
        "x": nrm(ks[0], (BATCH, SEQ, D), f32),
        "c": nrm(ks[1], (BATCH, D), f32),
        "w_ada": nrm(ks[2], (DEPTH, D, 6 * D), f32) * (0.5 * D ** -0.5),
        "b_ada": nrm(ks[3], (DEPTH, 6 * D), f32) * 0.01,
        "norm_pre_mix": 1.0 + 0.05 * nrm(ks[4], (DEPTH, D), f32),
        "norm_post_mix": 1.0 + 0.05 * nrm(ks[5], (DEPTH, D), f32),
        "w_in_mix": nrm(ks[6], (DEPTH, D, IN_COLS), f32) * D ** -0.5,
        "sc_conv_w": nrm(ks[7], (DEPTH, SC_KERNEL, SC_WIDTH), f32) * SC_KERNEL ** -0.5,
        "dn_conv_w": nrm(ks[8], (DEPTH, DN_CONV, 2 * DN_KEY + DN_VAL), f32) * DN_CONV ** -0.5,
        "dn_a_log": jnp.log(jax.random.uniform(ks[10], (DEPTH, DN_HEADS), f32, 1.0, 16.0)),
        "dn_dt_bias": dt + jnp.log(-jnp.expm1(-dt)),
        "dn_out_norm": 1.0 + 0.05 * nrm(ks[11], (DEPTH, DN_DV), f32),
        "w_sc_out": nrm(ks[12], (DEPTH, SC_WIDTH, D), f32) * SC_WIDTH ** -0.5,
        "w_dn_out": nrm(ks[13], (DEPTH, DN_VAL, D), f32) * DN_VAL ** -0.5,
        "w_mix_out": nrm(ks[14], (DEPTH, D, D), f32) * D ** -0.5,
        "norm_pre_ffn": 1.0 + 0.05 * nrm(ks[15], (DEPTH, D), f32),
        "norm_post_ffn": 1.0 + 0.05 * nrm(ks[16], (DEPTH, D), f32),
        "peer_w_q": nrm(ks[17], (DEPTH, D, PEER_HEADS * PEER_QDIM), f32) * D ** -0.5,
        "peer_sub_keys": nrm(ks[18], (DEPTH, PEER_HEADS, 2, PEER_NKEYS, PEER_HALF), f32) * PEER_HALF ** -0.5,
        "peer_u": nrm(ks[19], (PEER_EXPERTS, D), f32) * D ** -0.5,
        "peer_v": nrm(ks[20], (PEER_EXPERTS, D), f32) * (PEER_HEADS * PEER_TOPK) ** -0.5,
    }

def reference(x, c, w_ada, b_ada, norm_pre_mix, norm_post_mix, w_in_mix, sc_conv_w,
              dn_conv_w, dn_a_log, dn_dt_bias, dn_out_norm, w_sc_out, w_dn_out, w_mix_out,
              norm_pre_ffn, norm_post_ffn, peer_w_q, peer_sub_keys, peer_u, peer_v):
    for l in range(DEPTH):
        mod = jax.nn.silu(c) @ w_ada[l] + b_ada[l]
        sh1, sc1, gt1, sh2, sc2, gt2 = jnp.split(mod[:, None, :], 6, axis=-1)
        h = rmsnorm(x, norm_pre_mix[l]) * (1.0 + sc1) + sh1
        y = token_mixer(h, w_in_mix[l], sc_conv_w[l], dn_conv_w[l], dn_a_log[l],
                        dn_dt_bias[l], dn_out_norm[l], w_sc_out[l], w_dn_out[l], w_mix_out[l])
        x = x + gt1 * rmsnorm(y, norm_post_mix[l])
        h = rmsnorm(x, norm_pre_ffn[l]) * (1.0 + sc2) + sh2
        y = peer(h, peer_w_q[l], peer_sub_keys[l], peer_u, peer_v)
        x = x + gt2 * rmsnorm(y, norm_post_ffn[l])
    return x


_drawn_inputs = setup_inputs


def setup_inputs(seed=0):
    import zlib

    import numpy as np

    out = dict(_drawn_inputs(seed))
    spreads = {}
    factors = {'norm_post_ffn': 4.041}
    for name, (base, spread) in spreads.items():
        noise = np.random.default_rng([zlib.crc32(name.encode()), seed]).standard_normal(out[name].shape)
        drawn = base * np.exp(spread * noise) if base else spread * noise
        out[name] = __import__('jax').numpy.asarray(drawn.astype(out[name].dtype))
    for name, factor in factors.items():
        out[name] = (out[name] * factor).astype(out[name].dtype)
    return out
```

```python
from contextlib import ExitStack

import numpy as np

import concourse.bass as bass
from concourse import mybir

F32 = mybir.dt.float32
BF16 = mybir.dt.bfloat16
U32 = mybir.dt.uint32
ALU = mybir.AluOpType
ACT = mybir.ActivationFunctionType
AX = mybir.AxisListType

P = 128
T = 512
D = 1024
TT = T // P
KT = D // P
H, DK = 8, 64
HJ = H // 2
CH = 64
EPS = 1e-6
MOD = 6 * KT
SH1, SC1, GT1, SH2, SC2, GT2 = (KT * n for n in range(6))
N_SC, N_QKV, N_Z = 12, 12, 4
N_PROJ = N_SC + N_QKV + N_Z
NEG = -1e30
PH, TOPK, NKEYS = 8, 16, 128
EXP_TILES = NKEYS


class Steps:

    def __init__(self, sem, names, base=0):
        self.sem, self.base, self.at = sem, base, {n: i + 1 for i, n in enumerate(names)}
        assert len(self.at) == len(names)
        self.names, self.n = names, 0

    def after(self, name, it=0, back=0):
        value = self.base + self.at[name] - back * len(self.names)
        assert value > 0 or (back and not isinstance(it, int)), (name, value)
        return self.sem, it * len(self.names) + value

    def step(self, name):
        assert self.names[self.n % len(self.names)] == name, (name, self.names[self.n % len(self.names)])
        self.n += 1
        return self.sem, 1


def constants():
    i, j = np.arange(P)[:, None], np.arange(P)[None, :]
    chunk = i // CH == j // CH
    near = i // 16 == j // 16
    parts = {
        "ident": i == j,
        "headsum": i // DK == j // DK,
        "ones": np.ones((P, P)),
        "neg_near": -1.0 * (near & (j < i)),
        "neg_far": -1.0 * (chunk & ~near & (j < i)),
        "neg_nearT": -1.0 * (near & (i < j)),
        "neg_farT": -1.0 * (chunk & ~near & (i < j)),
        "causal": np.where(chunk & (j <= i), 0.0, NEG),
        "causalT": np.where(chunk & (i <= j), 0.0, NEG),
        "iota": np.broadcast_to(j, (P, P)),
    }
    wide = np.concatenate([v.astype(np.float32) for v in parts.values()], axis=1)
    h = np.arange(H)[:, None]
    m = np.arange(P)[None, :]
    sel_head = np.stack([np.broadcast_to(h == n, (H, P)) for n in range(H)], 1)
    sel_pair = np.stack([h == 2 * n + m // DK for n in range(HJ)], 1)
    carry = np.broadcast_to(np.arange(T)[None, :] % CH != 0, (H, T))
    small = np.concatenate([a.reshape(H, -1).astype(np.float32) for a in (sel_head, sel_pair, carry)], 1)
    return list(parts), np.ascontiguousarray(wide), np.ascontiguousarray(small)


def program(nc, a, out, spill, upto=9, dbg=None):
    top = ExitStack()
    const_names = constants()[0]

    def dump(view):
        with nc.semaphore("dumped") as s, nc.Block() as block:
            @block.sync
            def _(sp):
                sp.dma_start(dbg, view).then_inc(s, 16)
                sp.wait_ge(s, 16)

    with top:
        def sb(ctx, name, shape, dt=F32):
            return ctx.enter_context(nc.sbuf_tensor(name, shape, dt))

        def sem(ctx, name):
            return ctx.enter_context(nc.semaphore(name))

        bank = [top.enter_context(nc.psum_tensor(f"bank{i}", [P, 512], F32)) for i in range(8)]
        cst = sb(top, "cst", [P, len(const_names), P])
        C = {n: cst[:, i, :] for i, n in enumerate(const_names)}
        small = sb(top, "small", [H, 12 * P + T])
        sel_head = small[:, 0:8 * P].rearrange("h (n m) -> h n m", n=H)
        sel_pair = small[:, 8 * P:12 * P].rearrange("h (n m) -> h n m", n=HJ)
        carry = small[:, 12 * P:12 * P + T]
        eps = sb(top, "eps", [P, 1])
        mod = sb(top, "mod", [P, MOD])
        norms = sb(top, "norms", [P, 4, KT])
        x_tok = sb(top, "x_tok", [P, TT, D])
        hT = sb(top, "hT", [P, KT, T])
        stat = sb(top, "stat", [P, 4, TT])

        row_ffn = sb(top, "row_ffn", [P, D])
        env = dict(locals())
        mix = ExitStack()
        with mix:
            env["qkvT"] = sb(mix, "qkvT", [P, 12, T])
            env["zT"] = sb(mix, "zT", [P, HJ, T])
            env["scT"] = sb(mix, "scT", [P, HJ, T])
            env["abT"] = sb(mix, "abT", [H, 2, T])
            env["dt_bias"] = sb(mix, "dt_bias", [H, 1])
            env["a_log"] = sb(mix, "a_log", [H, 1])
            env["out_norm"] = sb(mix, "out_norm", [P, 1])
            project_stage(nc, a, env)
            if upto == 1:
                return dump({"mod": mod[:], "hT": hT[:], "qkvT": env["qkvT"][:], "scT": env["scT"][:], "zT": env["zT"][:], "abT": env["abT"][:]}[dbg.name.split("_", 1)[1]])
            delta_stage(nc, a, env)
            if upto == 2:
                return dump({"qkvT": env["qkvT"][:], "zT": env["zT"][:]}[dbg.name.split("_", 1)[1]])
            merge_stage(nc, a, env)
            if upto == 3:
                return dump({"hT": hT[:], "x": x_tok[:], "row": row_ffn[:]}[dbg.name.split("_", 1)[1]])
        pick = ExitStack()
        with pick:
            env["idxT"] = sb(pick, "idxT", [P, 2, T])
            env["gateT"] = sb(pick, "gateT", [P, 3, T])
            retrieve_stage(nc, a, env)
            if upto == 4:
                return dump({"idxT": env["idxT"][:], "gateT": env["gateT"][:]}[dbg.name.split("_", 1)[1]])
            scatter_stage(nc, a, env, spill)
        expert_stage(nc, a, env, spill, out)


def rms_scale(vec, act, V, A, stat, eps, tag, width):
    pass


def project_stage(nc, a, env):
    g = env
    bank, C, mod, norms, stat, eps = g["bank"], g["C"], g["mod"], g["norms"], g["stat"], g["eps"]
    x_tok, hT, qkvT, zT, scT, abT = g["x_tok"], g["hT"], g["qkvT"], g["zT"], g["scT"], g["abT"]
    sb, sem = g["sb"], g["sem"]
    AR, AW = 4, 256
    NA = 6 * D // AW
    NA1 = 2 * D // AW
    WR = 4
    with ExitStack() as ctx:
        ada = sb(ctx, "ada", [P, AR, KT, AW])
        wring = sb(ctx, "wring", [P, WR, KT, P])
        w_ab = sb(ctx, "w_ab", [P, KT, 2 * H])
        raw = sb(ctx, "raw", [P, WR, 3 + T])
        xn = sb(ctx, "xn", [P, TT, D])
        c_col = sb(ctx, "c_col", [P, KT])
        c_act = sb(ctx, "c_act", [P, 3, KT])
        b_ada = sb(ctx, "b_ada", [P, MOD])
        scale1 = sb(ctx, "scale1", [P, KT])
        sc_w = sb(ctx, "sc_w", [P, HJ, 3])
        dn_w = sb(ctx, "dn_w", [P, 12, 4])
        conv = sb(ctx, "conv", [P, 3, T])
        upad = sb(ctx, "upad", [P, 2 + T])
        acc = sb(ctx, "acc", [P, 2, T])

        s_c, s_const, s_x, s_small, s_wab = (sem(ctx, n) for n in ("c_landed", "const_landed", "x_landed", "small_landed", "wab_landed"))
        s_ada = [sem(ctx, f"ada_landed{i}") for i in range(AR)]
        s_w = [sem(ctx, f"w_landed{i}") for i in range(WR)]
        ada_used, w_used, raw_ready, raw_used = (sem(ctx, n) for n in ("ada_used", "w_used", "raw_ready", "raw_used"))
        conv_done, conv_taken = sem(ctx, "conv_done"), sem(ctx, "conv_taken")
        conv_chain = sem(ctx, "conv_chain")
        V = Steps(sem(ctx, "p_vector"), ["pads", "pads_u", "eps", "c_plus", "c_recip", "c_silu"]
                  + ["rstd"] + [f"xn{t}" for t in range(TT)] + ["mod1", "scale_p", "scale1"])
        A = Steps(sem(ctx, "p_scalar"), ["c_exp"] + [f"sq{t}" for t in range(TT)] + ["std"] + [f"h{k}" for k in range(KT)])
        E = Steps(sem(ctx, "p_tensor"), [f"xT{k}" for k in range(KT)])
        proj_done, ab_done, mod_done = sem(ctx, "proj_done"), sem(ctx, "ab_done"), sem(ctx, "mod_done")
        last_v = sem(ctx, "p_last")

        mod_ps = bank[0]
        xT_ps = bank[1:3]
        proj_ps = bank[3:7]
        ab_ps = [bank[1], bank[2]]

        with nc.Block() as block:
            @block.sync
            def _(sp):
                sp.dma_start(c_col[:], a["c_col"]).then_inc(s_c, 16)
                for t in range(TT):
                    sp.dma_start(x_tok[:, t, :], a["x"][t * P:(t + 1) * P, :]).then_inc(s_x, 16)

                def load_ada(n):
                    if n >= AR:
                        sp.wait_ge(ada_used, n - AR + 1)
                    sp.dma_start(ada[:, n % AR, :, :], a["w_ada"][n]).then_inc(s_ada[n % AR], 16)

                for n in range(AR):
                    load_ada(n)
                sp.dma_start(g["cst"][:], a["wide"]).then_inc(s_const, 16)
                for dst, name in ((g["small"][:], "narrow"), (b_ada[:], "b_ada"), (norms[:], "norms"), (sc_w[:], "sc_w"),
                                  (dn_w[:], "dn_w"), (g["dt_bias"][:], "dt_bias"), (g["a_log"][:], "a_log"),
                                  (g["out_norm"][:], "out_norm")):
                    sp.dma_start(dst, a[name]).then_inc(s_small, 16)
                for n in range(AR, NA1):
                    load_ada(n)
                for n in range(WR):
                    sp.dma_start(wring[:, n], a["w_proj"][n]).then_inc(s_w[n], 16)
                sp.dma_start(w_ab[:], a["w_ab"]).then_inc(s_wab, 16)
                with sp.Fori(1, N_PROJ // WR) as i:
                    for b in range(WR):
                        sp.wait_ge(w_used, i * WR + (b + 1 - WR))
                        sp.dma_start(wring[:, b], a["w_proj"][i * WR + b]).then_inc(s_w[b], 16)
                for n in range(NA1, NA):
                    load_ada(n)

            def mod_piece(pe, n):
                pe.wait_ge(s_ada[n % AR], 16 * (n // AR + 1))
                for m in range(AW // P):
                    col = n * (AW // P) + m
                    for k in range(KT):
                        last = nc.tensor.matmul(mod_ps[:, col:col + 1], ada[:, n % AR, k, m * P:(m + 1) * P],
                                                c_act[:, 2, k:k + 1], start=(k == 0), stop=(k == KT - 1))
                return last

            @block.tensor
            def _(pe):
                pe.wait_ge(*V.after("c_silu"))
                for n in range(NA1):
                    mod_piece(pe, n).then_inc(ada_used, 1)
                pe.wait_ge(s_const, 16)
                pe.wait_ge(*V.after(f"xn{TT - 1}"))
                for k in range(KT):
                    if k >= 2:
                        pe.wait_ge(*A.after(f"h{k - 2}"))
                    for t in range(TT):
                        last = nc.tensor.transpose(xT_ps[k % 2][:, t * P:(t + 1) * P], xn[:, t, k * P:(k + 1) * P], C["ident"])
                    last.then_inc(*E.step(f"xT{k}"))
                pe.wait_ge(*A.after(f"h{KT - 1}"))
                with pe.Fori(0, N_PROJ // WR) as i:
                    for b in range(WR):
                        pe.wait_ge(s_w[b], i * 16 + 16)
                        pe.wait_ge(raw_ready, i * WR + (b + 1))
                        for k in range(KT):
                            last = nc.tensor.matmul(proj_ps[b][:], wring[:, b, k, :], hT[:, k, :], start=(k == 0), stop=(k == KT - 1))
                        last.then_inc(w_used, 1)
                pe.wait_ge(s_wab, 16)
                for n in range(2):
                    for k in range(KT):
                        last = nc.tensor.matmul(ab_ps[n][0:H, :], w_ab[:, k, n * H:(n + 1) * H], hT[:, k, :], start=(k == 0), stop=(k == KT - 1))
                    last.then_inc(ab_done, 1)
                for n in range(NA1, NA):
                    mod_piece(pe, n).then_inc(ada_used, 1)

            @block.gpsimd
            def _(pool):
                pool.sem_inc(raw_ready, WR)
                pool.sem_inc(conv_taken, 2)

            @block.scalar
            def _(act):
                act.wait_ge(s_c, 16)
                nc.scalar.activation(c_act[:, 0, :], c_col[:], ACT.Exp, scale=-1.0).then_inc(*A.step("c_exp"))
                for t in range(TT):
                    act.wait_ge(s_x, 16 * TT)
                    nc.scalar.activation(xn[:, t, :], x_tok[:, t, :], ACT.Square, accum_out=stat[:, 0, t:t + 1]).then_inc(*A.step(f"sq{t}"))
                act.wait_ge(*A.after(f"sq{TT - 1}"))
                act.wait_ge(*V.after("eps"))
                nc.scalar.activation(stat[:, 1, :], stat[:, 0, :], ACT.Sqrt, bias=eps[:], scale=1.0 / D).then_inc(*A.step("std"))
                act.wait_ge(*V.after("scale1"))
                for k in range(KT):
                    act.wait_ge(*E.after(f"xT{k}"))
                    nc.scalar.activation(hT[:, k, :], xT_ps[k % 2][:], ACT.Identity, bias=mod[:, SH1 + k:SH1 + k + 1],
                                         scale=scale1[:, k:k + 1]).then_inc(*A.step(f"h{k}"))

                def take(slot, done, free):
                    act.wait_ge(w_used, done)
                    if free is not None:
                        act.wait_ge(raw_used, free)
                    nc.scalar.activation(raw[:, slot, 3:3 + T], proj_ps[slot][:], ACT.Copy).then_inc(raw_ready, 1)

                act.wait_ge(*V.after("pads"))
                for b in range(WR):
                    take(b, b + 1, None)
                with act.Fori(1, N_SC // WR) as i:
                    for b in range(WR):
                        take(b, i * WR + (b + 1), i * WR + (b + 1 - WR))
                with act.Fori(N_SC // WR, (N_SC + N_QKV) // WR) as i:
                    for b in range(WR):
                        take(b, i * WR + (b + 1), i * WR + (b + 1 - WR))
                        act.wait_ge(conv_done, i * WR + (b + 1 - N_SC))
                        nc.scalar.activation(qkvT[:, i * WR + (b - N_SC), :], acc[:, b % 2, :], ACT.Silu).then_inc(conv_taken, 1)
                for b in range(N_Z):
                    act.wait_ge(w_used, N_SC + N_QKV + b + 1)
                    nc.scalar.activation(zT[:, b, :], proj_ps[b][:], ACT.Silu).then_inc(raw_ready, 1)

            @block.vector
            def _(dve):
                nc.vector.memset(raw[:, :, 0:3], 0.0).then_inc(*V.step("pads"))
                nc.vector.memset(upad[:, 0:2], 0.0).then_inc(*V.step("pads_u"))
                nc.vector.memset(eps[:], EPS).then_inc(*V.step("eps"))
                dve.wait_ge(*A.after("c_exp"))
                nc.vector.tensor_scalar(c_act[:, 1, :], c_act[:, 0, :], 1.0, None, ALU.add).then_inc(*V.step("c_plus"))
                dve.wait_ge(*V.after("c_plus"))
                nc.vector.reciprocal(c_act[:, 0, :], c_act[:, 1, :]).then_inc(*V.step("c_recip"))
                dve.wait_ge(*V.after("c_recip"))
                nc.vector.tensor_tensor(c_act[:, 2, :], c_act[:, 0, :], c_col[:], ALU.mult).then_inc(*V.step("c_silu"))
                dve.wait_ge(*A.after("std"))
                nc.vector.reciprocal(stat[:, 2, :], stat[:, 1, :]).then_inc(*V.step("rstd"))
                dve.wait_ge(*V.after("rstd"))
                for t in range(TT):
                    nc.vector.tensor_scalar(xn[:, t, :], x_tok[:, t, :], stat[:, 2, t:t + 1], None, ALU.mult).then_inc(*V.step(f"xn{t}"))
                dve.wait_ge(ada_used, NA1)
                dve.wait_ge(s_small, 16 * 8)
                nc.vector.tensor_tensor(mod[:, SH1:SC1 + KT], mod_ps[:, SH1:SC1 + KT], b_ada[:, SH1:SC1 + KT], ALU.add).then_inc(*V.step("mod1"))
                dve.wait_ge(*V.after("mod1"))
                nc.vector.tensor_scalar(scale1[:], mod[:, SC1:SC1 + KT], 1.0, None, ALU.add).then_inc(*V.step("scale_p"))
                dve.wait_ge(*V.after("scale_p"))
                nc.vector.tensor_tensor(scale1[:], scale1[:], norms[:, 0, :], ALU.mult).then_inc(*V.step("scale1"))

                n_chain = 0
                for j in range(N_SC // 3):
                    c, x, b = (3 * j + m for m in range(3))
                    dve.wait_ge(raw_ready, WR + x + 1)
                    nc.vector.tensor_tensor(upad[:, 2:2 + T], raw[:, c % WR, 3:3 + T], raw[:, x % WR, 3:3 + T], ALU.mult).then_inc(raw_used, 2)
                    dve.wait_ge(raw_used, 3 * j + 2)
                    nc.vector.tensor_scalar(conv[:, 0, :], upad[:, 2:2 + T], sc_w[:, j, 2:3], None, ALU.mult).then_inc(conv_chain, 1)
                    for k in (1, 0):
                        n_chain += 1
                        dve.wait_ge(conv_chain, n_chain)
                        nc.vector.scalar_tensor_tensor(conv[:, 2 - k, :], upad[:, k:k + T], sc_w[:, j, k:k + 1], conv[:, 1 - k, :],
                                                       ALU.mult, ALU.add).then_inc(conv_chain, 1)
                    n_chain += 1
                    dve.wait_ge(conv_chain, n_chain)
                    dve.wait_ge(raw_ready, WR + b + 1)
                    nc.vector.tensor_tensor(scT[:, j, :], conv[:, 2, :], raw[:, b % WR, 3:3 + T], ALU.mult).then_inc(raw_used, 1)
                base = n_chain
                with dve.Fori(0, N_QKV // WR) as i:
                    for b in range(WR):
                        dve.wait_ge(raw_ready, i * WR + (WR + N_SC + b + 1))
                        chain = lambda k: i * (3 * WR) + (base + 3 * b + k)
                        nc.vector.tensor_scalar(conv[:, 0, :], raw[:, b, 3:3 + T], dn_w[:, i * WR + b, 3:4], None, ALU.mult).then_inc(conv_chain, 1)
                        dve.wait_ge(conv_chain, chain(1))
                        nc.vector.scalar_tensor_tensor(conv[:, 1, :], raw[:, b, 2:2 + T], dn_w[:, i * WR + b, 2:3], conv[:, 0, :],
                                                       ALU.mult, ALU.add).then_inc(conv_chain, 1)
                        dve.wait_ge(conv_chain, chain(2))
                        nc.vector.scalar_tensor_tensor(conv[:, 2, :], raw[:, b, 1:1 + T], dn_w[:, i * WR + b, 1:2], conv[:, 1, :],
                                                       ALU.mult, ALU.add).then_inc(conv_chain, 1)
                        dve.wait_ge(conv_chain, chain(3))
                        dve.wait_ge(conv_taken, i * WR + (b + 1))
                        nc.vector.scalar_tensor_tensor(acc[:, b % 2, :], raw[:, b, 0:T], dn_w[:, i * WR + b, 0:1], conv[:, 2, :],
                                                       ALU.mult, ALU.add).then_inc(conv_done, 1)
                        dve.wait_ge(conv_done, i * WR + (b + 1))
                        dve.sem_inc(raw_used, 1)
                for n in range(2):
                    dve.wait_ge(ab_done, n + 1)
                    nc.vector.tensor_copy(abT[:, n, :], ab_ps[n][0:H, :]).then_inc(last_v, 1)
                dve.wait_ge(ada_used, NA)
                nc.vector.tensor_tensor(mod[:, GT1:MOD], mod_ps[:, GT1:MOD], b_ada[:, GT1:MOD], ALU.add).then_inc(last_v, 1)


def delta_stage(nc, a, env):
    g_ = env
    bank, C, eps = g_["bank"], g_["C"], g_["eps"]
    qkvT, zT, abT = g_["qkvT"], g_["zT"], g_["abT"]
    sel_head, sel_pair, carry = g_["sel_head"], g_["sel_pair"], g_["carry"]
    sb, sem = g_["sb"], g_["sem"]
    G2 = range(2)
    with ExitStack() as ctx:
        sq = sb(ctx, "l2_square", [P, 2, T])
        nrm = sb(ctx, "l2_norm", [P, 2, T])
        ga = sb(ctx, "gate_work", [H, 8, T])
        rows = sb(ctx, "decay_rows", [H, 3, T])
        exp_a = sb(ctx, "exp_a", [H, 1])
        cols = sb(ctx, "decay_cols", [P, 3, TT, H])
        neg_g = sb(ctx, "neg_g", [P, TT, H])
        e_kd = sb(ctx, "e_kd", [P, TT, H])
        e_g = sb(ctx, "e_g", [P, TT, H])
        be_g = sb(ctx, "be_g", [P, TT, H])
        dec = sb(ctx, "decay", [P, 2, HJ, P])
        decT = sb(ctx, "decayT", [P, 2, HJ, P])
        kbT = sb(ctx, "kbT", [P, HJ, P])
        qgT = sb(ctx, "qgT", [P, HJ, P])
        egT = sb(ctx, "egT", [P, HJ, P])
        kdec = sb(ctx, "kdec", [P, H, DK])
        rw = sb(ctx, "rhs_w", [P, H, DK])
        rv = sb(ctx, "rhs_v", [P, H, DK])
        L, LT = (sb(ctx, n, [P, HJ, P]) for n in ("L", "LT"))
        aT = sb(ctx, "attnT", [P, 2, HJ, P])
        W = {(n, g): sb(ctx, f"{n}_{g}", [P, HJ, P]) for g in G2
             for n in ("A", "AT", "CT", "F", "B", "BT", "PT", "QT")}
        u = sb(ctx, "u", [P, 2, HJ, DK])
        wT = sb(ctx, "wT", [P, HJ, P])
        qkv = sb(ctx, "qkv_tile", [P, 12, P])
        S = sb(ctx, "state", [P, HJ, DK])
        Sd = sb(ctx, "state_decayed", [P, HJ, DK])
        vn = sb(ctx, "v_new", [P, 2, HJ, DK])
        oS = sb(ctx, "o_state", [P, 2, HJ, DK])
        o = sb(ctx, "o", [P, 2, HJ, DK])
        on = sb(ctx, "o_normed", [P, HJ, 2, DK])
        ost = sb(ctx, "o_stat", [P, 3, H])

        pre_v = ["a_bias", "a_max", "a_neg", "a_min", "b_plus", "beta", "softplus", "g", "G", "G_left", "cols", "neg_g", "be_g", "S0"]
        pre_v += ["sq0", "sq1"] + [x for j in range(8) for x in ([f"inv{j}", f"unit{j}"] + ([f"sq{j + 2}"] if j < 6 else []))]
        pre_a = ["exp_b", "exp_a", "exp_x", "log", "e_kd", "e_g"] + [f"norm{j}" for j in range(8)]
        pre_e = ["cols"] + [f"ss{j}" for j in range(8)]
        loop_v = ["pre0", "preT0", "pre1", "preT1", "kb", "kdec", "rw", "rv", "qg"]
        for g in G2:
            loop_v += [f"L{g}", f"LT{g}", f"aT{g}"]
        levels_v = ["P1", "P2", "P3", "P4", "MT", "Q1", "TT"]
        loop_v += [f"{x}{g}" for x in levels_v for g in G2] + ["u0", "u1"]
        for c in G2:
            loop_v += [f"Sd{c}", f"vn{c}0", f"vn{c}1", f"S{c}", f"o{c}"]
        loop_v += ["osq", "oss", "ostd", "on", "oT"]
        loop_a = ["egT"] + [f"dec{g}{j}" for g in G2 for j in range(HJ)] + [f"decT{g}{j}" for g in G2 for j in range(HJ)]
        loop_a += [f"{x}{g}" for x in ["A2", "A2T", "A4", "A4T", "A8", "P", "M", "M2"] for g in G2] + ["wT"]
        loop_a += ["oi00", "oi01", "oi10", "oi11", "ostd"]
        loop_p = ["tile"] + [f"{x}{g}" for g in G2 for x in ("near", "far", "nearT", "farT")]
        loop_e = ["grow0", "grow1", "betaT", "GT", "kX", "vX"] + [f"{x}{g}" for g in G2 for x in ("kk", "kkT", "qk")]
        loop_e += [f"{x}{g}" for x in ["A2", "A2T", "A4", "A4T", "PA2", "A8", "PA4", "PA8", "P", "M", "MT", "M2", "Q1", "TT"] for g in G2]
        loop_e += ["u0", "u1", "wT"]
        for c in G2:
            loop_e += [f"wS{c}0", f"wS{c}1", f"oi{c}0", f"oi{c}1", f"dS{c}", f"oa{c}"]
        loop_e += ["oT"]
        sv, sa, se, spl = (sem(ctx, f"dn_{n}") for n in ("vector", "scalar", "tensor", "pool"))
        V0, A0, E0 = Steps(sv, pre_v), Steps(sa, pre_a), Steps(se, pre_e)
        V, A, E = Steps(sv, loop_v, len(pre_v)), Steps(sa, loop_a, len(pre_a)), Steps(se, loop_e, len(pre_e))
        Q = Steps(spl, loop_p)
        held = sem(ctx, "held")

        def flat(t):
            return t.rearrange("p j m -> p (j m)")

        def mask(name):
            return C[name].unsqueeze(1).to_broadcast([P, HJ, P])

        def b4(n):
            return bank[n][:].rearrange("p (j m) -> p j m", j=HJ)

        with nc.Block() as block:
            @block.scalar
            def _(act):
                nc.scalar.activation(ga[:, 4, :], abT[:, 1, :], ACT.Exp, scale=-1.0).then_inc(*A0.step("exp_b"))
                nc.scalar.activation(exp_a[:], g_["a_log"][:], ACT.Exp).then_inc(*A0.step("exp_a"))
                act.wait_ge(*V0.after("a_min"))
                nc.scalar.activation(ga[:, 5, :], ga[:, 3, :], ACT.Exp).then_inc(*A0.step("exp_x"))
                act.wait_ge(*A0.after("exp_x"))
                nc.scalar.activation(ga[:, 6, :], ga[:, 5, :], ACT.Ln, bias=1.0).then_inc(*A0.step("log"))
                act.wait_ge(*V0.after("cols"))
                nc.scalar.activation(e_kd[:], cols[:, 2], ACT.Exp).then_inc(*A0.step("e_kd"))
                nc.scalar.activation(e_g[:], cols[:, 0], ACT.Exp).then_inc(*A0.step("e_g"))
                for j in range(8):
                    act.wait_ge(*E0.after(f"ss{j}"))
                    if j >= 2:
                        act.wait_ge(*V0.after(f"unit{j - 2}"))
                    nc.scalar.activation(nrm[:, j % 2, :], bank[j % 2][:], ACT.Sqrt, bias=eps[:]).then_inc(*A0.step(f"norm{j}"))
                with act.Fori(0, TT) as tt:
                    act.wait_ge(*E.after("GT", tt))
                    nc.scalar.activation(flat(egT[:]), bank[3][:], ACT.Exp).then_inc(*A.step("egT"))
                    for d, v, bias, name in ((dec, "pre", cols[:, 0], "dec"), (decT, "preT", neg_g[:], "decT")):
                        for g in G2:
                            act.wait_ge(*V.after(f"{v}{g}", tt))
                            for j in range(HJ):
                                h = 2 * j + g
                                nc.scalar.activation(d[:, g, j, :], d[:, g, j, :], ACT.Exp, bias=bias[:, tt, h:h + 1]).then_inc(*A.step(f"{name}{g}{j}"))

                    def take(name, dst, src, g):
                        act.wait_ge(*E.after(f"{name}{g}", tt))
                        nc.scalar.activation(flat(dst[:]), bank[src][:], ACT.Copy).then_inc(*A.step(f"{name}{g}"))

                    b0 = (4, 7)
                    b1 = (5, 0)
                    for name, dst, bs in (("A2", "B", b0), ("A2T", "BT", b1), ("A4", "A", b0), ("A4T", "AT", b1), ("A8", "B", b0),
                                          ("P", "BT", b0), ("M", "A", b1), ("M2", "B", b0)):
                        for g in G2:
                            if name == "A4T":
                                act.wait_ge(*V.after(f"P1{g}", tt))
                            take(name, W[dst, g], bs[g], g)
                    act.wait_ge(*E.after("wT", tt))
                    nc.scalar.activation(flat(wT[:]), bank[2][:], ACT.Copy).then_inc(*A.step("wT"))
                    for c in G2:
                        r = slice(CH * c, CH * c + CH)
                        for g in G2:
                            act.wait_ge(*E.after(f"oi{c}{g}", tt))
                            nc.scalar.activation(oS[r, g], bank[5 + g][r, 0:HJ * DK], ACT.Copy).then_inc(*A.step(f"oi{c}{g}"))
                    act.wait_ge(*V.after("oss", tt))
                    nc.scalar.activation(ost[:, 1, :], ost[:, 0, :], ACT.Sqrt, bias=eps[:], scale=1.0 / DK).then_inc(*A.step("ostd"))

            @block.gpsimd
            def _(pool):
                with pool.Fori(0, TT) as tt:
                    pool.wait_ge(*V.after("oT", tt, 1))
                    nc.gpsimd.tensor_copy(qkv[:], qkvT[:, :, bass.ds(tt * P, P)]).then_inc(*Q.step("tile"))
                    for g in G2:
                        pool.wait_ge(*V.after(f"L{g}", tt))
                        nc.gpsimd.tensor_tensor(W["A", g][:], L[:], mask("neg_near"), ALU.mult).then_inc(*Q.step(f"near{g}"))
                        nc.gpsimd.tensor_tensor(W["F", g][:], L[:], mask("neg_far"), ALU.mult).then_inc(*Q.step(f"far{g}"))
                        pool.wait_ge(*V.after(f"LT{g}", tt))
                        nc.gpsimd.tensor_tensor(W["AT", g][:], LT[:], mask("neg_nearT"), ALU.mult).then_inc(*Q.step(f"nearT{g}"))
                        nc.gpsimd.tensor_tensor(W["CT", g][:], LT[:], mask("neg_farT"), ALU.mult).then_inc(*Q.step(f"farT{g}"))

            @block.tensor
            def _(pe):
                pe.wait_ge(*V0.after("G_left"))
                for n in range(3):
                    for t in range(TT):
                        m = (n * TT + t) * H
                        last = nc.tensor.transpose(bank[2][:, m:m + H], rows[:, n, t * P:(t + 1) * P], C["ident"][0:H, 0:H])
                last.then_inc(*E0.step("cols"))
                for j in range(8):
                    pe.wait_ge(*V0.after(f"sq{j}"))
                    if j >= 2:
                        pe.wait_ge(*A0.after(f"norm{j - 2}"))
                    nc.tensor.matmul(bank[j % 2][:], C["headsum"], sq[:, j % 2, :], start=True, stop=True).then_inc(*E0.step(f"ss{j}"))
                pe.wait_ge(*V0.after("unit7"))
                pe.wait_ge(*A0.after("norm7"))
                pe.wait_ge(*V0.after("cols"))
                with pe.Fori(0, TT) as tt:
                    tok = bass.ds(tt * P, P)
                    pe.wait_ge(*V.after("oT", tt, 1))

                    def group(name, n, products, transpose=False):
                        for j in range(HJ):
                            lhs, rhs = products(j)
                            if transpose:
                                last = nc.tensor.transpose(bank[n][:, j * P:(j + 1) * P], lhs, C["ident"])
                            else:
                                last = nc.tensor.matmul(bank[n][:, j * P:(j + 1) * P], lhs, rhs, start=True, stop=True)
                        last.then_inc(*E.step(name))

                    for g in G2:
                        group(f"grow{g}", g, lambda j: (sel_head[:, 2 * j + g, :], rows[:, 0, tok]))
                    group("betaT", 2, lambda j: (sel_pair[:, j, :], rows[:, 1, tok]))
                    group("GT", 3, lambda j: (sel_pair[:, j, :], rows[:, 0, tok]))
                    pe.wait_ge(*Q.after("tile", tt))
                    group("kX", 4, lambda j: (qkv[:, HJ + j, :], None), transpose=True)
                    group("vX", 5, lambda j: (qkv[:, 2 * HJ + j, :], None), transpose=True)
                    pe.wait_ge(*V.after("kb", tt))
                    for g, banks in ((0, (6, 7, 0)), (1, (1, 2, 3))):
                        r = slice(DK * g, DK * g + DK)
                        if g == 1:
                            pe.wait_ge(*A.after("egT", tt))
                        group(f"kk{g}", banks[0], lambda j: (kbT[r, j, :], qkv[r, HJ + j, :]))
                        group(f"kkT{g}", banks[1], lambda j: (qkv[r, HJ + j, :], kbT[r, j, :]))
                        group(f"qk{g}", banks[2], lambda j: (qkv[r, HJ + j, :], qkv[r, j, :]))
                    b0, b1, b2 = (4, 7), (5, 0), (6, 1)

                    def level(name, banks, lhs, rhs, waits, transpose=False):
                        for g in G2:
                            for w in waits(g):
                                pe.wait_ge(*w)
                            group(f"{name}{g}", banks[g], lambda j: (W[lhs, g][:, j, :], rhs and W[rhs, g][:, j, :]), transpose)

                    VA, AA, PA = (lambda n: V.after(n, tt)), (lambda n: A.after(n, tt)), (lambda n: Q.after(n, tt))
                    level("A2", b0, "AT", "A", lambda g: [PA(f"nearT{g}"), VA("rv"), VA(f"LT{g}"), VA(f"aT{g}")])
                    level("A2T", b1, "A", "AT", lambda g: [])
                    level("A4", b0, "BT", "B", lambda g: [AA(f"A2{g}"), AA(f"A2T{g}")])
                    level("A4T", b1, "B", "BT", lambda g: [])
                    level("PA2", b2, "B", "PT", lambda g: [VA(f"P1{g}")])
                    level("A8", b0, "AT", "A", lambda g: [AA(f"A4{g}"), AA(f"A4T{g}")])
                    level("PA4", b2, "A", "PT", lambda g: [VA(f"P2{g}")])
                    level("PA8", b1, "B", "PT", lambda g: [AA(f"A8{g}"), VA(f"P3{g}")])
                    level("P", b0, "PT", None, lambda g: [VA(f"P4{g}")], transpose=True)
                    level("M", b1, "CT", "BT", lambda g: [PA(f"farT{g}"), AA(f"P{g}")])
                    level("MT", b2, "BT", "CT", lambda g: [])
                    level("M2", b0, "QT", "A", lambda g: [AA(f"M{g}"), VA(f"MT{g}")])
                    level("Q1", b1, "A", "PT", lambda g: [])
                    level("TT", b2, "B", "QT", lambda g: [AA(f"M2{g}"), VA(f"Q1{g}")])
                    for g in G2:
                        pe.wait_ge(*VA(f"TT{g}"))
                        for j in range(HJ):
                            last = nc.tensor.matmul(bank[b0[g]][:, j * DK:(j + 1) * DK], W["AT", g][:, j, :], rv[:, 2 * j + g, :], start=True, stop=True)
                        last.then_inc(*E.step(f"u{g}"))
                    for j in range(HJ):
                        for g in G2:
                            last = nc.tensor.matmul(bank[2][DK * g:DK * g + DK, j * P:(j + 1) * P], rw[:, 2 * j + g, :], W["AT", g][:, j, :], start=True, stop=True)
                    last.then_inc(*E.step("wT"))
                    for c in G2:
                        r = slice(CH * c, CH * c + CH)
                        if c == 0:
                            pe.wait_ge(*AA("wT"))
                            pe.wait_ge(*VA("u1"))
                        else:
                            pe.wait_ge(*VA("S0"))
                        pe.sem_inc(held, 1)
                        for g in G2:
                            q = slice(DK * g, DK * g + DK)
                            for j in range(HJ):
                                last = nc.tensor.matmul(bank[3 + g][r, j * DK:(j + 1) * DK], wT[q, j, r], S[q, j, :], start=True, stop=True)
                            last.then_inc(*E.step(f"wS{c}{g}"))
                        for g in G2:
                            q = slice(DK * g, DK * g + DK)
                            if c == 1:
                                pe.wait_ge(*AA(f"oi0{g}"))
                                pe.sem_inc(held, 1)
                            for j in range(HJ):
                                last = nc.tensor.matmul(bank[5 + g][r, j * DK:(j + 1) * DK], qgT[q, j, r], S[q, j, :], start=True, stop=True)
                            last.then_inc(*E.step(f"oi{c}{g}"))
                        pe.wait_ge(*VA(f"vn{c}1"))
                        pe.sem_inc(held, 1)
                        for j in range(HJ):
                            for g in G2:
                                last = nc.tensor.matmul(bank[0][DK * g:DK * g + DK, j * DK:(j + 1) * DK], kdec[r, 2 * j + g, :], vn[r, g, j, :], start=True, stop=True)
                        last.then_inc(*E.step(f"dS{c}"))
                        if c == 1:
                            pe.wait_ge(*VA("o0"))
                            pe.sem_inc(held, 1)
                        for g in G2:
                            for j in range(HJ):
                                m = (g * HJ + j) * DK
                                last = nc.tensor.matmul(bank[7][r, m:m + DK], aT[r, g, j, r], vn[r, g, j, :], start=True, stop=True)
                        last.then_inc(*E.step(f"oa{c}"))
                    pe.wait_ge(*VA("on"))
                    group("oT", 1, lambda j: (on[:, j].rearrange("p g d -> p (g d)"), None), transpose=True)

            @block.vector
            def _(dve):
                nc.vector.tensor_scalar(ga[:, 0, :], abT[:, 0, :], g_["dt_bias"][:], None, ALU.add).then_inc(*V0.step("a_bias"))
                dve.wait_ge(*V0.after("a_bias"))
                nc.vector.tensor_scalar(ga[:, 1, :], ga[:, 0, :], 0.0, None, ALU.max).then_inc(*V0.step("a_max"))
                nc.vector.tensor_scalar(ga[:, 2, :], ga[:, 0, :], -1.0, None, ALU.mult).then_inc(*V0.step("a_neg"))
                dve.wait_ge(*V0.after("a_neg"))
                nc.vector.tensor_tensor(ga[:, 3, :], ga[:, 0, :], ga[:, 2, :], ALU.min).then_inc(*V0.step("a_min"))
                dve.wait_ge(*A0.after("exp_b"))
                nc.vector.tensor_scalar(ga[:, 7, :], ga[:, 4, :], 1.0, None, ALU.add).then_inc(*V0.step("b_plus"))
                dve.wait_ge(*V0.after("b_plus"))
                nc.vector.reciprocal(rows[:, 1, :], ga[:, 7, :]).then_inc(*V0.step("beta"))
                dve.wait_ge(*A0.after("log"))
                nc.vector.tensor_tensor(ga[:, 0, :], ga[:, 1, :], ga[:, 6, :], ALU.add).then_inc(*V0.step("softplus"))
                dve.wait_ge(*V0.after("softplus"))
                nc.vector.tensor_scalar(ga[:, 2, :], ga[:, 0, :], exp_a[:], -1.0, ALU.mult, ALU.mult).then_inc(*V0.step("g"))
                dve.wait_ge(*V0.after("g"))
                nc.vector.tensor_tensor_scan(rows[:, 0, :], carry, ga[:, 2, :], 0.0, ALU.mult, ALU.add).then_inc(*V0.step("G"))
                dve.wait_ge(*V0.after("G"))
                by_chunk = rows[:, 0, :].rearrange("h (n c) -> h n c", c=CH)
                nc.vector.tensor_tensor(rows[:, 2, :].rearrange("h (n c) -> h n c", c=CH), by_chunk[:, :, CH - 1:CH].to_broadcast([H, T // CH, CH]),
                                        by_chunk, ALU.subtract).then_inc(*V0.step("G_left"))
                dve.wait_ge(*E0.after("cols"))
                nc.vector.tensor_copy(cols[:].rearrange("p a t h -> p (a t h)"), bank[2][:, 0:3 * TT * H]).then_inc(*V0.step("cols"))
                dve.wait_ge(*V0.after("cols"))
                nc.vector.tensor_scalar(neg_g[:], cols[:, 0], -1.0, None, ALU.mult).then_inc(*V0.step("neg_g"))
                dve.wait_ge(*A0.after("e_g"))
                nc.vector.tensor_tensor(be_g[:], e_g[:], cols[:, 1], ALU.mult).then_inc(*V0.step("be_g"))
                nc.vector.memset(S[:], 0.0).then_inc(*V0.step("S0"))

                def square(j):
                    if j >= 2:
                        dve.wait_ge(*E0.after(f"ss{j - 2}"))
                    nc.vector.tensor_tensor(sq[:, j % 2, :], qkvT[:, j, :], qkvT[:, j, :], ALU.mult).then_inc(*V0.step(f"sq{j}"))

                square(0)
                square(1)
                for j in range(8):
                    dve.wait_ge(*A0.after(f"norm{j}"))
                    nc.vector.reciprocal(nrm[:, j % 2, :], nrm[:, j % 2, :]).then_inc(*V0.step(f"inv{j}"))
                    dve.wait_ge(*V0.after(f"inv{j}"))
                    nc.vector.scalar_tensor_tensor(qkvT[:, j, :], nrm[:, j % 2, :], DK ** -0.5 if j < HJ else 1.0, qkvT[:, j, :],
                                                   ALU.mult, ALU.mult).then_inc(*V0.step(f"unit{j}"))
                    if j < 6:
                        square(j + 2)

                with dve.Fori(0, TT) as tt:
                    tok = bass.ds(tt * P, P)
                    VA, AA, EA, PA = ((lambda n, s=s: s.after(n, tt)) for s in (V, A, E, Q))

                    def per_head(c):
                        return c[:, tt, :].unsqueeze(2).to_broadcast([P, H, DK])

                    for g in G2:
                        dve.wait_ge(*EA(f"grow{g}"))
                        nc.vector.scalar_tensor_tensor(dec[:, g], b4(g), -1.0, mask("causal"), ALU.mult, ALU.add).then_inc(*V.step(f"pre{g}"))
                        nc.vector.tensor_tensor(decT[:, g], b4(g), mask("causalT"), ALU.add).then_inc(*V.step(f"preT{g}"))
                    dve.wait_ge(*PA("tile"))
                    dve.wait_ge(*EA("betaT"))
                    nc.vector.tensor_tensor(kbT[:], qkv[:, HJ:2 * HJ, :], b4(2), ALU.mult).then_inc(*V.step("kb"))
                    dve.wait_ge(*EA("kX"))
                    heads = bank[4][:].rearrange("p (h d) -> p h d", h=H)
                    nc.vector.tensor_tensor(kdec[:], heads, per_head(e_kd), ALU.mult).then_inc(*V.step("kdec"))
                    nc.vector.tensor_tensor(rw[:], heads, per_head(be_g), ALU.mult).then_inc(*V.step("rw"))
                    dve.wait_ge(*EA("vX"))
                    nc.vector.tensor_tensor(rv[:], bank[5][:].rearrange("p (h d) -> p h d", h=H), per_head(cols[:, 1]), ALU.mult).then_inc(*V.step("rv"))
                    dve.wait_ge(*AA("egT"))
                    nc.vector.tensor_tensor(qgT[:], qkv[:, 0:HJ, :], egT[:], ALU.mult).then_inc(*V.step("qg"))
                    for g, banks in ((0, (6, 7, 0)), (1, (1, 2, 3))):
                        dve.wait_ge(*AA(f"decT{g}{HJ - 1}"))
                        dve.wait_ge(*EA(f"kk{g}"))
                        if g:
                            dve.wait_ge(*PA("far0"))
                        nc.vector.tensor_tensor(L[:], b4(banks[0]), dec[:, g], ALU.mult).then_inc(*V.step(f"L{g}"))
                        dve.wait_ge(*EA(f"kkT{g}"))
                        if g:
                            dve.wait_ge(*PA("farT0"))
                        nc.vector.tensor_tensor(LT[:], b4(banks[1]), decT[:, g], ALU.mult).then_inc(*V.step(f"LT{g}"))
                        dve.wait_ge(*EA(f"qk{g}"))
                        nc.vector.tensor_tensor(aT[:, g], b4(banks[2]), decT[:, g], ALU.mult).then_inc(*V.step(f"aT{g}"))
                    b1, b2 = (5, 0), (6, 1)

                    def plus(name, dst, add, banks, product):
                        for g in G2:
                            dve.wait_ge(*EA(f"{product}{g}"))
                            nc.vector.tensor_tensor(flat(W[dst, g][:]), flat(W[add, g][:]), bank[banks[g]][:], ALU.add).then_inc(*V.step(f"{name}{g}"))

                    for g in G2:
                        dve.wait_ge(*PA(f"nearT{g}"))
                        nc.vector.tensor_tensor(W["PT", g][:], W["AT", g][:], mask("ident"), ALU.add).then_inc(*V.step(f"P1{g}"))
                    dve.wait_ge(*VA("P11"))
                    plus("P2", "PT", "PT", b2, "PA2")
                    dve.wait_ge(*VA("P21"))
                    plus("P3", "PT", "PT", b2, "PA4")
                    dve.wait_ge(*VA("P31"))
                    plus("P4", "PT", "PT", b1, "PA8")
                    for g in G2:
                        dve.wait_ge(*EA(f"MT{g}"))
                        nc.vector.tensor_copy(flat(W["QT", g][:]), bank[b2[g]][:]).then_inc(*V.step(f"MT{g}"))
                    for g in G2:
                        dve.wait_ge(*EA(f"M2{g}"))
                        dve.wait_ge(*EA(f"Q1{g}"))
                        nc.vector.tensor_tensor(flat(W["QT", g][:]), flat(W["PT", g][:]), bank[b1[g]][:], ALU.add).then_inc(*V.step(f"Q1{g}"))
                    dve.wait_ge(*VA("Q11"))
                    plus("TT", "AT", "QT", b2, "TT")
                    for g in G2:
                        dve.wait_ge(*EA(f"u{g}"))
                        nc.vector.tensor_copy(u[:, g].rearrange("p j d -> p (j d)"), bank[(4, 7)[g]][:, 0:HJ * DK]).then_inc(*V.step(f"u{g}"))
                    for c in G2:
                        r = slice(CH * c, CH * c + CH)
                        last = CH * c + CH - 1
                        nc.vector.tensor_tensor(Sd[:], S[:], egT[:, :, last:last + 1].to_broadcast([P, HJ, DK]), ALU.mult).then_inc(*V.step(f"Sd{c}"))
                        for g in G2:
                            dve.wait_ge(*EA(f"wS{c}{g}"))
                            nc.vector.tensor_tensor(vn[r, g], u[r, g], bank[3 + g][r, 0:HJ * DK].rearrange("p (j d) -> p j d", j=HJ),
                                                    ALU.subtract).then_inc(*V.step(f"vn{c}{g}"))
                        dve.wait_ge(*EA(f"dS{c}"))
                        nc.vector.tensor_tensor(S[:], Sd[:], bank[0][:, 0:HJ * DK].rearrange("p (j d) -> p j d", j=HJ), ALU.add).then_inc(*V.step(f"S{c}"))
                        dve.wait_ge(*EA(f"oa{c}"))
                        dve.wait_ge(*AA(f"oi{c}1"))
                        nc.vector.tensor_tensor(o[r], oS[r], bank[7][r, :].rearrange("p (g j d) -> p g j d", g=2, j=HJ), ALU.add).then_inc(*V.step(f"o{c}"))
                        dve.wait_ge(*VA(f"S{c}"))
                    dve.wait_ge(*VA("o1"))
                    o8 = o[:].rearrange("p g j d -> p (g j) d")
                    sq8 = oS[:].rearrange("p g j d -> p (g j) d")
                    nc.vector.tensor_tensor(sq8, o8, o8, ALU.mult).then_inc(*V.step("osq"))
                    dve.wait_ge(*VA("osq"))
                    nc.vector.tensor_reduce(ost[:, 0, :], sq8, AX.X, ALU.add).then_inc(*V.step("oss"))
                    dve.wait_ge(*AA("ostd"))
                    nc.vector.reciprocal(ost[:, 2, :], ost[:, 1, :]).then_inc(*V.step("ostd"))
                    dve.wait_ge(*VA("ostd"))
                    nc.vector.tensor_tensor(on[:].rearrange("p j g d -> p g j d"), o[:],
                                            ost[:, 2, :].rearrange("p (g j) -> p g j", g=2).unsqueeze(3).to_broadcast([P, 2, HJ, DK]),
                                            ALU.mult).then_inc(*V.step("on"))
                    dve.wait_ge(*EA("oT"))
                    nc.vector.scalar_tensor_tensor(zT[:, :, tok], b4(1), g_["out_norm"][:], zT[:, :, tok], ALU.mult, ALU.mult).then_inc(*V.step("oT"))


def merge_stage(nc, a, env):
    g_ = env
    bank, C, mod, norms, stat, eps = g_["bank"], g_["C"], g_["mod"], g_["norms"], g_["stat"], g_["eps"]
    x_tok, hT, scT, oT = g_["x_tok"], g_["hT"], g_["scT"], g_["zT"]
    row_ffn = g_["row_ffn"]
    sb, sem = g_["sb"], g_["sem"]
    KM = 2 * KT + 2 * HJ
    with ExitStack() as ctx:
        row_mix = sb(ctx, "row_mix", [P, D])
        wm = sb(ctx, "w_merge", [P, 2, KM, P])
        w_mix = sb(ctx, "w_mix", [P, KT, D])
        sg = sb(ctx, "sigmoids", [P, 2, 2, T])
        part = sb(ctx, "branch", [P, 2, 2, T])
        merged = sb(ctx, "mergedT", [P, KT, T])
        diag = sb(ctx, "diag", [P, KT, P])
        gate = sb(ctx, "gate", [P, 2, KT])
        scale2 = sb(ctx, "scale2", [P, KT])
        xn = sb(ctx, "xn2", [P, TT, D])
        tmp = xn
        ss = sb(ctx, "y_squares", [P, TT, 2])
        s_m = [sem(ctx, f"merge_landed{i}") for i in range(2)]
        s_mix = sem(ctx, "mix_landed")
        pre_v = ["gate0", "diag0", "gate1", "diag1", "scale_p", "scale2"]
        pre_a = ["row0", "row1", "row2", "row3"]
        pre_e = ["row0", "row1", "row2", "row3"]
        loop_v = [f"{x}{b}" for b in range(2) for x in ("sc", "dn", "sum")]
        loop_a = [f"{x}{b}" for b in range(2) for x in ("sg_sc", "sg_dn")]
        loop_e = [f"{x}{b}" for b in range(2) for x in ("g_sc", "g_dn", "b_sc", "b_dn")]
        n_loop = KT // 2
        post_v = [f"{x}{t}" for t in range(TT) for x in ("ss", "rstd", "y0_", "y1_", "x", "rstd2_", "xn")]
        post_a = [f"{x}{t}" for t in range(TT) for x in ("sq0_", "sq1_", "std", "sqx", "std2_")] + [f"h{k}" for k in range(KT)]
        post_e = [f"y{half}_{t}" for t in range(TT) for half in range(2)] + [f"xT{k}" for k in range(KT)]
        sv, sa, se = (sem(ctx, f"mg_{n}") for n in ("vector", "scalar", "tensor"))
        V0, A0, E0 = Steps(sv, pre_v), Steps(sa, pre_a), Steps(se, pre_e)
        V, A, E = Steps(sv, loop_v, len(pre_v)), Steps(sa, loop_a, len(pre_a)), Steps(se, loop_e, len(pre_e))
        V2, A2, E2 = (Steps(s, p, len(a0) + n_loop * len(lp)) for s, p, a0, lp in
                      ((sv, post_v, pre_v, loop_v), (sa, post_a, pre_a, loop_a), (se, post_e, pre_e, loop_e)))

        with nc.Block() as block:
            @block.sync
            def _(sp):
                for b in range(2):
                    sp.dma_start(wm[:, b], a["w_merge"][b]).then_inc(s_m[b], 16)
                sp.dma_start(w_mix[:], a["w_mix"]).then_inc(s_mix, 16)
                with sp.Fori(1, n_loop) as i:
                    for b in range(2):
                        sp.wait_ge(*E.after(f"b_dn{b}", i, 1))
                        sp.dma_start(wm[:, b], a["w_merge"][i * 2 + b]).then_inc(s_m[b], 16)

            @block.tensor
            def _(pe):
                for n in range(2):
                    pe.wait_ge(*V0.after(f"diag{n}"))
                    for half in range(2):
                        for k in range(HJ):
                            last = nc.tensor.matmul(bank[2 * n + half][:, k * P:(k + 1) * P], C["ones"], diag[:, HJ * half + k, :], start=True, stop=True)
                        last.then_inc(*E0.step(f"row{2 * n + half}"))
                pe.wait_ge(*A0.after("row3"))
                with pe.Fori(0, n_loop) as i:
                    for b in range(2):
                        pe.wait_ge(*V.after(f"sum{b}", i, 1))
                        pe.wait_ge(s_m[b], i * 16 + 16)
                        for n, (name, src, k0, kn) in enumerate((("g_sc", hT, 0, KT), ("g_dn", hT, KT, KT),
                                                                ("b_sc", scT, 2 * KT, HJ), ("b_dn", oT, 2 * KT + HJ, HJ))):
                            for k in range(kn):
                                last = nc.tensor.matmul(bank[4 * b + n][:], wm[:, b, k0 + k, :], src[:, k, :], start=(k == 0), stop=(k == kn - 1))
                            last.then_inc(*E.step(f"{name}{b}"))
                pe.wait_ge(*V.after("sum1", n_loop - 1))
                pe.wait_ge(s_mix, 16)
                for t in range(TT):
                    for half in range(2):
                        for k in range(KT):
                            last = nc.tensor.matmul(bank[2 * t + half][:], merged[:, k, t * P:(t + 1) * P], w_mix[:, k, half * 512:half * 512 + 512],
                                                    start=(k == 0), stop=(k == KT - 1))
                        last.then_inc(*E2.step(f"y{half}_{t}"))
                pe.wait_ge(*V2.after(f"xn{TT - 1}"))
                for k in range(KT):
                    if k >= 2:
                        pe.wait_ge(*A2.after(f"h{k - 2}"))
                    for t in range(TT):
                        last = nc.tensor.transpose(bank[k % 2][:, t * P:(t + 1) * P], xn[:, t, k * P:(k + 1) * P], C["ident"])
                    last.then_inc(*E2.step(f"xT{k}"))

            @block.scalar
            def _(act):
                for n in range(4):
                    act.wait_ge(*E0.after(f"row{n}"))
                    dst = (row_mix, row_ffn)[n // 2]
                    nc.scalar.activation(dst[:, 512 * (n % 2):512 * (n % 2) + 512], bank[n][:], ACT.Copy).then_inc(*A0.step(f"row{n}"))
                with act.Fori(0, n_loop) as i:
                    for b in range(2):
                        act.wait_ge(*V.after(f"sum{b}", i, 1))
                        for n, x in enumerate(("sc", "dn")):
                            act.wait_ge(*E.after(f"g_{x}{b}", i))
                            nc.scalar.activation(sg[:, b, n, :], bank[4 * b + n][:], ACT.Sigmoid).then_inc(*A.step(f"sg_{x}{b}"))
                for t in range(TT):
                    for half in range(2):
                        act.wait_ge(*E2.after(f"y{half}_{t}"))
                        nc.scalar.activation(tmp[:, t, half * 512:half * 512 + 512], bank[2 * t + half][:], ACT.Square,
                                             accum_out=ss[:, t, half:half + 1]).then_inc(*A2.step(f"sq{half}_{t}"))
                    act.wait_ge(*V2.after(f"ss{t}"))
                    nc.scalar.activation(stat[:, 1, t:t + 1], stat[:, 0, t:t + 1], ACT.Sqrt, bias=eps[:], scale=1.0 / D).then_inc(*A2.step(f"std{t}"))
                    act.wait_ge(*V2.after(f"x{t}"))
                    nc.scalar.activation(xn[:, t, :], x_tok[:, t, :], ACT.Square, accum_out=stat[:, 2, t:t + 1]).then_inc(*A2.step(f"sqx{t}"))
                    act.wait_ge(*A2.after(f"sqx{t}"))
                    nc.scalar.activation(stat[:, 3, t:t + 1], stat[:, 2, t:t + 1], ACT.Sqrt, bias=eps[:], scale=1.0 / D).then_inc(*A2.step(f"std2_{t}"))
                for k in range(KT):
                    act.wait_ge(*E2.after(f"xT{k}"))
                    nc.scalar.activation(hT[:, k, :], bank[k % 2][:], ACT.Identity, bias=mod[:, SH2 + k:SH2 + k + 1],
                                         scale=scale2[:, k:k + 1]).then_inc(*A2.step(f"h{k}"))

            @block.vector
            def _(dve):
                for n, (col, norm) in enumerate(((GT1, 1), (GT2, 3))):
                    if n:
                        dve.wait_ge(*E0.after("row1"))
                    nc.vector.tensor_tensor(gate[:, n, :], mod[:, col:col + KT], norms[:, norm, :], ALU.mult).then_inc(*V0.step(f"gate{n}"))
                    dve.wait_ge(*V0.after(f"gate{n}"))
                    nc.vector.tensor_tensor(diag[:], C["ident"].unsqueeze(1).to_broadcast([P, KT, P]),
                                            gate[:, n, :].unsqueeze(2).to_broadcast([P, KT, P]), ALU.mult).then_inc(*V0.step(f"diag{n}"))
                nc.vector.tensor_scalar(gate[:, 0, :], mod[:, SC2:SC2 + KT], 1.0, None, ALU.add).then_inc(*V0.step("scale_p"))
                dve.wait_ge(*V0.after("scale_p"))
                nc.vector.tensor_tensor(scale2[:], gate[:, 0, :], norms[:, 2, :], ALU.mult).then_inc(*V0.step("scale2"))
                with dve.Fori(0, n_loop) as i:
                    for b in range(2):
                        for n, x in enumerate(("sc", "dn")):
                            dve.wait_ge(*A.after(f"sg_{x}{b}", i))
                            dve.wait_ge(*E.after(f"b_{x}{b}", i))
                            nc.vector.tensor_tensor(part[:, b, n, :], sg[:, b, n, :], bank[4 * b + 2 + n][:], ALU.mult).then_inc(*V.step(f"{x}{b}"))
                        dve.wait_ge(*V.after(f"dn{b}", i))
                        nc.vector.tensor_tensor(merged[:, i * 2 + b, :], part[:, b, 0, :], part[:, b, 1, :], ALU.add).then_inc(*V.step(f"sum{b}"))
                for t in range(TT):
                    dve.wait_ge(*A2.after(f"sq1_{t}"))
                    nc.vector.tensor_tensor(stat[:, 0, t:t + 1], ss[:, t, 0:1], ss[:, t, 1:2], ALU.add).then_inc(*V2.step(f"ss{t}"))
                    dve.wait_ge(*A2.after(f"std{t}"))
                    nc.vector.reciprocal(stat[:, 0, t:t + 1], stat[:, 1, t:t + 1]).then_inc(*V2.step(f"rstd{t}"))
                    dve.wait_ge(*V2.after(f"rstd{t}"))
                    for half in range(2):
                        nc.vector.scalar_tensor_tensor(tmp[:, t, half * 512:half * 512 + 512], bank[2 * t + half][:], stat[:, 0, t:t + 1],
                                                       row_mix[:, half * 512:half * 512 + 512], ALU.mult, ALU.mult).then_inc(*V2.step(f"y{half}_{t}"))
                    dve.wait_ge(*V2.after(f"y1_{t}"))
                    nc.vector.tensor_tensor(x_tok[:, t, :], x_tok[:, t, :], tmp[:, t, :], ALU.add).then_inc(*V2.step(f"x{t}"))
                    dve.wait_ge(*A2.after(f"std2_{t}"))
                    nc.vector.reciprocal(stat[:, 2, t:t + 1], stat[:, 3, t:t + 1]).then_inc(*V2.step(f"rstd2_{t}"))
                    dve.wait_ge(*V2.after(f"rstd2_{t}"))
                    nc.vector.tensor_scalar(xn[:, t, :], x_tok[:, t, :], stat[:, 2, t:t + 1], None, ALU.mult).then_inc(*V2.step(f"xn{t}"))


def retrieve_stage(nc, a, env):
    g_ = env
    bank, C, hT = g_["bank"], g_["C"], g_["hT"]
    idxT, gateT = g_["idxT"], g_["gateT"]
    sb, sem = g_["sb"], g_["sem"]
    K2 = TOPK * TOPK
    with ExitStack() as ctx:
        wq = sb(ctx, "w_q", [P, 4, KT, P])
        keys = sb(ctx, "sub_keys", [P, 2 * PH, NKEYS])
        qT = sb(ctx, "queryT", [P, 2, T])
        s = sb(ctx, "scores", [P, 2, TT, NKEYS])
        v = sb(ctx, "top_half", [P, 2, TT, TOPK])
        iu = sb(ctx, "top_half_at", [P, 2, TT, TOPK], U32)
        fi = sb(ctx, "top_half_key", [P, 2, TT, TOPK])
        cand = sb(ctx, "candidates", [P, TT, K2])
        ts = sb(ctx, "top", [P, TT, TOPK])
        pos = sb(ctx, "top_at", [P, TT, TOPK], U32)
        ab = sb(ctx, "top_ab", [P, 2, TT, TOPK], U32)
        abf = sb(ctx, "top_ab_f", [P, 2, TT, TOPK])
        hot = sb(ctx, "rank_hot", [P, 2, TT, K2])
        score = sb(ctx, "top_all", [P, TT, PH, TOPK])
        sel = sb(ctx, "key_all", [P, 2, TT, PH, TOPK])
        gates = sb(ctx, "gates", [P, TT, PH, TOPK])
        gsum = sb(ctx, "gate_sum", [P, 2, TT, PH])
        gb = sb(ctx, "gate_part", [P, T], BF16)
        gr = sb(ctx, "gate_rest", [P, 2, T])
        s_q = [sem(ctx, f"wq_landed{i}") for i in range(4)]
        s_k = sem(ctx, "keys_landed")
        loop_e = ["q0", "q1", "s0", "s1"]
        loop_a = ["q0", "q1", "s0", "s1"]
        R4 = range(TT)
        loop_v = [f"{x}{p}{t}" for p in range(2) for x in ("max", "at", "rest", "max2_", "at2_") for t in R4]
        loop_v += ["key"] + [f"{x}{t}" for x in ("cand", "cmax", "cat", "crest", "cmax2_", "cat2_") for t in R4]
        loop_v += ["score", "shift", "mask", "ab_f", "hot0", "hot1", "sel0", "sel1"]
        loop_p = ["pick0", "pick1"]
        se, sa, sv, spl = (sem(ctx, f"rt_{n}") for n in ("tensor", "scalar", "vector", "pool"))
        E, A, V, Q = Steps(se, loop_e), Steps(sa, loop_a, len(loop_a)), Steps(sv, loop_v, len(loop_v)), Steps(spl, loop_p)
        post_v = ["gsub", "gsum", "grec", "gates", "idx0", "idx1", "gT", "b0", "g0", "r1", "b1", "g1", "r2"]
        V2 = Steps(sv, post_v, (1 + PH) * len(loop_v))
        A2 = Steps(sa, ["gexp"], (1 + PH) * len(loop_a))
        E2 = Steps(se, ["idx0", "idx1", "gate"], PH * len(loop_e))
        held = sem(ctx, "rt_held")

        with nc.Block() as block:
            @block.sync
            def _(sp):
                for n in range(4):
                    sp.dma_start(wq[:, n], a["w_q"][n]).then_inc(s_q[n], 16)
                sp.dma_start(keys[:], a["sub_keys"]).then_inc(s_k, 16)
                with sp.Fori(1, PH // 2) as i:
                    for b in range(4):
                        sp.wait_ge(*E.after(f"q{b % 2}", i * 2 + b // 2, 2))
                        sp.dma_start(wq[:, b], a["w_q"][i * 4 + b]).then_inc(s_q[b], 16)

            @block.tensor
            def _(pe):
                pe.wait_ge(s_k, 16)
                with pe.Fori(0, PH // 2) as i:
                    for b in range(2):
                        h = 2 * i + b
                        for p in range(2):
                            pe.wait_ge(s_q[2 * b + p], i * 16 + 16)
                            pe.wait_ge(*A.after(f"s{p}", h, 1))
                            for k in range(KT):
                                last = nc.tensor.matmul(bank[p][:], wq[:, 2 * b + p, k, :], hT[:, k, :], start=(k == 0), stop=(k == KT - 1))
                            last.then_inc(*E.step(f"q{p}"))
                        for p in range(2):
                            pe.wait_ge(*A.after(f"q{p}", h))
                            for t in R4:
                                last = nc.tensor.matmul(bank[2 + p][:, t * P:(t + 1) * P], qT[:, p, t * P:(t + 1) * P], keys[:, 2 * h + p, :], start=True, stop=True)
                            last.then_inc(*E.step(f"s{p}"))
                for n in range(3):
                    pe.wait_ge(*V2.after("gates"))
                    for t in R4:
                        src = (sel[:, n, t] if n < 2 else gates[:, t]).rearrange("p h k -> p (h k)")
                        last = nc.tensor.transpose(bank[4 + n][:, t * P:(t + 1) * P], src, C["ident"])
                    last.then_inc(*E2.step(("idx0", "idx1", "gate")[n]))

            @block.scalar
            def _(act):
                act.sem_inc(sa, len(loop_a))
                with act.Fori(0, PH) as h:
                    for p in range(2):
                        act.wait_ge(*E.after(f"q{p}", h))
                        nc.scalar.activation(qT[:, p, :], bank[p][:], ACT.Copy).then_inc(*A.step(f"q{p}"))
                    for p in range(2):
                        act.wait_ge(*V.after(f"at2_{p}{TT - 1}", h, 1))
                        act.wait_ge(*E.after(f"s{p}", h))
                        nc.scalar.activation(s[:, p].rearrange("p t n -> p (t n)"), bank[2 + p][:], ACT.Copy).then_inc(*A.step(f"s{p}"))
                act.wait_ge(*V2.after("gsub"))
                nc.scalar.activation(gates[:], gates[:], ACT.Exp).then_inc(*A2.step("gexp"))

            @block.gpsimd
            def _(pool):
                with pool.Fori(0, PH) as h:
                    for n in range(2):
                        pool.wait_ge(*V.after(f"hot{n}", h))
                        nc.gpsimd.tensor_tensor(hot[:, n].rearrange("p t (k r) -> p t k r", r=TOPK), hot[:, n].rearrange("p t (k r) -> p t k r", r=TOPK),
                                                fi[:, n].unsqueeze(2).to_broadcast([P, TT, TOPK, TOPK]), ALU.mult).then_inc(*Q.step(f"pick{n}"))

            @block.vector
            def _(dve):
                dve.sem_inc(sv, len(loop_v))
                with dve.Fori(0, PH) as h:
                    VA = lambda n: V.after(n, h)

                    def ready(*w):
                        for x in w:
                            dve.wait_ge(*x)
                        dve.sem_inc(held, 1)

                    for p in range(2):
                        ready(A.after(f"s{p}", h))
                        for t in R4:
                            nc.vector.max(v[:, p, t, 0:8], s[:, p, t]).then_inc(*V.step(f"max{p}{t}"))
                        ready(VA(f"max{p}{TT - 1}"))
                        for t in R4:
                            nc.vector.max_index(iu[:, p, t, 0:8], v[:, p, t, 0:8], s[:, p, t]).then_inc(*V.step(f"at{p}{t}"))
                        for t in R4:
                            nc.vector.match_replace(s[:, p, t], v[:, p, t, 0:8], s[:, p, t], -3e38).then_inc(*V.step(f"rest{p}{t}"))
                        ready(VA(f"rest{p}{TT - 1}"))
                        for t in R4:
                            nc.vector.max(v[:, p, t, 8:16], s[:, p, t]).then_inc(*V.step(f"max2_{p}{t}"))
                        ready(VA(f"max2_{p}{TT - 1}"))
                        for t in R4:
                            nc.vector.max_index(iu[:, p, t, 8:16], v[:, p, t, 8:16], s[:, p, t]).then_inc(*V.step(f"at2_{p}{t}"))
                    dve.wait_ge(*VA(f"at2_1{TT - 1}"))
                    nc.vector.tensor_copy(fi[:], iu[:]).then_inc(*V.step("key"))
                    for t in R4:
                        nc.vector.tensor_tensor(cand[:, t].rearrange("p (x y) -> p x y", x=TOPK), v[:, 0, t].unsqueeze(2).to_broadcast([P, TOPK, TOPK]),
                                                v[:, 1, t].unsqueeze(1).to_broadcast([P, TOPK, TOPK]), ALU.add).then_inc(*V.step(f"cand{t}"))
                    ready(VA(f"cand{TT - 1}"))
                    for t in R4:
                        nc.vector.max(ts[:, t, 0:8], cand[:, t]).then_inc(*V.step(f"cmax{t}"))
                    ready(VA(f"cmax{TT - 1}"))
                    for t in R4:
                        nc.vector.max_index(pos[:, t, 0:8], ts[:, t, 0:8], cand[:, t]).then_inc(*V.step(f"cat{t}"))
                    for t in R4:
                        nc.vector.match_replace(cand[:, t], ts[:, t, 0:8], cand[:, t], -3e38).then_inc(*V.step(f"crest{t}"))
                    ready(VA(f"crest{TT - 1}"))
                    for t in R4:
                        nc.vector.max(ts[:, t, 8:16], cand[:, t]).then_inc(*V.step(f"cmax2_{t}"))
                    ready(VA(f"cmax2_{TT - 1}"))
                    for t in R4:
                        nc.vector.max_index(pos[:, t, 8:16], ts[:, t, 8:16], cand[:, t]).then_inc(*V.step(f"cat2_{t}"))
                    nc.vector.tensor_copy(score[:, :, h, :], ts[:]).then_inc(*V.step("score"))
                    dve.wait_ge(*VA(f"cat2_{TT - 1}"))
                    nc.vector.tensor_scalar(ab[:, 0], pos[:], 4, None, ALU.logical_shift_right).then_inc(*V.step("shift"))
                    nc.vector.tensor_scalar(ab[:, 1], pos[:], TOPK - 1, None, ALU.bitwise_and).then_inc(*V.step("mask"))
                    dve.wait_ge(*VA("mask"))
                    nc.vector.tensor_copy(abf[:], ab[:]).then_inc(*V.step("ab_f"))
                    dve.wait_ge(*VA("ab_f"))
                    for n in range(2):
                        nc.vector.tensor_tensor(hot[:, n].rearrange("p t (k r) -> p (t k) r", r=TOPK),
                                                abf[:, n].rearrange("p t k -> p (t k)").unsqueeze(2).to_broadcast([P, TT * TOPK, TOPK]),
                                                C["iota"][:, 0:TOPK].unsqueeze(1).to_broadcast([P, TT * TOPK, TOPK]), ALU.is_equal).then_inc(*V.step(f"hot{n}"))
                    for n in range(2):
                        dve.wait_ge(*Q.after(f"pick{n}", h))
                        nc.vector.tensor_reduce(sel[:, n, :, h, :], hot[:, n].rearrange("p t (k r) -> p t k r", r=TOPK), AX.X, ALU.add).then_inc(*V.step(f"sel{n}"))
                dve.wait_ge(*V.after("sel1", PH - 1))
                th = lambda x: x.rearrange("p t h k -> p (t h) k")
                nc.vector.tensor_tensor(th(gates[:]), th(score[:]), th(score[:])[:, :, 0:1].to_broadcast([P, TT * PH, TOPK]), ALU.subtract).then_inc(*V2.step("gsub"))
                dve.wait_ge(*A2.after("gexp"))
                nc.vector.tensor_reduce(gsum[:, 0].rearrange("p t h -> p (t h)"), th(gates[:]), AX.X, ALU.add).then_inc(*V2.step("gsum"))
                dve.wait_ge(*V2.after("gsum"))
                nc.vector.reciprocal(gsum[:, 1], gsum[:, 0]).then_inc(*V2.step("grec"))
                dve.wait_ge(*V2.after("grec"))
                nc.vector.tensor_tensor(th(gates[:]), th(gates[:]), gsum[:, 1].rearrange("p t h -> p (t h)").unsqueeze(2).to_broadcast([P, TT * PH, TOPK]),
                                        ALU.mult).then_inc(*V2.step("gates"))
                for n in range(2):
                    dve.wait_ge(*E2.after(f"idx{n}"))
                    nc.vector.tensor_copy(idxT[:, n, :], bank[4 + n][:]).then_inc(*V2.step(f"idx{n}"))
                dve.wait_ge(*E2.after("gate"))
                nc.vector.tensor_copy(gr[:, 0, :], bank[6][:]).then_inc(*V2.step("gT"))
                dve.wait_ge(*V2.after("gT"))
                for n in range(2):
                    nc.vector.tensor_copy(gb[:], gr[:, n, :]).then_inc(*V2.step(f"b{n}"))
                    dve.wait_ge(*V2.after(f"b{n}"))
                    nc.vector.tensor_copy(gateT[:, n, :], gb[:]).then_inc(*V2.step(f"g{n}"))
                    dve.wait_ge(*V2.after(f"g{n}"))
                    nc.vector.tensor_tensor(gr[:, 1, :] if n == 0 else gateT[:, 2, :], gr[:, n, :], gateT[:, n, :], ALU.subtract).then_inc(*V2.step(f"r{n + 1}"))
                    dve.wait_ge(*V2.after(f"r{n + 1}"))


def scatter_stage(nc, a, env, spill):
    g_ = env
    bank, C, idxT, gateT = g_["bank"], g_["C"], g_["idxT"], g_["gateT"]
    sb, sem = g_["sb"], g_["sem"]
    TB, GT = 64, 4
    NG = TB // GT
    with ExitStack() as ctx:
        iota = sb(ctx, "iota_bf", [P, P], BF16)
        hot1 = sb(ctx, "hot_i1", [P, 2, GT, P], BF16)
        hot2 = sb(ctx, "gated_i2", [P, 2, GT, 3, P], BF16)
        block_g = sb(ctx, "gate_block", [P, 2, P, TB])
        iota_ready, hot_ready, dense, copied = (sem(ctx, n) for n in ("iota_ready", "hot_ready", "dense", "copied"))
        stored = [sem(ctx, f"stored{i}") for i in range(2)]
        LAG = 2

        def groups():
            pass

        with nc.Block() as block:
            @block.vector
            def _(dve):
                nc.vector.tensor_copy(iota[:], C["iota"]).then_inc(iota_ready, 1)
                dve.wait_ge(iota_ready, 1)
                with dve.Fori(0, T // (2 * GT)) as i:
                    for b in range(2):
                        dve.wait_ge(dense, i * 2 + (b + 1))
                        for t in range(GT):
                            at = i * (2 * GT) + (b * GT + t)
                            nc.vector.tensor_scalar(hot1[:, b, t, :], iota[:], idxT[:, 0, bass.ds(at, 1)], None, ALU.is_equal)
                            for n in range(3):
                                last = nc.vector.tensor_scalar(hot2[:, b, t, n, :], iota[:], idxT[:, 1, bass.ds(at, 1)], gateT[:, n, bass.ds(at, 1)],
                                                               ALU.is_equal, ALU.mult)
                        last.then_inc(hot_ready, 1)

            @block.gpsimd
            def _(pool):
                pool.sem_inc(dense, LAG)
                pool.sem_inc(copied, LAG)

            @block.tensor
            def _(pe):
                with pe.Fori(0, T // (2 * GT)) as i:
                    for b in range(2):
                        pe.wait_ge(copied, i * 2 + (b + 1))
                        pe.wait_ge(hot_ready, i * 2 + (b + 1))
                        for t in range(GT):
                            for n in range(3):
                                last = nc.tensor.matmul(bank[b][:, t * P:(t + 1) * P], hot1[:, b, t, :], hot2[:, b, t, n, :], start=(n == 0), stop=(n == 2))
                        last.then_inc(dense, 1)

            @block.scalar
            def _(act):
                with act.Fori(0, T // TB // 2) as o:
                    for slot in range(2):
                        act.wait_ge(stored[slot], o * 16 + 16)
                        with act.Fori(0, NG // 2) as i:
                            for b in range(2):
                                act.wait_ge(dense, (o * 2 + slot) * NG + i * 2 + (b + 1 + LAG))
                                nc.scalar.activation(block_g[:, slot, :, bass.ds(i * (2 * GT) + b * GT, GT)],
                                                     bank[b][:].rearrange("p (t n) -> p n t", t=GT), ACT.Copy).then_inc(copied, 1)

            @block.sync
            def _(sp):
                for s in stored:
                    sp.sem_inc(s, 16)
                with sp.Fori(0, T // TB // 2) as o:
                    for slot in range(2):
                        sp.wait_ge(copied, o * (2 * NG) + ((slot + 1) * NG + LAG))
                        sp.dma_start(spill[:, bass.ds(o * 2 + slot, 1)], block_g[:, slot:slot + 1]).then_inc(stored[slot], 16)
                for s in stored:
                    sp.wait_ge(s, 16 * (T // TB // 2 + 1))


def expert_stage(nc, a, env, spill, out):
    g_ = env
    bank, stat, eps, x_tok, hT, row_ffn = (g_[n] for n in ("bank", "stat", "eps", "x_tok", "hT", "row_ffn"))
    sb, sem = g_["sb"], g_["sem"]
    GE, UR, GC = 8, 4, 4
    NGRP = EXP_TILES // GE
    with ExitStack() as ctx:
        ut = sb(ctx, "u_tiles", [P, UR, KT, P])
        vt = sb(ctx, "v_tiles", [P, GE, D])
        gt = sb(ctx, "gate_tiles", [P, 2, T // 64, GC, 64])
        act_u = sb(ctx, "gelu", [P, 2, T])
        pt = sb(ctx, "coef", [P, GE, T])
        y = sb(ctx, "y", [P, TT, D])
        ss = sb(ctx, "y_sq", [P, 4, TT])
        s_u = [sem(ctx, f"u_landed{i}") for i in range(UR)]
        s_v = sem(ctx, "v_landed")
        s_g = [sem(ctx, f"gates_landed{i}") for i in range(2)]
        zeroed, stored = sem(ctx, "y_zeroed"), sem(ctx, "out_stored")
        loop_e = [f"u{e}" for e in range(GE)] + [f"y{half}{t}" for half in range(2) for t in range(TT)]
        loop_a = [f"gelu{e}" for e in range(GE)]
        loop_v = [f"coef{e}" for e in range(GE)] + [f"add{half}{t}" for half in range(2) for t in range(TT)]
        se, sa, sv = (sem(ctx, f"ex_{n}") for n in ("tensor", "scalar", "vector"))
        E, A, V = Steps(se, loop_e), Steps(sa, loop_a), Steps(sv, loop_v, len(loop_v))
        A2 = Steps(sa, [f"sq{t}" for t in range(TT)] + ["std"], NGRP * len(loop_a))
        V2 = Steps(sv, ["rstd"] + [f"{x}{t}" for t in range(TT) for x in ("scaled", "out")], (1 + NGRP) * len(loop_v))
        a_banks, y_banks = (2, 3, 4, 5), ((2, 3, 4, 5), (6, 7, 0, 1))

        with nc.Block() as block:
            @block.sync
            def _(sp):
                for n in range(UR):
                    sp.dma_start(ut[:, n], a["peer_u"][n]).then_inc(s_u[n], 16)

                def group_loads(i, last=False):
                    for e in range(GE):
                        if e % GC == 0:
                            sp.wait_ge(*V.after(f"coef{e + GC - 1}", i, 1))
                            sp.dma_start(gt[:, e // GC], spill[:, :, bass.ds(i * GE + e, GC), :]).then_inc(s_g[e // GC], 16)
                        if e == 0:
                            sp.wait_ge(*V.after(f"add1{TT - 1}", i, 1))
                            sp.dma_start(vt[:], a["peer_v"][bass.ds(i * GE, GE)].rearrange("e p d -> p e d")).then_inc(s_v, 16)
                        if e < UR or not last:
                            sp.wait_ge(*E.after(f"u{e}", i))
                            sp.dma_start(ut[:, e % UR], a["peer_u"][i * GE + (e + UR)]).then_inc(s_u[e % UR], 16)

                with sp.Fori(0, NGRP - 1) as i:
                    group_loads(i)
                group_loads(NGRP - 1, last=True)

            @block.tensor
            def _(pe):
                with pe.Fori(0, NGRP) as i:
                    for e in range(GE):
                        pe.wait_ge(s_u[e % UR], i * 32 + 16 * (e // UR + 1))
                        pe.wait_ge(*(V.after(f"add0{e}", i, 1) if e < 4 else A.after(f"gelu{e - 4}", i)))
                        for k in range(KT):
                            last = nc.tensor.matmul(bank[a_banks[e % 4]][:], ut[:, e % UR, k, :], hT[:, k, :], start=(k == 0), stop=(k == KT - 1))
                        last.then_inc(*E.step(f"u{e}"))
                    pe.wait_ge(s_v, i * 16 + 16)
                    for half in range(2):
                        for e in range(GE):
                            if half == 0:
                                pe.wait_ge(*V.after(f"coef{e}", i))
                            for t in range(TT):
                                if e == 0:
                                    pe.wait_ge(*(A.after(f"gelu{4 + t}", i) if half == 0 else V.after(f"add1{t}", i, 1)))
                                last = nc.tensor.matmul(bank[y_banks[half][t]][:], pt[:, e, t * P:(t + 1) * P], vt[:, e, half * 512:half * 512 + 512],
                                                        start=(e == 0), stop=(e == GE - 1))
                                if e == GE - 1:
                                    last.then_inc(*E.step(f"y{half}{t}"))

            @block.gpsimd
            def _(pool):
                nc.gpsimd.memset(y[:], 0.0).then_inc(zeroed, 1)

            @block.scalar
            def _(act):
                with act.Fori(0, NGRP) as i:
                    for e in range(GE):
                        act.wait_ge(*(V.after(f"coef{e - 2}", i) if e >= 2 else V.after(f"coef{GE - 2 + e}", i, 1)))
                        act.wait_ge(*E.after(f"u{e}", i))
                        nc.scalar.activation(act_u[:, e % 2, :], bank[a_banks[e % 4]][:], ACT.Gelu).then_inc(*A.step(f"gelu{e}"))
                act.wait_ge(*V.after(f"add1{TT - 1}", NGRP - 1))
                for t in range(TT):
                    nc.scalar.activation(vt[:, t, :], y[:, t, :], ACT.Square, accum_out=ss[:, 0, t:t + 1]).then_inc(*A2.step(f"sq{t}"))
                act.wait_ge(*A2.after(f"sq{TT - 1}"))
                nc.scalar.activation(ss[:, 1, :], ss[:, 0, :], ACT.Sqrt, bias=eps[:], scale=1.0 / D).then_inc(*A2.step("std"))
                for t in range(TT):
                    act.wait_ge(*V2.after(f"out{t}"))
                    act.dma_start(out[t * P:(t + 1) * P, :], y[:, t, :]).then_inc(stored, 16)
                act.wait_ge(stored, 16 * TT)

            @block.vector
            def _(dve):
                dve.wait_ge(zeroed, 1)
                dve.sem_inc(sv, len(loop_v))
                with dve.Fori(0, NGRP) as i:
                    for e in range(GE):
                        if e % GC == 0:
                            dve.wait_ge(s_g[e // GC], i * 16 + 16)
                        dve.wait_ge(*A.after(f"gelu{e}", i))
                        nc.vector.tensor_tensor(pt[:, e].rearrange("p (b t) -> p b t", t=64), act_u[:, e % 2].rearrange("p (b t) -> p b t", t=64),
                                                gt[:, e // GC, :, e % GC, :], ALU.mult).then_inc(*V.step(f"coef{e}"))
                    for half in range(2):
                        for t in range(TT):
                            dve.wait_ge(*E.after(f"y{half}{t}", i))
                            c = slice(half * 512, half * 512 + 512)
                            nc.vector.tensor_tensor(y[:, t, c], y[:, t, c], bank[y_banks[half][t]][:], ALU.add).then_inc(*V.step(f"add{half}{t}"))
                dve.wait_ge(*A2.after("std"))
                nc.vector.reciprocal(ss[:, 2, :], ss[:, 1, :]).then_inc(*V2.step("rstd"))
                dve.wait_ge(*V2.after("rstd"))
                for t in range(TT):
                    nc.vector.scalar_tensor_tensor(y[:, t, :], y[:, t, :], ss[:, 2, t:t + 1], row_ffn[:], ALU.mult, ALU.mult).then_inc(*V2.step(f"scaled{t}"))
                    dve.wait_ge(*V2.after(f"scaled{t}"))
                    nc.vector.tensor_tensor(y[:, t, :], y[:, t, :], x_tok[:, t, :], ALU.add).then_inc(*V2.step(f"out{t}"))


def lay_out(inputs):
    f = {k: np.asarray(v) for k, v in inputs.items()}

    def cols(w, c0, n):
        k = w.shape[0] // P
        return w[:, c0:c0 + n * P].reshape(k, P, n, P).transpose(2, 1, 0, 3)

    w_in = f["w_in_mix"][0]
    sc, qkv, z, ab = 0, 1536, 3072, 3584
    gates = 3600
    b_t, c_t, x_t = (cols(w_in, sc + 512 * n, 4) for n in range(3))
    sc_tiles = np.stack([c_t, x_t, b_t], 1).reshape(12, P, KT, P)
    g_sc, g_dn = cols(w_in, gates, KT), cols(w_in, gates + D, KT)
    merge = np.concatenate([g_sc, g_dn, cols(f["w_sc_out"][0], 0, KT), cols(f["w_dn_out"][0], 0, KT)], axis=2)
    _, wide, narrow = constants()
    r = {
        "x": f["x"][0],
        "c_col": f["c"][0].reshape(KT, P).T,
        "w_ada": f["w_ada"][0].reshape(KT, P, 24, 256).transpose(2, 1, 0, 3),
        "b_ada": f["b_ada"][0].reshape(MOD, P).T,
        "norms": np.stack([f[n][0].reshape(KT, P).T for n in ("norm_pre_mix", "norm_post_mix", "norm_pre_ffn", "norm_post_ffn")], 1),
        "w_proj": np.concatenate([sc_tiles, cols(w_in, qkv, 12), cols(w_in, z, 4)], 0),
        "w_ab": w_in[:, ab:ab + 16].reshape(KT, P, 16).transpose(1, 0, 2),
        "sc_w": f["sc_conv_w"][0].reshape(3, 4, P).transpose(2, 1, 0),
        "dn_w": f["dn_conv_w"][0].reshape(4, 12, P).transpose(2, 1, 0),
        "dt_bias": f["dn_dt_bias"][0][:, None],
        "a_log": f["dn_a_log"][0][:, None],
        "out_norm": np.concatenate([f["dn_out_norm"][0]] * 2)[:, None],
        "w_merge": merge,
        "w_mix": f["w_mix_out"][0].reshape(KT, P, D).transpose(1, 0, 2),
        "w_q": cols(f["peer_w_q"][0], 0, 16),
        "sub_keys": f["peer_sub_keys"][0].reshape(16, P, P).transpose(2, 0, 1),
        "peer_u": f["peer_u"].reshape(P, P, KT, P).transpose(1, 3, 2, 0),
        "peer_v": f["peer_v"].reshape(P, P, D).transpose(1, 0, 2),
        "wide": wide,
        "narrow": narrow,
    }
    return {k: np.ascontiguousarray(v) for k, v in r.items()}


SPILL = (P, T // 64, P, 64)


def kernel(**inputs):
    import concourse.bacc as _bacc
    from concourse.bass_utils import run_bass_kernel_spmd as _run

    nc = _bacc.Bacc("TRN2", target_bir_lowering=False, num_devices=1)
    laid = lay_out(inputs)
    aps = {n: nc.dram_tensor(f"in_{n}_dram", v.shape, mybir.dt.from_np(v.dtype), kind="ExternalInput").ap() for n, v in laid.items()}
    out = nc.dram_tensor("out_dram", (T, D), F32, kind="ExternalOutput").ap()
    spill = nc.dram_tensor("gate_scratch", SPILL, F32, kind="Internal").ap()
    program(nc, aps, out, spill)
    r = _run(nc, [{f"in_{n}_dram": v for n, v in laid.items()}], core_ids=[0])
    return r.results[0]["out_dram"].reshape(1, T, D)
```

```python
from contextlib import ExitStack

import numpy as np

import concourse.bass as bass
from concourse import mybir

F32 = mybir.dt.float32
F32R = mybir.dt.float32r
U32 = mybir.dt.uint32
ALU = mybir.AluOpType
ACT = mybir.ActivationFunctionType
AX = mybir.AxisListType

P = 128
T = 512
D = 1024
TT = T // P
KT = D // P
H, DK = 8, 64
HJ = H // 2
CH = 64
EPS = 1e-6
MOD = 6 * KT
SH1, SC1, GT1, SH2, SC2, GT2 = (KT * n for n in range(6))
N_SC, N_QKV, N_Z = 12, 12, 4
N_PROJ = N_SC + N_QKV + N_Z
NEG = -1e30
PH, TOPK, NKEYS = 8, 16, 128
TB = 32
EXP_TILES = NKEYS


class Steps:

    def __init__(self, sem, names, base=0):
        self.sem, self.base, self.at = sem, base, {n: i + 1 for i, n in enumerate(names)}
        assert len(self.at) == len(names)
        self.names, self.n = names, 0

    def after(self, name, it=0, back=0):
        value = self.base + self.at[name] - back * len(self.names)
        assert value > 0 or (back and not isinstance(it, int)), (name, value)
        return self.sem, it * len(self.names) + value

    def step(self, name):
        assert self.names[self.n % len(self.names)] == name, (name, self.names[self.n % len(self.names)])
        self.n += 1
        return self.sem, 1


def constants():
    i, j = np.arange(P)[:, None], np.arange(P)[None, :]
    chunk = i // CH == j // CH
    near = i // 16 == j // 16
    parts = {
        "ident": i == j,
        "headsum": i // DK == j // DK,
        "ones": np.ones((P, P)),
        "neg_near": -1.0 * (near & (j < i)),
        "neg_far": -1.0 * (chunk & ~near & (j < i)),
        "neg_nearT": -1.0 * (near & (i < j)),
        "neg_farT": -1.0 * (chunk & ~near & (i < j)),
        "causal": np.where(chunk & (j <= i), 0.0, NEG),
        "causalT": np.where(chunk & (i <= j), 0.0, NEG),
        "iota": np.broadcast_to(j, (P, P)),
    }
    wide = np.concatenate([v.astype(np.float32) for v in parts.values()], axis=1)
    h = np.arange(H)[:, None]
    m = np.arange(P)[None, :]
    sel_head = np.stack([np.broadcast_to(h == n, (H, P)) for n in range(H)], 1)
    sel_pair = np.stack([h == 2 * n + m // DK for n in range(HJ)], 1)
    carry = np.broadcast_to(np.arange(T)[None, :] % CH != 0, (H, T))
    small = np.concatenate([a.reshape(H, -1).astype(np.float32) for a in (sel_head, sel_pair, carry)], 1)
    return list(parts), np.ascontiguousarray(wide), np.ascontiguousarray(small)


def program(nc, a, out, spill, upto=9, dbg=None):
    top = ExitStack()
    const_names = constants()[0]

    def dump(view):
        with nc.semaphore("dumped") as s, nc.Block() as block:
            @block.sync
            def _(sp):
                sp.dma_start(dbg, view).then_inc(s, 16)
                sp.wait_ge(s, 16)

    with top:
        def sb(ctx, name, shape, dt=F32):
            return ctx.enter_context(nc.sbuf_tensor(name, shape, dt))

        def sem(ctx, name):
            return ctx.enter_context(nc.semaphore(name))

        bank = [top.enter_context(nc.psum_tensor(f"bank{i}", [P, 512], F32)) for i in range(8)]
        cst = sb(top, "cst", [P, len(const_names), P])
        C = {n: cst[:, i, :] for i, n in enumerate(const_names)}
        small = sb(top, "small", [H, 12 * P + T])
        sel_head = small[:, 0:8 * P].rearrange("h (n m) -> h n m", n=H)
        sel_pair = small[:, 8 * P:12 * P].rearrange("h (n m) -> h n m", n=HJ)
        carry = small[:, 12 * P:12 * P + T]
        eps = sb(top, "eps", [P, 1])
        mod = sb(top, "mod", [P, MOD])
        norms = sb(top, "norms", [P, 4, KT])
        x_tok = sb(top, "x_tok", [P, TT, D])
        stat = sb(top, "stat", [P, 4, TT])

        row_ffn = sb(top, "row_ffn", [P, D])
        env = dict(locals())
        mix = ExitStack()
        with mix:
            env["hT"] = hT = sb(mix, "hT", [P, KT, T])
            env["qkvT"] = sb(mix, "qkvT", [P, 12, T])
            env["zT"] = sb(mix, "zT", [P, HJ, T])
            env["scT"] = sb(mix, "scT", [P, HJ, T])
            env["abT"] = sb(mix, "abT", [H, 2, T])
            env["dt_bias"] = sb(mix, "dt_bias", [H, 1])
            env["a_log"] = sb(mix, "a_log", [H, 1])
            env["out_norm"] = sb(mix, "out_norm", [P, 1])
            project_stage(nc, a, env)
            if upto == 1:
                return dump({"mod": mod[:], "hT": hT[:], "qkvT": env["qkvT"][:], "scT": env["scT"][:], "zT": env["zT"][:], "abT": env["abT"][:]}[dbg.name.split("_", 1)[1]])
            delta_stage(nc, a, env)
            if upto == 2:
                return dump({"qkvT": env["qkvT"][:], "zT": env["zT"][:]}[dbg.name.split("_", 1)[1]])
            merge_stage(nc, a, env)
            if upto == 3:
                return dump({"x": x_tok[:], "row": row_ffn[:]}[dbg.name.split("_", 1)[1]])
        env["h_hi"] = sb(top, "h_hi", [P, KT, T], F32R)
        env["h_lo"] = sb(top, "h_lo", [P, KT, T], F32R)
        pick = ExitStack()
        with pick:
            env["idxT"] = sb(pick, "idxT", [P, 2, T])
            env["gateT"] = sb(pick, "gateT", [P, T])
            retrieve_stage(nc, a, env)
            if upto == 4:
                return dump({"idxT": env["idxT"][:], "gateT": env["gateT"][:]}[dbg.name.split("_", 1)[1]])
            scatter_stage(nc, a, env, spill)
        expert_stage(nc, a, env, spill, out)


def project_stage(nc, a, env):
    g = env
    bank, C, mod, norms, stat, eps = g["bank"], g["C"], g["mod"], g["norms"], g["stat"], g["eps"]
    x_tok, hT, qkvT, zT, scT, abT = g["x_tok"], g["hT"], g["qkvT"], g["zT"], g["scT"], g["abT"]
    sb, sem = g["sb"], g["sem"]
    AR, AW = 4, 256
    NA = 6 * D // AW
    NA1 = 2 * D // AW
    WR = 4
    with ExitStack() as ctx:
        ada = sb(ctx, "ada", [P, AR, KT, AW])
        wring = sb(ctx, "wring", [P, WR, KT, P])
        w_ab = sb(ctx, "w_ab", [P, KT, 2 * H])
        raw = sb(ctx, "raw", [P, WR, 3 + T])
        xn = sb(ctx, "xn", [P, TT, D])
        c_col = sb(ctx, "c_col", [P, KT])
        c_act = sb(ctx, "c_act", [P, 3, KT])
        b_ada = sb(ctx, "b_ada", [P, MOD])
        scale1 = sb(ctx, "scale1", [P, KT])
        sc_w = sb(ctx, "sc_w", [P, HJ, 3])
        dn_w = sb(ctx, "dn_w", [P, 12, 4])
        conv = sb(ctx, "conv", [P, 3, T])
        upad = sb(ctx, "upad", [P, 2 + T])
        acc = sb(ctx, "acc", [P, 2, T])

        s_c, s_const, s_x, s_small, s_wab = (sem(ctx, n) for n in ("c_landed", "const_landed", "x_landed", "small_landed", "wab_landed"))
        s_ada = [sem(ctx, f"ada_landed{i}") for i in range(AR)]
        s_w = [sem(ctx, f"w_landed{i}") for i in range(WR)]
        ada_used, w_used, raw_ready, raw_used = (sem(ctx, n) for n in ("ada_used", "w_used", "raw_ready", "raw_used"))
        conv_done, conv_taken = sem(ctx, "conv_done"), sem(ctx, "conv_taken")
        conv_chain = sem(ctx, "conv_chain")
        V = Steps(sem(ctx, "p_vector"), ["pads", "pads_u", "eps", "c_plus", "c_recip", "c_silu"]
                  + ["rstd"] + [f"xn{t}" for t in range(TT)] + ["mod1", "scale_p", "scale1"])
        A = Steps(sem(ctx, "p_scalar"), ["c_exp"] + [f"sq{t}" for t in range(TT)] + ["std"] + [f"h{k}" for k in range(KT)])
        E = Steps(sem(ctx, "p_tensor"), [f"xT{k}" for k in range(KT)])
        proj_done, ab_done, mod_done = sem(ctx, "proj_done"), sem(ctx, "ab_done"), sem(ctx, "mod_done")
        last_v = sem(ctx, "p_last")

        mod_ps = bank[0]
        xT_ps = bank[1:3]
        proj_ps = bank[3:7]
        ab_ps = [bank[1], bank[2]]

        with nc.Block() as block:
            @block.sync
            def _(sp):
                sp.dma_start(c_col[:], a["c_col"]).then_inc(s_c, 16)
                for t in range(TT):
                    sp.dma_start(x_tok[:, t, :], a["x"][t * P:(t + 1) * P, :]).then_inc(s_x, 16)

                def load_ada(n):
                    if n >= AR:
                        sp.wait_ge(ada_used, n - AR + 1)
                    sp.dma_start(ada[:, n % AR, :, :], a["w_ada"][n]).then_inc(s_ada[n % AR], 16)

                for n in range(AR):
                    load_ada(n)
                sp.dma_start(g["cst"][:], a["wide"]).then_inc(s_const, 16)
                for dst, name in ((g["small"][:], "narrow"), (b_ada[:], "b_ada"), (norms[:], "norms"), (sc_w[:], "sc_w"),
                                  (dn_w[:], "dn_w"), (g["dt_bias"][:], "dt_bias"), (g["a_log"][:], "a_log"),
                                  (g["out_norm"][:], "out_norm")):
                    sp.dma_start(dst, a[name]).then_inc(s_small, 16)
                for n in range(AR, NA1):
                    load_ada(n)
                for n in range(WR):
                    sp.dma_start(wring[:, n], a["w_proj"][n]).then_inc(s_w[n], 16)
                sp.dma_start(w_ab[:], a["w_ab"]).then_inc(s_wab, 16)
                with sp.Fori(1, N_PROJ // WR) as i:
                    for b in range(WR):
                        sp.wait_ge(w_used, i * WR + (b + 1 - WR))
                        sp.dma_start(wring[:, b], a["w_proj"][i * WR + b]).then_inc(s_w[b], 16)
                for n in range(NA1, NA):
                    load_ada(n)

            def mod_piece(pe, n):
                pe.wait_ge(s_ada[n % AR], 16 * (n // AR + 1))
                for m in range(AW // P):
                    col = n * (AW // P) + m
                    for k in range(KT):
                        last = nc.tensor.matmul(mod_ps[:, col:col + 1], ada[:, n % AR, k, m * P:(m + 1) * P],
                                                c_act[:, 2, k:k + 1], start=(k == 0), stop=(k == KT - 1))
                return last

            @block.tensor
            def _(pe):
                pe.wait_ge(*V.after("c_silu"))
                for n in range(NA1):
                    mod_piece(pe, n).then_inc(ada_used, 1)
                pe.wait_ge(s_const, 16)
                pe.wait_ge(*V.after(f"xn{TT - 1}"))
                for k in range(KT):
                    if k >= 2:
                        pe.wait_ge(*A.after(f"h{k - 2}"))
                    for t in range(TT):
                        last = nc.tensor.transpose(xT_ps[k % 2][:, t * P:(t + 1) * P], xn[:, t, k * P:(k + 1) * P], C["ident"])
                    last.then_inc(*E.step(f"xT{k}"))
                pe.wait_ge(*A.after(f"h{KT - 1}"))
                with pe.Fori(0, N_PROJ // WR) as i:
                    for b in range(WR):
                        pe.wait_ge(s_w[b], i * 16 + 16)
                        pe.wait_ge(raw_ready, i * WR + (b + 1))
                        for k in range(KT):
                            last = nc.tensor.matmul(proj_ps[b][:], wring[:, b, k, :], hT[:, k, :], start=(k == 0), stop=(k == KT - 1))
                        last.then_inc(w_used, 1)
                pe.wait_ge(s_wab, 16)
                for n in range(2):
                    for k in range(KT):
                        last = nc.tensor.matmul(ab_ps[n][0:H, :], w_ab[:, k, n * H:(n + 1) * H], hT[:, k, :], start=(k == 0), stop=(k == KT - 1))
                    last.then_inc(ab_done, 1)
                for n in range(NA1, NA):
                    mod_piece(pe, n).then_inc(ada_used, 1)

            @block.gpsimd
            def _(pool):
                pool.sem_inc(raw_ready, WR)
                pool.sem_inc(conv_taken, 2)

            @block.scalar
            def _(act):
                act.wait_ge(s_c, 16)
                nc.scalar.activation(c_act[:, 0, :], c_col[:], ACT.Exp, scale=-1.0).then_inc(*A.step("c_exp"))
                for t in range(TT):
                    act.wait_ge(s_x, 16 * TT)
                    nc.scalar.activation(xn[:, t, :], x_tok[:, t, :], ACT.Square, accum_out=stat[:, 0, t:t + 1]).then_inc(*A.step(f"sq{t}"))
                act.wait_ge(*A.after(f"sq{TT - 1}"))
                act.wait_ge(*V.after("eps"))
                nc.scalar.activation(stat[:, 1, :], stat[:, 0, :], ACT.Sqrt, bias=eps[:], scale=1.0 / D).then_inc(*A.step("std"))
                act.wait_ge(*V.after("scale1"))
                for k in range(KT):
                    act.wait_ge(*E.after(f"xT{k}"))
                    nc.scalar.activation(hT[:, k, :], xT_ps[k % 2][:], ACT.Identity, bias=mod[:, SH1 + k:SH1 + k + 1],
                                         scale=scale1[:, k:k + 1]).then_inc(*A.step(f"h{k}"))

                def take(slot, done, free):
                    act.wait_ge(w_used, done)
                    if free is not None:
                        act.wait_ge(raw_used, free)
                    nc.scalar.activation(raw[:, slot, 3:3 + T], proj_ps[slot][:], ACT.Copy).then_inc(raw_ready, 1)

                act.wait_ge(*V.after("pads"))
                for b in range(WR):
                    take(b, b + 1, None)
                with act.Fori(1, N_SC // WR) as i:
                    for b in range(WR):
                        take(b, i * WR + (b + 1), i * WR + (b + 1 - WR))
                with act.Fori(N_SC // WR, (N_SC + N_QKV) // WR) as i:
                    for b in range(WR):
                        take(b, i * WR + (b + 1), i * WR + (b + 1 - WR))
                        act.wait_ge(conv_done, i * WR + (b + 1 - N_SC))
                        nc.scalar.activation(qkvT[:, i * WR + (b - N_SC), :], acc[:, b % 2, :], ACT.Silu).then_inc(conv_taken, 1)
                for b in range(N_Z):
                    act.wait_ge(w_used, N_SC + N_QKV + b + 1)
                    nc.scalar.activation(zT[:, b, :], proj_ps[b][:], ACT.Silu).then_inc(raw_ready, 1)

            @block.vector
            def _(dve):
                nc.vector.memset(raw[:, :, 0:3], 0.0).then_inc(*V.step("pads"))
                nc.vector.memset(upad[:, 0:2], 0.0).then_inc(*V.step("pads_u"))
                nc.vector.memset(eps[:], EPS).then_inc(*V.step("eps"))
                dve.wait_ge(*A.after("c_exp"))
                nc.vector.tensor_scalar(c_act[:, 1, :], c_act[:, 0, :], 1.0, None, ALU.add).then_inc(*V.step("c_plus"))
                dve.wait_ge(*V.after("c_plus"))
                nc.vector.reciprocal(c_act[:, 0, :], c_act[:, 1, :]).then_inc(*V.step("c_recip"))
                dve.wait_ge(*V.after("c_recip"))
                nc.vector.tensor_tensor(c_act[:, 2, :], c_act[:, 0, :], c_col[:], ALU.mult).then_inc(*V.step("c_silu"))
                dve.wait_ge(*A.after("std"))
                nc.vector.reciprocal(stat[:, 2, :], stat[:, 1, :]).then_inc(*V.step("rstd"))
                dve.wait_ge(*V.after("rstd"))
                for t in range(TT):
                    nc.vector.tensor_scalar(xn[:, t, :], x_tok[:, t, :], stat[:, 2, t:t + 1], None, ALU.mult).then_inc(*V.step(f"xn{t}"))
                dve.wait_ge(ada_used, NA1)
                dve.wait_ge(s_small, 16 * 8)
                nc.vector.tensor_tensor(mod[:, SH1:SC1 + KT], mod_ps[:, SH1:SC1 + KT], b_ada[:, SH1:SC1 + KT], ALU.add).then_inc(*V.step("mod1"))
                dve.wait_ge(*V.after("mod1"))
                nc.vector.tensor_scalar(scale1[:], mod[:, SC1:SC1 + KT], 1.0, None, ALU.add).then_inc(*V.step("scale_p"))
                dve.wait_ge(*V.after("scale_p"))
                nc.vector.tensor_tensor(scale1[:], scale1[:], norms[:, 0, :], ALU.mult).then_inc(*V.step("scale1"))

                n_chain = 0
                for j in range(N_SC // 3):
                    c, x, b = (3 * j + m for m in range(3))
                    dve.wait_ge(raw_ready, WR + x + 1)
                    nc.vector.tensor_tensor(upad[:, 2:2 + T], raw[:, c % WR, 3:3 + T], raw[:, x % WR, 3:3 + T], ALU.mult).then_inc(raw_used, 2)
                    dve.wait_ge(raw_used, 3 * j + 2)
                    nc.vector.tensor_scalar(conv[:, 0, :], upad[:, 2:2 + T], sc_w[:, j, 2:3], None, ALU.mult).then_inc(conv_chain, 1)
                    for k in (1, 0):
                        n_chain += 1
                        dve.wait_ge(conv_chain, n_chain)
                        nc.vector.scalar_tensor_tensor(conv[:, 2 - k, :], upad[:, k:k + T], sc_w[:, j, k:k + 1], conv[:, 1 - k, :],
                                                       ALU.mult, ALU.add).then_inc(conv_chain, 1)
                    n_chain += 1
                    dve.wait_ge(conv_chain, n_chain)
                    dve.wait_ge(raw_ready, WR + b + 1)
                    nc.vector.tensor_tensor(scT[:, j, :], conv[:, 2, :], raw[:, b % WR, 3:3 + T], ALU.mult).then_inc(raw_used, 1)
                base = n_chain
                with dve.Fori(0, N_QKV // WR) as i:
                    for b in range(WR):
                        dve.wait_ge(raw_ready, i * WR + (WR + N_SC + b + 1))
                        chain = lambda k: i * (3 * WR) + (base + 3 * b + k)
                        nc.vector.tensor_scalar(conv[:, 0, :], raw[:, b, 3:3 + T], dn_w[:, i * WR + b, 3:4], None, ALU.mult).then_inc(conv_chain, 1)
                        dve.wait_ge(conv_chain, chain(1))
                        nc.vector.scalar_tensor_tensor(conv[:, 1, :], raw[:, b, 2:2 + T], dn_w[:, i * WR + b, 2:3], conv[:, 0, :],
                                                       ALU.mult, ALU.add).then_inc(conv_chain, 1)
                        dve.wait_ge(conv_chain, chain(2))
                        nc.vector.scalar_tensor_tensor(conv[:, 2, :], raw[:, b, 1:1 + T], dn_w[:, i * WR + b, 1:2], conv[:, 1, :],
                                                       ALU.mult, ALU.add).then_inc(conv_chain, 1)
                        dve.wait_ge(conv_chain, chain(3))
                        dve.wait_ge(conv_taken, i * WR + (b + 1))
                        nc.vector.scalar_tensor_tensor(acc[:, b % 2, :], raw[:, b, 0:T], dn_w[:, i * WR + b, 0:1], conv[:, 2, :],
                                                       ALU.mult, ALU.add).then_inc(conv_done, 1)
                        dve.wait_ge(conv_done, i * WR + (b + 1))
                        dve.sem_inc(raw_used, 1)
                for n in range(2):
                    dve.wait_ge(ab_done, n + 1)
                    nc.vector.tensor_copy(abT[:, n, :], ab_ps[n][0:H, :]).then_inc(last_v, 1)
                dve.wait_ge(ada_used, NA)
                nc.vector.tensor_tensor(mod[:, GT1:MOD], mod_ps[:, GT1:MOD], b_ada[:, GT1:MOD], ALU.add).then_inc(last_v, 1)


def delta_stage(nc, a, env):
    g_ = env
    bank, C, eps = g_["bank"], g_["C"], g_["eps"]
    qkvT, zT, abT = g_["qkvT"], g_["zT"], g_["abT"]
    sel_head, sel_pair, carry = g_["sel_head"], g_["sel_pair"], g_["carry"]
    sb, sem = g_["sb"], g_["sem"]
    G2 = range(2)
    with ExitStack() as ctx:
        sq = sb(ctx, "l2_square", [P, 2, T])
        nrm = sb(ctx, "l2_norm", [P, 2, T])
        ga = sb(ctx, "gate_work", [H, 8, T])
        rows = sb(ctx, "decay_rows", [H, 3, T])
        exp_a = sb(ctx, "exp_a", [H, 1])
        cols = sb(ctx, "decay_cols", [P, 3, TT, H])
        neg_g = sb(ctx, "neg_g", [P, TT, H])
        e_kd = sb(ctx, "e_kd", [P, TT, H])
        e_g = sb(ctx, "e_g", [P, TT, H])
        be_g = sb(ctx, "be_g", [P, TT, H])
        dec = sb(ctx, "decay", [P, 2, HJ, P])
        decT = sb(ctx, "decayT", [P, 2, HJ, P])
        kbT = sb(ctx, "kbT", [P, HJ, P])
        qgT = sb(ctx, "qgT", [P, HJ, P])
        egT = sb(ctx, "egT", [P, HJ, P])
        kdec = sb(ctx, "kdec", [P, H, DK])
        rw = sb(ctx, "rhs_w", [P, H, DK])
        rv = sb(ctx, "rhs_v", [P, H, DK])
        L, LT = (sb(ctx, n, [P, HJ, P]) for n in ("L", "LT"))
        aT = sb(ctx, "attnT", [P, 2, HJ, P])
        W = {(n, g): sb(ctx, f"{n}_{g}", [P, HJ, P]) for g in G2
             for n in ("A", "AT", "CT", "F", "B", "BT", "PT", "QT")}
        u = sb(ctx, "u", [P, 2, HJ, DK])
        wT = sb(ctx, "wT", [P, HJ, P])
        qkv = sb(ctx, "qkv_tile", [P, 12, P])
        S = sb(ctx, "state", [P, HJ, DK])
        Sd = sb(ctx, "state_decayed", [P, HJ, DK])
        vn = sb(ctx, "v_new", [P, 2, HJ, DK])
        oS = sb(ctx, "o_state", [P, 2, HJ, DK])
        o = sb(ctx, "o", [P, 2, HJ, DK])
        on = sb(ctx, "o_normed", [P, HJ, 2, DK])
        ost = sb(ctx, "o_stat", [P, 3, H])

        pre_v = ["a_bias", "a_max", "a_neg", "a_min", "b_plus", "beta", "softplus", "g", "G", "G_left", "cols", "neg_g", "be_g", "S0"]
        pre_v += ["sq0", "sq1"] + [x for j in range(8) for x in ([f"inv{j}", f"unit{j}"] + ([f"sq{j + 2}"] if j < 6 else []))]
        pre_a = ["exp_b", "exp_a", "exp_x", "log", "e_kd", "e_g"] + [f"norm{j}" for j in range(8)]
        pre_e = ["cols"] + [f"ss{j}" for j in range(8)]
        loop_v = ["pre0", "preT0", "pre1", "preT1", "kb", "kdec", "rw", "rv", "qg"]
        for g in G2:
            loop_v += [f"L{g}", f"LT{g}", f"aT{g}"]
        levels_v = ["P1", "P2", "P3", "P4", "MT", "Q1", "TT"]
        loop_v += [f"{x}{g}" for x in levels_v for g in G2] + ["u0", "u1"]
        for c in G2:
            loop_v += [f"Sd{c}", f"vn{c}0", f"vn{c}1", f"S{c}", f"o{c}"]
        loop_v += ["osq", "oss", "ostd", "on", "oT"]
        loop_a = ["egT"] + [f"dec{g}{j}" for g in G2 for j in range(HJ)] + [f"decT{g}{j}" for g in G2 for j in range(HJ)]
        loop_a += [f"{x}{g}" for x in ["A2", "A2T", "A4", "A4T", "A8", "P", "M", "M2"] for g in G2] + ["wT"]
        loop_a += ["oi00", "oi01", "oi10", "oi11", "ostd"]
        loop_p = ["tile"] + [f"{x}{g}" for g in G2 for x in ("near", "far", "nearT", "farT")]
        loop_e = ["grow0", "grow1", "betaT", "GT", "kX", "vX"] + [f"{x}{g}" for g in G2 for x in ("kk", "kkT", "qk")]
        loop_e += [f"{x}{g}" for x in ["A2", "A2T", "A4", "A4T", "PA2", "A8", "PA4", "PA8", "P", "M", "MT", "M2", "Q1", "TT"] for g in G2]
        loop_e += ["u0", "u1", "wT"]
        for c in G2:
            loop_e += [f"wS{c}0", f"wS{c}1", f"oi{c}0", f"oi{c}1", f"dS{c}", f"oa{c}"]
        loop_e += ["oT"]
        sv, sa, se, spl = (sem(ctx, f"dn_{n}") for n in ("vector", "scalar", "tensor", "pool"))
        V0, A0, E0 = Steps(sv, pre_v), Steps(sa, pre_a), Steps(se, pre_e)
        V, A, E = Steps(sv, loop_v, len(pre_v)), Steps(sa, loop_a, len(pre_a)), Steps(se, loop_e, len(pre_e))
        Q = Steps(spl, loop_p)
        held = sem(ctx, "held")

        def flat(t):
            return t.rearrange("p j m -> p (j m)")

        def mask(name):
            return C[name].unsqueeze(1).to_broadcast([P, HJ, P])

        def b4(n):
            return bank[n][:].rearrange("p (j m) -> p j m", j=HJ)

        with nc.Block() as block:
            @block.scalar
            def _(act):
                nc.scalar.activation(ga[:, 4, :], abT[:, 1, :], ACT.Exp, scale=-1.0).then_inc(*A0.step("exp_b"))
                nc.scalar.activation(exp_a[:], g_["a_log"][:], ACT.Exp).then_inc(*A0.step("exp_a"))
                act.wait_ge(*V0.after("a_min"))
                nc.scalar.activation(ga[:, 5, :], ga[:, 3, :], ACT.Exp).then_inc(*A0.step("exp_x"))
                act.wait_ge(*A0.after("exp_x"))
                nc.scalar.activation(ga[:, 6, :], ga[:, 5, :], ACT.Ln, bias=1.0).then_inc(*A0.step("log"))
                act.wait_ge(*V0.after("cols"))
                nc.scalar.activation(e_kd[:], cols[:, 2], ACT.Exp).then_inc(*A0.step("e_kd"))
                nc.scalar.activation(e_g[:], cols[:, 0], ACT.Exp).then_inc(*A0.step("e_g"))
                for j in range(8):
                    act.wait_ge(*E0.after(f"ss{j}"))
                    if j >= 2:
                        act.wait_ge(*V0.after(f"unit{j - 2}"))
                    nc.scalar.activation(nrm[:, j % 2, :], bank[j % 2][:], ACT.Sqrt, bias=eps[:]).then_inc(*A0.step(f"norm{j}"))
                with act.Fori(0, TT) as tt:
                    act.wait_ge(*E.after("GT", tt))
                    nc.scalar.activation(flat(egT[:]), bank[3][:], ACT.Exp).then_inc(*A.step("egT"))
                    for d, v, bias, name in ((dec, "pre", cols[:, 0], "dec"), (decT, "preT", neg_g[:], "decT")):
                        for g in G2:
                            act.wait_ge(*V.after(f"{v}{g}", tt))
                            for j in range(HJ):
                                h = 2 * j + g
                                nc.scalar.activation(d[:, g, j, :], d[:, g, j, :], ACT.Exp, bias=bias[:, tt, h:h + 1]).then_inc(*A.step(f"{name}{g}{j}"))

                    def take(name, dst, src, g):
                        act.wait_ge(*E.after(f"{name}{g}", tt))
                        nc.scalar.activation(flat(dst[:]), bank[src][:], ACT.Copy).then_inc(*A.step(f"{name}{g}"))

                    b0 = (4, 7)
                    b1 = (5, 0)
                    for name, dst, bs in (("A2", "B", b0), ("A2T", "BT", b1), ("A4", "A", b0), ("A4T", "AT", b1), ("A8", "B", b0),
                                          ("P", "BT", b0), ("M", "A", b1), ("M2", "B", b0)):
                        for g in G2:
                            if name == "A4T":
                                act.wait_ge(*V.after(f"P1{g}", tt))
                            take(name, W[dst, g], bs[g], g)
                    act.wait_ge(*E.after("wT", tt))
                    nc.scalar.activation(flat(wT[:]), bank[2][:], ACT.Copy).then_inc(*A.step("wT"))
                    for c in G2:
                        r = slice(CH * c, CH * c + CH)
                        for g in G2:
                            act.wait_ge(*E.after(f"oi{c}{g}", tt))
                            nc.scalar.activation(oS[r, g], bank[5 + g][r, 0:HJ * DK], ACT.Copy).then_inc(*A.step(f"oi{c}{g}"))
                    act.wait_ge(*V.after("oss", tt))
                    nc.scalar.activation(ost[:, 1, :], ost[:, 0, :], ACT.Sqrt, bias=eps[:], scale=1.0 / DK).then_inc(*A.step("ostd"))

            @block.gpsimd
            def _(pool):
                with pool.Fori(0, TT) as tt:
                    pool.wait_ge(*V.after("oT", tt, 1))
                    nc.gpsimd.tensor_copy(qkv[:], qkvT[:, :, bass.ds(tt * P, P)]).then_inc(*Q.step("tile"))
                    for g in G2:
                        pool.wait_ge(*V.after(f"L{g}", tt))
                        nc.gpsimd.tensor_tensor(W["A", g][:], L[:], mask("neg_near"), ALU.mult).then_inc(*Q.step(f"near{g}"))
                        nc.gpsimd.tensor_tensor(W["F", g][:], L[:], mask("neg_far"), ALU.mult).then_inc(*Q.step(f"far{g}"))
                        pool.wait_ge(*V.after(f"LT{g}", tt))
                        nc.gpsimd.tensor_tensor(W["AT", g][:], LT[:], mask("neg_nearT"), ALU.mult).then_inc(*Q.step(f"nearT{g}"))
                        nc.gpsimd.tensor_tensor(W["CT", g][:], LT[:], mask("neg_farT"), ALU.mult).then_inc(*Q.step(f"farT{g}"))

            @block.tensor
            def _(pe):
                pe.wait_ge(*V0.after("G_left"))
                for n in range(3):
                    for t in range(TT):
                        m = (n * TT + t) * H
                        last = nc.tensor.transpose(bank[2][:, m:m + H], rows[:, n, t * P:(t + 1) * P], C["ident"][0:H, 0:H])
                last.then_inc(*E0.step("cols"))
                for j in range(8):
                    pe.wait_ge(*V0.after(f"sq{j}"))
                    if j >= 2:
                        pe.wait_ge(*A0.after(f"norm{j - 2}"))
                    nc.tensor.matmul(bank[j % 2][:], C["headsum"], sq[:, j % 2, :], start=True, stop=True).then_inc(*E0.step(f"ss{j}"))
                pe.wait_ge(*V0.after("unit7"))
                pe.wait_ge(*A0.after("norm7"))
                pe.wait_ge(*V0.after("cols"))
                with pe.Fori(0, TT) as tt:
                    tok = bass.ds(tt * P, P)
                    pe.wait_ge(*V.after("oT", tt, 1))

                    def group(name, n, products, transpose=False):
                        for j in range(HJ):
                            lhs, rhs = products(j)
                            if transpose:
                                last = nc.tensor.transpose(bank[n][:, j * P:(j + 1) * P], lhs, C["ident"])
                            else:
                                last = nc.tensor.matmul(bank[n][:, j * P:(j + 1) * P], lhs, rhs, start=True, stop=True)
                        last.then_inc(*E.step(name))

                    for g in G2:
                        group(f"grow{g}", g, lambda j: (sel_head[:, 2 * j + g, :], rows[:, 0, tok]))
                    group("betaT", 2, lambda j: (sel_pair[:, j, :], rows[:, 1, tok]))
                    group("GT", 3, lambda j: (sel_pair[:, j, :], rows[:, 0, tok]))
                    pe.wait_ge(*Q.after("tile", tt))
                    group("kX", 4, lambda j: (qkv[:, HJ + j, :], None), transpose=True)
                    group("vX", 5, lambda j: (qkv[:, 2 * HJ + j, :], None), transpose=True)
                    pe.wait_ge(*V.after("kb", tt))
                    for g, banks in ((0, (6, 7, 0)), (1, (1, 2, 3))):
                        r = slice(DK * g, DK * g + DK)
                        if g == 1:
                            pe.wait_ge(*A.after("egT", tt))
                        group(f"kk{g}", banks[0], lambda j: (kbT[r, j, :], qkv[r, HJ + j, :]))
                        group(f"kkT{g}", banks[1], lambda j: (qkv[r, HJ + j, :], kbT[r, j, :]))
                        group(f"qk{g}", banks[2], lambda j: (qkv[r, HJ + j, :], qkv[r, j, :]))
                    b0, b1, b2 = (4, 7), (5, 0), (6, 1)

                    def level(name, banks, lhs, rhs, waits, transpose=False):
                        for g in G2:
                            for w in waits(g):
                                pe.wait_ge(*w)
                            group(f"{name}{g}", banks[g], lambda j: (W[lhs, g][:, j, :], rhs and W[rhs, g][:, j, :]), transpose)

                    VA, AA, PA = (lambda n: V.after(n, tt)), (lambda n: A.after(n, tt)), (lambda n: Q.after(n, tt))
                    level("A2", b0, "AT", "A", lambda g: [PA(f"nearT{g}"), VA("rv"), VA(f"LT{g}"), VA(f"aT{g}")])
                    level("A2T", b1, "A", "AT", lambda g: [])
                    level("A4", b0, "BT", "B", lambda g: [AA(f"A2{g}"), AA(f"A2T{g}")])
                    level("A4T", b1, "B", "BT", lambda g: [])
                    level("PA2", b2, "B", "PT", lambda g: [VA(f"P1{g}")])
                    level("A8", b0, "AT", "A", lambda g: [AA(f"A4{g}"), AA(f"A4T{g}")])
                    level("PA4", b2, "A", "PT", lambda g: [VA(f"P2{g}")])
                    level("PA8", b1, "B", "PT", lambda g: [AA(f"A8{g}"), VA(f"P3{g}")])
                    level("P", b0, "PT", None, lambda g: [VA(f"P4{g}")], transpose=True)
                    level("M", b1, "CT", "BT", lambda g: [PA(f"farT{g}"), AA(f"P{g}")])
                    level("MT", b2, "BT", "CT", lambda g: [])
                    level("M2", b0, "QT", "A", lambda g: [AA(f"M{g}"), VA(f"MT{g}")])
                    level("Q1", b1, "A", "PT", lambda g: [])
                    level("TT", b2, "B", "QT", lambda g: [AA(f"M2{g}"), VA(f"Q1{g}")])
                    for g in G2:
                        pe.wait_ge(*VA(f"TT{g}"))
                        for j in range(HJ):
                            last = nc.tensor.matmul(bank[b0[g]][:, j * DK:(j + 1) * DK], W["AT", g][:, j, :], rv[:, 2 * j + g, :], start=True, stop=True)
                        last.then_inc(*E.step(f"u{g}"))
                    for j in range(HJ):
                        for g in G2:
                            last = nc.tensor.matmul(bank[2][DK * g:DK * g + DK, j * P:(j + 1) * P], rw[:, 2 * j + g, :], W["AT", g][:, j, :], start=True, stop=True)
                    last.then_inc(*E.step("wT"))
                    for c in G2:
                        r = slice(CH * c, CH * c + CH)
                        if c == 0:
                            pe.wait_ge(*AA("wT"))
                            pe.wait_ge(*VA("u1"))
                        else:
                            pe.wait_ge(*VA("S0"))
                        pe.sem_inc(held, 1)
                        for g in G2:
                            q = slice(DK * g, DK * g + DK)
                            for j in range(HJ):
                                last = nc.tensor.matmul(bank[3 + g][r, j * DK:(j + 1) * DK], wT[q, j, r], S[q, j, :], start=True, stop=True)
                            last.then_inc(*E.step(f"wS{c}{g}"))
                        for g in G2:
                            q = slice(DK * g, DK * g + DK)
                            if c == 1:
                                pe.wait_ge(*AA(f"oi0{g}"))
                                pe.sem_inc(held, 1)
                            for j in range(HJ):
                                last = nc.tensor.matmul(bank[5 + g][r, j * DK:(j + 1) * DK], qgT[q, j, r], S[q, j, :], start=True, stop=True)
                            last.then_inc(*E.step(f"oi{c}{g}"))
                        pe.wait_ge(*VA(f"vn{c}1"))
                        pe.sem_inc(held, 1)
                        for j in range(HJ):
                            for g in G2:
                                last = nc.tensor.matmul(bank[0][DK * g:DK * g + DK, j * DK:(j + 1) * DK], kdec[r, 2 * j + g, :], vn[r, g, j, :], start=True, stop=True)
                        last.then_inc(*E.step(f"dS{c}"))
                        if c == 1:
                            pe.wait_ge(*VA("o0"))
                            pe.sem_inc(held, 1)
                        for g in G2:
                            for j in range(HJ):
                                m = (g * HJ + j) * DK
                                last = nc.tensor.matmul(bank[7][r, m:m + DK], aT[r, g, j, r], vn[r, g, j, :], start=True, stop=True)
                        last.then_inc(*E.step(f"oa{c}"))
                    pe.wait_ge(*VA("on"))
                    group("oT", 1, lambda j: (on[:, j].rearrange("p g d -> p (g d)"), None), transpose=True)

            @block.vector
            def _(dve):
                nc.vector.tensor_scalar(ga[:, 0, :], abT[:, 0, :], g_["dt_bias"][:], None, ALU.add).then_inc(*V0.step("a_bias"))
                dve.wait_ge(*V0.after("a_bias"))
                nc.vector.tensor_scalar(ga[:, 1, :], ga[:, 0, :], 0.0, None, ALU.max).then_inc(*V0.step("a_max"))
                nc.vector.tensor_scalar(ga[:, 2, :], ga[:, 0, :], -1.0, None, ALU.mult).then_inc(*V0.step("a_neg"))
                dve.wait_ge(*V0.after("a_neg"))
                nc.vector.tensor_tensor(ga[:, 3, :], ga[:, 0, :], ga[:, 2, :], ALU.min).then_inc(*V0.step("a_min"))
                dve.wait_ge(*A0.after("exp_b"))
                nc.vector.tensor_scalar(ga[:, 7, :], ga[:, 4, :], 1.0, None, ALU.add).then_inc(*V0.step("b_plus"))
                dve.wait_ge(*V0.after("b_plus"))
                nc.vector.reciprocal(rows[:, 1, :], ga[:, 7, :]).then_inc(*V0.step("beta"))
                dve.wait_ge(*A0.after("log"))
                nc.vector.tensor_tensor(ga[:, 0, :], ga[:, 1, :], ga[:, 6, :], ALU.add).then_inc(*V0.step("softplus"))
                dve.wait_ge(*V0.after("softplus"))
                nc.vector.tensor_scalar(ga[:, 2, :], ga[:, 0, :], exp_a[:], -1.0, ALU.mult, ALU.mult).then_inc(*V0.step("g"))
                dve.wait_ge(*V0.after("g"))
                nc.vector.tensor_tensor_scan(rows[:, 0, :], carry, ga[:, 2, :], 0.0, ALU.mult, ALU.add).then_inc(*V0.step("G"))
                dve.wait_ge(*V0.after("G"))
                by_chunk = rows[:, 0, :].rearrange("h (n c) -> h n c", c=CH)
                nc.vector.tensor_tensor(rows[:, 2, :].rearrange("h (n c) -> h n c", c=CH), by_chunk[:, :, CH - 1:CH].to_broadcast([H, T // CH, CH]),
                                        by_chunk, ALU.subtract).then_inc(*V0.step("G_left"))
                dve.wait_ge(*E0.after("cols"))
                nc.vector.tensor_copy(cols[:].rearrange("p a t h -> p (a t h)"), bank[2][:, 0:3 * TT * H]).then_inc(*V0.step("cols"))
                dve.wait_ge(*V0.after("cols"))
                nc.vector.tensor_scalar(neg_g[:], cols[:, 0], -1.0, None, ALU.mult).then_inc(*V0.step("neg_g"))
                dve.wait_ge(*A0.after("e_g"))
                nc.vector.tensor_tensor(be_g[:], e_g[:], cols[:, 1], ALU.mult).then_inc(*V0.step("be_g"))
                nc.vector.memset(S[:], 0.0).then_inc(*V0.step("S0"))

                def square(j):
                    if j >= 2:
                        dve.wait_ge(*E0.after(f"ss{j - 2}"))
                    nc.vector.tensor_tensor(sq[:, j % 2, :], qkvT[:, j, :], qkvT[:, j, :], ALU.mult).then_inc(*V0.step(f"sq{j}"))

                square(0)
                square(1)
                for j in range(8):
                    dve.wait_ge(*A0.after(f"norm{j}"))
                    nc.vector.reciprocal(nrm[:, j % 2, :], nrm[:, j % 2, :]).then_inc(*V0.step(f"inv{j}"))
                    dve.wait_ge(*V0.after(f"inv{j}"))
                    nc.vector.scalar_tensor_tensor(qkvT[:, j, :], nrm[:, j % 2, :], DK ** -0.5 if j < HJ else 1.0, qkvT[:, j, :],
                                                   ALU.mult, ALU.mult).then_inc(*V0.step(f"unit{j}"))
                    if j < 6:
                        square(j + 2)

                with dve.Fori(0, TT) as tt:
                    tok = bass.ds(tt * P, P)
                    VA, AA, EA, PA = ((lambda n, s=s: s.after(n, tt)) for s in (V, A, E, Q))

                    def per_head(c):
                        return c[:, tt, :].unsqueeze(2).to_broadcast([P, H, DK])

                    for g in G2:
                        dve.wait_ge(*EA(f"grow{g}"))
                        nc.vector.scalar_tensor_tensor(dec[:, g], b4(g), -1.0, mask("causal"), ALU.mult, ALU.add).then_inc(*V.step(f"pre{g}"))
                        nc.vector.tensor_tensor(decT[:, g], b4(g), mask("causalT"), ALU.add).then_inc(*V.step(f"preT{g}"))
                    dve.wait_ge(*PA("tile"))
                    dve.wait_ge(*EA("betaT"))
                    nc.vector.tensor_tensor(kbT[:], qkv[:, HJ:2 * HJ, :], b4(2), ALU.mult).then_inc(*V.step("kb"))
                    dve.wait_ge(*EA("kX"))
                    heads = bank[4][:].rearrange("p (h d) -> p h d", h=H)
                    nc.vector.tensor_tensor(kdec[:], heads, per_head(e_kd), ALU.mult).then_inc(*V.step("kdec"))
                    nc.vector.tensor_tensor(rw[:], heads, per_head(be_g), ALU.mult).then_inc(*V.step("rw"))
                    dve.wait_ge(*EA("vX"))
                    nc.vector.tensor_tensor(rv[:], bank[5][:].rearrange("p (h d) -> p h d", h=H), per_head(cols[:, 1]), ALU.mult).then_inc(*V.step("rv"))
                    dve.wait_ge(*AA("egT"))
                    nc.vector.tensor_tensor(qgT[:], qkv[:, 0:HJ, :], egT[:], ALU.mult).then_inc(*V.step("qg"))
                    for g, banks in ((0, (6, 7, 0)), (1, (1, 2, 3))):
                        dve.wait_ge(*AA(f"decT{g}{HJ - 1}"))
                        dve.wait_ge(*EA(f"kk{g}"))
                        if g:
                            dve.wait_ge(*PA("far0"))
                        nc.vector.tensor_tensor(L[:], b4(banks[0]), dec[:, g], ALU.mult).then_inc(*V.step(f"L{g}"))
                        dve.wait_ge(*EA(f"kkT{g}"))
                        if g:
                            dve.wait_ge(*PA("farT0"))
                        nc.vector.tensor_tensor(LT[:], b4(banks[1]), decT[:, g], ALU.mult).then_inc(*V.step(f"LT{g}"))
                        dve.wait_ge(*EA(f"qk{g}"))
                        nc.vector.tensor_tensor(aT[:, g], b4(banks[2]), decT[:, g], ALU.mult).then_inc(*V.step(f"aT{g}"))
                    b1, b2 = (5, 0), (6, 1)

                    def plus(name, dst, add, banks, product):
                        for g in G2:
                            dve.wait_ge(*EA(f"{product}{g}"))
                            nc.vector.tensor_tensor(flat(W[dst, g][:]), flat(W[add, g][:]), bank[banks[g]][:], ALU.add).then_inc(*V.step(f"{name}{g}"))

                    for g in G2:
                        dve.wait_ge(*PA(f"nearT{g}"))
                        nc.vector.tensor_tensor(W["PT", g][:], W["AT", g][:], mask("ident"), ALU.add).then_inc(*V.step(f"P1{g}"))
                    dve.wait_ge(*VA("P11"))
                    plus("P2", "PT", "PT", b2, "PA2")
                    dve.wait_ge(*VA("P21"))
                    plus("P3", "PT", "PT", b2, "PA4")
                    dve.wait_ge(*VA("P31"))
                    plus("P4", "PT", "PT", b1, "PA8")
                    for g in G2:
                        dve.wait_ge(*EA(f"MT{g}"))
                        nc.vector.tensor_copy(flat(W["QT", g][:]), bank[b2[g]][:]).then_inc(*V.step(f"MT{g}"))
                    for g in G2:
                        dve.wait_ge(*EA(f"M2{g}"))
                        dve.wait_ge(*EA(f"Q1{g}"))
                        nc.vector.tensor_tensor(flat(W["QT", g][:]), flat(W["PT", g][:]), bank[b1[g]][:], ALU.add).then_inc(*V.step(f"Q1{g}"))
                    dve.wait_ge(*VA("Q11"))
                    plus("TT", "AT", "QT", b2, "TT")
                    for g in G2:
                        dve.wait_ge(*EA(f"u{g}"))
                        nc.vector.tensor_copy(u[:, g].rearrange("p j d -> p (j d)"), bank[(4, 7)[g]][:, 0:HJ * DK]).then_inc(*V.step(f"u{g}"))
                    for c in G2:
                        r = slice(CH * c, CH * c + CH)
                        last = CH * c + CH - 1
                        nc.vector.tensor_tensor(Sd[:], S[:], egT[:, :, last:last + 1].to_broadcast([P, HJ, DK]), ALU.mult).then_inc(*V.step(f"Sd{c}"))
                        for g in G2:
                            dve.wait_ge(*EA(f"wS{c}{g}"))
                            nc.vector.tensor_tensor(vn[r, g], u[r, g], bank[3 + g][r, 0:HJ * DK].rearrange("p (j d) -> p j d", j=HJ),
                                                    ALU.subtract).then_inc(*V.step(f"vn{c}{g}"))
                        dve.wait_ge(*EA(f"dS{c}"))
                        nc.vector.tensor_tensor(S[:], Sd[:], bank[0][:, 0:HJ * DK].rearrange("p (j d) -> p j d", j=HJ), ALU.add).then_inc(*V.step(f"S{c}"))
                        dve.wait_ge(*EA(f"oa{c}"))
                        dve.wait_ge(*AA(f"oi{c}1"))
                        nc.vector.tensor_tensor(o[r], oS[r], bank[7][r, :].rearrange("p (g j d) -> p g j d", g=2, j=HJ), ALU.add).then_inc(*V.step(f"o{c}"))
                        dve.wait_ge(*VA(f"S{c}"))
                    dve.wait_ge(*VA("o1"))
                    o8 = o[:].rearrange("p g j d -> p (g j) d")
                    sq8 = oS[:].rearrange("p g j d -> p (g j) d")
                    nc.vector.tensor_tensor(sq8, o8, o8, ALU.mult).then_inc(*V.step("osq"))
                    dve.wait_ge(*VA("osq"))
                    nc.vector.tensor_reduce(ost[:, 0, :], sq8, AX.X, ALU.add).then_inc(*V.step("oss"))
                    dve.wait_ge(*AA("ostd"))
                    nc.vector.reciprocal(ost[:, 2, :], ost[:, 1, :]).then_inc(*V.step("ostd"))
                    dve.wait_ge(*VA("ostd"))
                    nc.vector.tensor_tensor(on[:].rearrange("p j g d -> p g j d"), o[:],
                                            ost[:, 2, :].rearrange("p (g j) -> p g j", g=2).unsqueeze(3).to_broadcast([P, 2, HJ, DK]),
                                            ALU.mult).then_inc(*V.step("on"))
                    dve.wait_ge(*EA("oT"))
                    nc.vector.scalar_tensor_tensor(zT[:, :, tok], b4(1), g_["out_norm"][:], zT[:, :, tok], ALU.mult, ALU.mult).then_inc(*V.step("oT"))


def merge_stage(nc, a, env):
    g_ = env
    bank, C, mod, norms, stat, eps = g_["bank"], g_["C"], g_["mod"], g_["norms"], g_["stat"], g_["eps"]
    x_tok, hT, scT, oT = g_["x_tok"], g_["hT"], g_["scT"], g_["zT"]
    row_ffn = g_["row_ffn"]
    sb, sem = g_["sb"], g_["sem"]
    KM = 2 * KT + 2 * HJ
    with ExitStack() as ctx:
        row_mix = sb(ctx, "row_mix", [P, D])
        wm = sb(ctx, "w_merge", [P, 2, KM, P])
        w_mix = sb(ctx, "w_mix", [P, KT, D])
        sg = sb(ctx, "sigmoids", [P, 2, 2, T])
        part = sb(ctx, "branch", [P, 2, 2, T])
        merged = sb(ctx, "mergedT", [P, KT, T])
        diag = sb(ctx, "diag", [P, KT, P])
        gate = sb(ctx, "gate", [P, 2, KT])
        xn = sb(ctx, "y_scaled", [P, TT, D])
        tmp = xn
        ss = sb(ctx, "y_squares", [P, TT, 2])
        s_m = [sem(ctx, f"merge_landed{i}") for i in range(2)]
        s_mix = sem(ctx, "mix_landed")
        pre_v = ["gate0", "diag0", "gate1", "diag1"]
        pre_a = ["row0", "row1", "row2", "row3"]
        pre_e = ["row0", "row1", "row2", "row3"]
        loop_v = [f"{x}{b}" for b in range(2) for x in ("sc", "dn", "sum")]
        loop_a = [f"{x}{b}" for b in range(2) for x in ("sg_sc", "sg_dn")]
        loop_e = [f"{x}{b}" for b in range(2) for x in ("g_sc", "g_dn", "b_sc", "b_dn")]
        n_loop = KT // 2
        post_v = [f"{x}{t}" for t in range(TT) for x in ("ss", "rstd", "y0_", "y1_", "x", "rstd2_")]
        post_a = [f"{x}{t}" for t in range(TT) for x in ("sq0_", "sq1_", "std", "sqx", "std2_")] 
        post_e = [f"y{half}_{t}" for t in range(TT) for half in range(2)] 
        sv, sa, se = (sem(ctx, f"mg_{n}") for n in ("vector", "scalar", "tensor"))
        V0, A0, E0 = Steps(sv, pre_v), Steps(sa, pre_a), Steps(se, pre_e)
        V, A, E = Steps(sv, loop_v, len(pre_v)), Steps(sa, loop_a, len(pre_a)), Steps(se, loop_e, len(pre_e))
        V2, A2, E2 = (Steps(s, p, len(a0) + n_loop * len(lp)) for s, p, a0, lp in
                      ((sv, post_v, pre_v, loop_v), (sa, post_a, pre_a, loop_a), (se, post_e, pre_e, loop_e)))

        with nc.Block() as block:
            @block.sync
            def _(sp):
                for b in range(2):
                    sp.dma_start(wm[:, b], a["w_merge"][b]).then_inc(s_m[b], 16)
                sp.dma_start(w_mix[:], a["w_mix"]).then_inc(s_mix, 16)
                with sp.Fori(1, n_loop) as i:
                    for b in range(2):
                        sp.wait_ge(*E.after(f"b_dn{b}", i, 1))
                        sp.dma_start(wm[:, b], a["w_merge"][i * 2 + b]).then_inc(s_m[b], 16)

            @block.tensor
            def _(pe):
                for n in range(2):
                    pe.wait_ge(*V0.after(f"diag{n}"))
                    for half in range(2):
                        for k in range(HJ):
                            last = nc.tensor.matmul(bank[2 * n + half][:, k * P:(k + 1) * P], C["ones"], diag[:, HJ * half + k, :], start=True, stop=True)
                        last.then_inc(*E0.step(f"row{2 * n + half}"))
                pe.wait_ge(*A0.after("row3"))
                with pe.Fori(0, n_loop) as i:
                    for b in range(2):
                        pe.wait_ge(*V.after(f"sum{b}", i, 1))
                        pe.wait_ge(s_m[b], i * 16 + 16)
                        for n, (name, src, k0, kn) in enumerate((("g_sc", hT, 0, KT), ("g_dn", hT, KT, KT),
                                                                ("b_sc", scT, 2 * KT, HJ), ("b_dn", oT, 2 * KT + HJ, HJ))):
                            for k in range(kn):
                                last = nc.tensor.matmul(bank[4 * b + n][:], wm[:, b, k0 + k, :], src[:, k, :], start=(k == 0), stop=(k == kn - 1))
                            last.then_inc(*E.step(f"{name}{b}"))
                pe.wait_ge(*V.after("sum1", n_loop - 1))
                pe.wait_ge(s_mix, 16)
                for t in range(TT):
                    for half in range(2):
                        for k in range(KT):
                            last = nc.tensor.matmul(bank[2 * t + half][:], merged[:, k, t * P:(t + 1) * P], w_mix[:, k, half * 512:half * 512 + 512],
                                                    start=(k == 0), stop=(k == KT - 1))
                        last.then_inc(*E2.step(f"y{half}_{t}"))

            @block.scalar
            def _(act):
                for n in range(4):
                    act.wait_ge(*E0.after(f"row{n}"))
                    dst = (row_mix, row_ffn)[n // 2]
                    nc.scalar.activation(dst[:, 512 * (n % 2):512 * (n % 2) + 512], bank[n][:], ACT.Copy).then_inc(*A0.step(f"row{n}"))
                with act.Fori(0, n_loop) as i:
                    for b in range(2):
                        act.wait_ge(*V.after(f"sum{b}", i, 1))
                        for n, x in enumerate(("sc", "dn")):
                            act.wait_ge(*E.after(f"g_{x}{b}", i))
                            nc.scalar.activation(sg[:, b, n, :], bank[4 * b + n][:], ACT.Sigmoid).then_inc(*A.step(f"sg_{x}{b}"))
                for t in range(TT):
                    for half in range(2):
                        act.wait_ge(*E2.after(f"y{half}_{t}"))
                        nc.scalar.activation(tmp[:, t, half * 512:half * 512 + 512], bank[2 * t + half][:], ACT.Square,
                                             accum_out=ss[:, t, half:half + 1]).then_inc(*A2.step(f"sq{half}_{t}"))
                    act.wait_ge(*V2.after(f"ss{t}"))
                    nc.scalar.activation(stat[:, 1, t:t + 1], stat[:, 0, t:t + 1], ACT.Sqrt, bias=eps[:], scale=1.0 / D).then_inc(*A2.step(f"std{t}"))
                    act.wait_ge(*V2.after(f"x{t}"))
                    nc.scalar.activation(xn[:, t, :], x_tok[:, t, :], ACT.Square, accum_out=stat[:, 2, t:t + 1]).then_inc(*A2.step(f"sqx{t}"))
                    act.wait_ge(*A2.after(f"sqx{t}"))
                    nc.scalar.activation(stat[:, 3, t:t + 1], stat[:, 2, t:t + 1], ACT.Sqrt, bias=eps[:], scale=1.0 / D).then_inc(*A2.step(f"std2_{t}"))

            @block.vector
            def _(dve):
                for n, (col, norm) in enumerate(((GT1, 1), (GT2, 3))):
                    if n:
                        dve.wait_ge(*E0.after("row1"))
                    nc.vector.tensor_tensor(gate[:, n, :], mod[:, col:col + KT], norms[:, norm, :], ALU.mult).then_inc(*V0.step(f"gate{n}"))
                    dve.wait_ge(*V0.after(f"gate{n}"))
                    nc.vector.tensor_tensor(diag[:], C["ident"].unsqueeze(1).to_broadcast([P, KT, P]),
                                            gate[:, n, :].unsqueeze(2).to_broadcast([P, KT, P]), ALU.mult).then_inc(*V0.step(f"diag{n}"))
                with dve.Fori(0, n_loop) as i:
                    for b in range(2):
                        for n, x in enumerate(("sc", "dn")):
                            dve.wait_ge(*A.after(f"sg_{x}{b}", i))
                            dve.wait_ge(*E.after(f"b_{x}{b}", i))
                            nc.vector.tensor_tensor(part[:, b, n, :], sg[:, b, n, :], bank[4 * b + 2 + n][:], ALU.mult).then_inc(*V.step(f"{x}{b}"))
                        dve.wait_ge(*V.after(f"dn{b}", i))
                        nc.vector.tensor_tensor(merged[:, i * 2 + b, :], part[:, b, 0, :], part[:, b, 1, :], ALU.add).then_inc(*V.step(f"sum{b}"))
                for t in range(TT):
                    dve.wait_ge(*A2.after(f"sq1_{t}"))
                    nc.vector.tensor_tensor(stat[:, 0, t:t + 1], ss[:, t, 0:1], ss[:, t, 1:2], ALU.add).then_inc(*V2.step(f"ss{t}"))
                    dve.wait_ge(*A2.after(f"std{t}"))
                    nc.vector.reciprocal(stat[:, 0, t:t + 1], stat[:, 1, t:t + 1]).then_inc(*V2.step(f"rstd{t}"))
                    dve.wait_ge(*V2.after(f"rstd{t}"))
                    for half in range(2):
                        nc.vector.scalar_tensor_tensor(tmp[:, t, half * 512:half * 512 + 512], bank[2 * t + half][:], stat[:, 0, t:t + 1],
                                                       row_mix[:, half * 512:half * 512 + 512], ALU.mult, ALU.mult).then_inc(*V2.step(f"y{half}_{t}"))
                    dve.wait_ge(*V2.after(f"y1_{t}"))
                    nc.vector.tensor_tensor(x_tok[:, t, :], x_tok[:, t, :], tmp[:, t, :], ALU.add).then_inc(*V2.step(f"x{t}"))
                    dve.wait_ge(*A2.after(f"std2_{t}"))
                    nc.vector.reciprocal(stat[:, 2, t:t + 1], stat[:, 3, t:t + 1]).then_inc(*V2.step(f"rstd2_{t}"))


def retrieve_stage(nc, a, env):
    g_ = env
    bank, C, mod, norms, stat, x_tok, h_hi, h_lo = (g_[n] for n in ("bank", "C", "mod", "norms", "stat", "x_tok", "h_hi", "h_lo"))
    idxT, gateT = g_["idxT"], g_["gateT"]
    sb, sem = g_["sb"], g_["sem"]
    K2 = TOPK * TOPK
    with ExitStack() as ctx:
        xn = sb(ctx, "xn2", [P, TT, D])
        h_raw = sb(ctx, "h_raw", [P, 2, T])
        scale2 = sb(ctx, "scale2", [P, KT])
        wq = sb(ctx, "w_q", [P, 2, KT, P])
        wq_hi = sb(ctx, "w_q_hi", [P, 2, KT, P], F32R)
        wq_lo = sb(ctx, "w_q_lo", [P, 2, KT, P], F32R)
        keys = sb(ctx, "sub_keys", [P, 2 * PH, NKEYS])
        qT = sb(ctx, "queryT", [P, 2, T])
        s = sb(ctx, "scores", [P, 2, TT, NKEYS])
        v = sb(ctx, "top_half", [P, 2, TT, TOPK])
        iu = sb(ctx, "top_half_at", [P, 2, TT, TOPK], U32)
        fi = sb(ctx, "top_half_key", [P, 2, TT, TOPK])
        cand = sb(ctx, "candidates", [P, TT, K2])
        ts = sb(ctx, "top", [P, TT, TOPK])
        pos = sb(ctx, "top_at", [P, TT, TOPK], U32)
        ab = sb(ctx, "top_ab", [P, 2, TT, TOPK], U32)
        abf = sb(ctx, "top_ab_f", [P, 2, TT, TOPK])
        hot = sb(ctx, "rank_hot", [P, 2, TT, K2])
        score = sb(ctx, "top_all", [P, TT, PH, TOPK])
        sel = sb(ctx, "key_all", [P, 2, TT, PH, TOPK])
        gates = sb(ctx, "gates", [P, TT, PH, TOPK])
        gsum = sb(ctx, "gate_sum", [P, 2, TT, PH])
        s_q = [sem(ctx, f"wq_landed{i}") for i in range(2)]
        s_k = sem(ctx, "keys_landed")
        loop_e = ["q0", "q1", "s0", "s1"]
        loop_a = ["w0", "w1", "q0", "q1", "s0", "s1"]
        pre_e = [f"xT{k}" for k in range(KT)]
        pre_a = [x for k in range(KT) for x in (f"h{k}", f"hi{k}")]
        pre_v = ["scale_p", "scale2"] + [f"xn{t}" for t in range(TT)] + [f"lo{k}" for k in range(KT)]
        R4 = range(TT)
        loop_v = [f"{x}{p}{t}" for p in range(2) for x in ("max", "at", "rest", "max2_", "at2_") for t in R4]
        loop_v += ["key"] + [f"{x}{t}" for x in ("cand", "cmax", "cat", "crest", "cmax2_", "cat2_") for t in R4]
        loop_v += ["score", "shift", "mask", "ab_f", "hot0", "hot1", "sel0", "sel1"]
        loop_p = ["w0", "w1", "pick0", "pick1"]
        se, sa, sv, spl = (sem(ctx, f"rt_{n}") for n in ("tensor", "scalar", "vector", "pool"))
        E0, A0, V0 = Steps(se, pre_e), Steps(sa, pre_a), Steps(sv, pre_v)
        E, A = Steps(se, loop_e, len(pre_e)), Steps(sa, loop_a, len(pre_a))
        V, Q = Steps(sv, loop_v, len(pre_v) + len(loop_v)), Steps(spl, loop_p, len(loop_p))
        post_v = ["gsub", "gsum", "grec", "gates", "idx0", "idx1", "gT"]
        V2 = Steps(sv, post_v, len(pre_v) + (1 + PH) * len(loop_v))
        A2 = Steps(sa, ["gexp"], len(pre_a) + PH * len(loop_a))
        E2 = Steps(se, ["idx0", "idx1", "gate"], len(pre_e) + PH * len(loop_e))
        held = sem(ctx, "rt_held")

        with nc.Block() as block:
            @block.sync
            def _(sp):
                sp.dma_start(keys[:], a["sub_keys"]).then_inc(s_k, 16)
                for p in range(2):
                    sp.dma_start(wq[:, p], a["w_q"][p]).then_inc(s_q[p], 16)
                with sp.Fori(1, PH) as h:
                    for p in range(2):
                        sp.wait_ge(*Q.after(f"w{p}", h, 1))
                        sp.dma_start(wq[:, p], a["w_q"][h * 2 + p]).then_inc(s_q[p], 16)

            @block.tensor
            def _(pe):
                for k in range(KT):
                    if k == 0:
                        pe.wait_ge(*V0.after(f"xn{TT - 1}"))
                    if k >= 2:
                        pe.wait_ge(*A0.after(f"h{k - 2}"))
                    for t in R4:
                        last = nc.tensor.transpose(bank[4 + k % 2][:, t * P:(t + 1) * P], xn[:, t, k * P:(k + 1) * P], C["ident"])
                    last.then_inc(*E0.step(f"xT{k}"))
                pe.wait_ge(*V0.after(f"lo{KT - 1}"))
                pe.wait_ge(s_k, 16)
                with pe.Fori(0, PH) as h:
                    for p in range(2):
                        pe.wait_ge(*Q.after(f"w{p}", h))
                        pe.wait_ge(*A.after(f"s{p}", h, 1))
                        for k in range(KT):
                            for w, x in ((wq_hi, h_hi), (wq_hi, h_lo), (wq_lo, h_hi)):
                                last = nc.tensor.matmul(bank[p][:], w[:, p, k, :], x[:, k, :], start=(k == 0 and x is h_hi and w is wq_hi),
                                                        stop=(k == KT - 1 and w is wq_lo))
                        last.then_inc(*E.step(f"q{p}"))
                    for p in range(2):
                        pe.wait_ge(*A.after(f"q{p}", h))
                        for t in R4:
                            last = nc.tensor.matmul(bank[2 + p][:, t * P:(t + 1) * P], qT[:, p, t * P:(t + 1) * P], keys[:, 2 * h + p, :], start=True, stop=True)
                        last.then_inc(*E.step(f"s{p}"))
                for n in range(3):
                    pe.wait_ge(*V2.after("gates"))
                    for t in R4:
                        src = (sel[:, n, t] if n < 2 else gates[:, t]).rearrange("p h k -> p (h k)")
                        last = nc.tensor.transpose(bank[4 + n][:, t * P:(t + 1) * P], src, C["ident"])
                    last.then_inc(*E2.step(("idx0", "idx1", "gate")[n]))

            @block.scalar
            def _(act):
                act.wait_ge(*V0.after("scale2"))
                for k in range(KT):
                    act.wait_ge(*E0.after(f"xT{k}"))
                    if k >= 2:
                        act.wait_ge(*V0.after(f"lo{k - 2}"))
                    nc.scalar.activation(h_raw[:, k % 2], bank[4 + k % 2][:], ACT.Identity, bias=mod[:, SH2 + k:SH2 + k + 1],
                                         scale=scale2[:, k:k + 1]).then_inc(*A0.step(f"h{k}"))
                    act.wait_ge(*A0.after(f"h{k}"))
                    nc.scalar.activation(h_hi[:, k, :], h_raw[:, k % 2], ACT.Copy).then_inc(*A0.step(f"hi{k}"))
                with act.Fori(0, PH) as h:
                    for p in range(2):
                        act.wait_ge(s_q[p], h * 16 + 16)
                        act.wait_ge(*E.after(f"q{p}", h, 1))
                        nc.scalar.activation(wq_hi[:, p], wq[:, p], ACT.Copy).then_inc(*A.step(f"w{p}"))
                    for p in range(2):
                        act.wait_ge(*E.after(f"q{p}", h))
                        nc.scalar.activation(qT[:, p, :], bank[p][:], ACT.Copy).then_inc(*A.step(f"q{p}"))
                    for p in range(2):
                        act.wait_ge(*V.after(f"at2_{p}{TT - 1}", h, 1))
                        act.wait_ge(*E.after(f"s{p}", h))
                        nc.scalar.activation(s[:, p].rearrange("p t n -> p (t n)"), bank[2 + p][:], ACT.Copy).then_inc(*A.step(f"s{p}"))
                act.wait_ge(*V2.after("gsub"))
                nc.scalar.activation(gates[:], gates[:], ACT.Exp).then_inc(*A2.step("gexp"))

            @block.gpsimd
            def _(pool):
                pool.sem_inc(spl, len(loop_p))
                with pool.Fori(0, PH) as h:
                    for p in range(2):
                        pool.wait_ge(*A.after(f"w{p}", h))
                        nc.gpsimd.tensor_tensor(wq_lo[:, p], wq[:, p], wq_hi[:, p].bitcast(F32), ALU.subtract).then_inc(*Q.step(f"w{p}"))
                    for n in range(2):
                        pool.wait_ge(*V.after(f"hot{n}", h))
                        nc.gpsimd.tensor_tensor(hot[:, n].rearrange("p t (k r) -> p t k r", r=TOPK), hot[:, n].rearrange("p t (k r) -> p t k r", r=TOPK),
                                                fi[:, n].unsqueeze(2).to_broadcast([P, TT, TOPK, TOPK]), ALU.mult).then_inc(*Q.step(f"pick{n}"))

            @block.vector
            def _(dve):
                nc.vector.tensor_scalar(scale2[:], mod[:, SC2:SC2 + KT], 1.0, None, ALU.add).then_inc(*V0.step("scale_p"))
                dve.wait_ge(*V0.after("scale_p"))
                nc.vector.tensor_tensor(scale2[:], scale2[:], norms[:, 2, :], ALU.mult).then_inc(*V0.step("scale2"))
                for t in R4:
                    nc.vector.tensor_scalar(xn[:, t, :], x_tok[:, t, :], stat[:, 2, t:t + 1], None, ALU.mult).then_inc(*V0.step(f"xn{t}"))
                for k in range(KT):
                    dve.wait_ge(*A0.after(f"hi{k}"))
                    nc.vector.tensor_tensor(h_lo[:, k, :], h_raw[:, k % 2], h_hi[:, k, :].bitcast(F32), ALU.subtract).then_inc(*V0.step(f"lo{k}"))
                dve.wait_ge(*V0.after(f"lo{KT - 1}"))
                dve.sem_inc(sv, len(loop_v))
                with dve.Fori(0, PH) as h:
                    VA = lambda n: V.after(n, h)

                    def ready(*w):
                        for x in w:
                            dve.wait_ge(*x)
                        dve.sem_inc(held, 1)

                    for p in range(2):
                        ready(A.after(f"s{p}", h))
                        for t in R4:
                            nc.vector.max(v[:, p, t, 0:8], s[:, p, t]).then_inc(*V.step(f"max{p}{t}"))
                        ready(VA(f"max{p}{TT - 1}"))
                        for t in R4:
                            nc.vector.max_index(iu[:, p, t, 0:8], v[:, p, t, 0:8], s[:, p, t]).then_inc(*V.step(f"at{p}{t}"))
                        for t in R4:
                            nc.vector.match_replace(s[:, p, t], v[:, p, t, 0:8], s[:, p, t], -3e38).then_inc(*V.step(f"rest{p}{t}"))
                        ready(VA(f"rest{p}{TT - 1}"))
                        for t in R4:
                            nc.vector.max(v[:, p, t, 8:16], s[:, p, t]).then_inc(*V.step(f"max2_{p}{t}"))
                        ready(VA(f"max2_{p}{TT - 1}"))
                        for t in R4:
                            nc.vector.max_index(iu[:, p, t, 8:16], v[:, p, t, 8:16], s[:, p, t]).then_inc(*V.step(f"at2_{p}{t}"))
                    dve.wait_ge(*VA(f"at2_1{TT - 1}"))
                    nc.vector.tensor_copy(fi[:], iu[:]).then_inc(*V.step("key"))
                    for t in R4:
                        nc.vector.tensor_tensor(cand[:, t].rearrange("p (x y) -> p x y", x=TOPK), v[:, 0, t].unsqueeze(2).to_broadcast([P, TOPK, TOPK]),
                                                v[:, 1, t].unsqueeze(1).to_broadcast([P, TOPK, TOPK]), ALU.add).then_inc(*V.step(f"cand{t}"))
                    ready(VA(f"cand{TT - 1}"))
                    for t in R4:
                        nc.vector.max(ts[:, t, 0:8], cand[:, t]).then_inc(*V.step(f"cmax{t}"))
                    ready(VA(f"cmax{TT - 1}"))
                    for t in R4:
                        nc.vector.max_index(pos[:, t, 0:8], ts[:, t, 0:8], cand[:, t]).then_inc(*V.step(f"cat{t}"))
                    for t in R4:
                        nc.vector.match_replace(cand[:, t], ts[:, t, 0:8], cand[:, t], -3e38).then_inc(*V.step(f"crest{t}"))
                    ready(VA(f"crest{TT - 1}"))
                    for t in R4:
                        nc.vector.max(ts[:, t, 8:16], cand[:, t]).then_inc(*V.step(f"cmax2_{t}"))
                    ready(VA(f"cmax2_{TT - 1}"))
                    for t in R4:
                        nc.vector.max_index(pos[:, t, 8:16], ts[:, t, 8:16], cand[:, t]).then_inc(*V.step(f"cat2_{t}"))
                    nc.vector.tensor_copy(score[:, :, h, :], ts[:]).then_inc(*V.step("score"))
                    dve.wait_ge(*VA(f"cat2_{TT - 1}"))
                    nc.vector.tensor_scalar(ab[:, 0], pos[:], 4, None, ALU.logical_shift_right).then_inc(*V.step("shift"))
                    nc.vector.tensor_scalar(ab[:, 1], pos[:], TOPK - 1, None, ALU.bitwise_and).then_inc(*V.step("mask"))
                    dve.wait_ge(*VA("mask"))
                    nc.vector.tensor_copy(abf[:], ab[:]).then_inc(*V.step("ab_f"))
                    dve.wait_ge(*VA("ab_f"))
                    for n in range(2):
                        nc.vector.tensor_tensor(hot[:, n].rearrange("p t (k r) -> p (t k) r", r=TOPK),
                                                abf[:, n].rearrange("p t k -> p (t k)").unsqueeze(2).to_broadcast([P, TT * TOPK, TOPK]),
                                                C["iota"][:, 0:TOPK].unsqueeze(1).to_broadcast([P, TT * TOPK, TOPK]), ALU.is_equal).then_inc(*V.step(f"hot{n}"))
                    for n in range(2):
                        dve.wait_ge(*Q.after(f"pick{n}", h))
                        nc.vector.tensor_reduce(sel[:, n, :, h, :], hot[:, n].rearrange("p t (k r) -> p t k r", r=TOPK), AX.X, ALU.add).then_inc(*V.step(f"sel{n}"))
                dve.wait_ge(*V.after("sel1", PH - 1))
                th = lambda x: x.rearrange("p t h k -> p (t h) k")
                nc.vector.tensor_tensor(th(gates[:]), th(score[:]), th(score[:])[:, :, 0:1].to_broadcast([P, TT * PH, TOPK]), ALU.subtract).then_inc(*V2.step("gsub"))
                dve.wait_ge(*A2.after("gexp"))
                nc.vector.tensor_reduce(gsum[:, 0].rearrange("p t h -> p (t h)"), th(gates[:]), AX.X, ALU.add).then_inc(*V2.step("gsum"))
                dve.wait_ge(*V2.after("gsum"))
                nc.vector.reciprocal(gsum[:, 1], gsum[:, 0]).then_inc(*V2.step("grec"))
                dve.wait_ge(*V2.after("grec"))
                nc.vector.tensor_tensor(th(gates[:]), th(gates[:]), gsum[:, 1].rearrange("p t h -> p (t h)").unsqueeze(2).to_broadcast([P, TT * PH, TOPK]),
                                        ALU.mult).then_inc(*V2.step("gates"))
                for n in range(2):
                    dve.wait_ge(*E2.after(f"idx{n}"))
                    nc.vector.tensor_copy(idxT[:, n, :], bank[4 + n][:]).then_inc(*V2.step(f"idx{n}"))
                dve.wait_ge(*E2.after("gate"))
                nc.vector.tensor_copy(gateT[:], bank[6][:]).then_inc(*V2.step("gT"))


def scatter_stage(nc, a, env, spill):
    g_ = env
    bank, C, idxT, gateT = g_["bank"], g_["C"], g_["idxT"], g_["gateT"]
    sb, sem = g_["sb"], g_["sem"]
    UT = 8
    UB, SLOTS = TB // UT, 2
    NU = UB * SLOTS
    with ExitStack() as ctx:
        hot1 = sb(ctx, "hot_i1", [P, 2, UT, P])
        hot2 = sb(ctx, "gated_i2", [P, 2, UT, P])
        block_g = sb(ctx, "gate_block", [P, SLOTS, P, TB])
        units = [f"unit{u}" for u in range(NU)]
        sv, se, sa = (sem(ctx, n) for n in ("hot_ready", "dense", "copied"))
        stored = [sem(ctx, f"stored{i}") for i in range(SLOTS)]
        V, E, A = Steps(sv, units), Steps(se, units, NU), Steps(sa, units, NU)

        with nc.Block() as block:
            @block.vector
            def _(dve):
                with dve.Fori(0, T // (NU * UT)) as i:
                    for u in range(NU):
                        dve.wait_ge(*(E.after(f"unit{u - 2}", i) if u >= 2 else E.after(f"unit{NU + u - 2}", i, 1)))
                        nc.vector.tensor_tensor(hot1[:, u % 2], C["iota"].unsqueeze(1).to_broadcast([P, UT, P]),
                                                idxT[:, 0, bass.ds(i * (NU * UT) + u * UT, UT)].unsqueeze(2).to_broadcast([P, UT, P]), ALU.is_equal)
                        for t in range(UT):
                            at = bass.ds(i * (NU * UT) + (u * UT + t), 1)
                            last = nc.vector.tensor_scalar(hot2[:, u % 2, t, :], C["iota"], idxT[:, 1, at], gateT[:, at], ALU.is_equal, ALU.mult)
                        last.then_inc(*V.step(f"unit{u}"))

            @block.gpsimd
            def _(pool):
                pool.sem_inc(se, NU)
                pool.sem_inc(sa, NU)
                for s in stored:
                    pool.sem_inc(s, 16)

            @block.tensor
            def _(pe):
                with pe.Fori(0, T // (NU * UT)) as i:
                    for u in range(NU):
                        pe.wait_ge(*(A.after(f"unit{u - 2}", i) if u >= 2 else A.after(f"unit{NU + u - 2}", i, 1)))
                        pe.wait_ge(*V.after(f"unit{u}", i))
                        for t in range(UT):
                            last = nc.tensor.matmul(bank[2 * (u % 2) + t // 4][:, t % 4 * P:(t % 4 + 1) * P], hot1[:, u % 2, t, :], hot2[:, u % 2, t, :],
                                                    start=True, stop=True)
                        last.then_inc(*E.step(f"unit{u}"))

            @block.scalar
            def _(act):
                with act.Fori(0, T // (NU * UT)) as i:
                    for u in range(NU):
                        slot = u // UB
                        if u % UB == 0:
                            act.wait_ge(stored[slot], i * 16 + 16)
                        act.wait_ge(*E.after(f"unit{u}", i))
                        for b in range(2):
                            t = u % UB * UT + 4 * b
                            last = nc.scalar.activation(block_g[:, slot, :, t:t + 4], bank[2 * (u % 2) + b][:].rearrange("p (t n) -> p n t", t=4), ACT.Copy)
                        last.then_inc(*A.step(f"unit{u}"))

            @block.sync
            def _(sp):
                with sp.Fori(0, T // (NU * UT)) as i:
                    for slot in range(SLOTS):
                        sp.wait_ge(*A.after(f"unit{slot * UB + UB - 1}", i))
                        sp.dma_start(spill[:, bass.ds(i * SLOTS + slot, 1)], block_g[:, slot:slot + 1]).then_inc(stored[slot], 16)
                for s in stored:
                    sp.wait_ge(s, 16 * (T // (NU * UT) + 1))


def expert_stage(nc, a, env, spill, out):
    g_ = env
    bank, eps, x_tok, h_hi, h_lo, row_ffn = (g_[n] for n in ("bank", "eps", "x_tok", "h_hi", "h_lo", "row_ffn"))
    sb, sem = g_["sb"], g_["sem"]
    GE = 4
    NGRP = EXP_TILES // GE
    with ExitStack() as ctx:
        ut = sb(ctx, "u_tile", [P, 2, KT, P])
        u_hi = sb(ctx, "u_hi", [P, 2, KT, P], F32R)
        u_lo = sb(ctx, "u_lo", [P, 2, KT, P], F32R)
        vt = sb(ctx, "v_tile", [P, 2, D])
        v_hi = sb(ctx, "v_hi", [P, GE, D], F32R)
        v_lo = sb(ctx, "v_lo", [P, GE, D], F32R)
        gt = sb(ctx, "gate_tiles", [P, T // TB, GE, TB])
        gel = sb(ctx, "gelu", [P, 2, T])
        coef = sb(ctx, "coef", [P, 2, T])
        c_hi = sb(ctx, "coef_hi", [P, GE, T], F32R)
        c_lo = sb(ctx, "coef_lo", [P, GE, T], F32R)
        y = sb(ctx, "y", [P, TT, D])
        ss = sb(ctx, "y_sq", [P, 4, TT])
        s_u = [sem(ctx, f"u_landed{i}") for i in range(2)]
        s_v = [sem(ctx, f"v_landed{i}") for i in range(2)]
        s_g = sem(ctx, "gates_landed")
        zeroed, stored = sem(ctx, "y_zeroed"), sem(ctx, "out_stored")
        loop_e = [f"u{e}" for e in range(GE)] + [f"y{half}{t}" for half in range(2) for t in range(TT)]
        order = ["v0", "v1", "u2", "c0", "v2", "u3", "c1", "v3", "c2", "c3", "u0", "u1"]
        loop_a = [x for n in order for x in ([f"gelu{n[1]}", f"hi_c{n[1]}"] if n[0] == "c" else [f"hi_{n}"])]
        loop_v = [x for n in order for x in ([f"coef{n[1]}", f"lo_c{n[1]}"] if n[0] == "c" else [f"lo_{n}"])]
        adds = [f"add{half}{t}" for half in range(2) for t in range(TT)]
        loop_v += adds
        se, sa, sv = (sem(ctx, f"ex_{n}") for n in ("tensor", "scalar", "vector"))
        E, A, V = Steps(se, loop_e, len(loop_e)), Steps(sa, loop_a, len(loop_a)), Steps(sv, loop_v, len(loop_v))
        A2 = Steps(sa, [f"sq{t}" for t in range(TT)] + ["std"], (1 + NGRP) * len(loop_a))
        V2 = Steps(sv, ["rstd"] + [f"{x}{t}" for t in range(TT) for x in ("scaled", "out")], (1 + NGRP) * len(loop_v))
        a_banks, y_banks = (2, 3, 4, 5), ((2, 3, 4, 5), (6, 7, 0, 1))

        with nc.Block() as block:
            def u_split(S, part, e, i):
                return S.after(f"{part}_u{e}", i, 1 if e < 2 else 0)

            @block.sync
            def _(sp):
                for n in range(2):
                    sp.dma_start(ut[:, n], a["peer_u"][n]).then_inc(s_u[n], 16)

                with sp.Fori(0, NGRP) as i:
                    sp.wait_ge(*V.after(f"coef{GE - 1}", i, 1))
                    sp.dma_start(gt[:], spill[:, :, bass.ds(i * GE, GE), :]).then_inc(s_g, 16)
                    for e in range(GE):
                        sp.wait_ge(*(V.after(f"lo_v{e - 2}", i) if e >= 2 else V.after(f"lo_v{e + 2}", i, 1)))
                        sp.dma_start(vt[:, e % 2], a["peer_v"][i * GE + e]).then_inc(s_v[e % 2], 16)
                        sp.wait_ge(*u_split(V, "lo", e, i))
                        sp.dma_start(ut[:, e % 2], a["peer_u"][(i * GE + (e + 2)) % EXP_TILES]).then_inc(s_u[e % 2], 16)

            @block.tensor
            def _(pe):
                with pe.Fori(0, NGRP) as i:
                    for e in range(GE):
                        pe.wait_ge(*u_split(V, "lo", e, i))
                        pe.wait_ge(*V.after(f"add0{e}", i, 1))
                        for k in range(KT):
                            for n, (w, x) in enumerate(((u_hi, h_hi), (u_hi, h_lo), (u_lo, h_hi))):
                                last = nc.tensor.matmul(bank[a_banks[e]][:], w[:, e % 2, k, :], x[:, k, :], start=(k == 0 and n == 0), stop=(k == KT - 1 and n == 2))
                        last.then_inc(*E.step(f"u{e}"))
                    for half in range(2):
                        c = slice(half * 512, half * 512 + 512)
                        for e in range(GE):
                            if half == 0:
                                pe.wait_ge(*V.after(f"lo_v{e}", i))
                                pe.wait_ge(*V.after(f"lo_c{e}", i))
                            for t in range(TT):
                                if e == 0:
                                    pe.wait_ge(*(A.after(f"gelu{t}", i) if half == 0 else V.after(f"add1{t}", i, 1)))
                                for n, (w, x) in enumerate(((c_hi, v_hi), (c_hi, v_lo), (c_lo, v_hi))):
                                    last = nc.tensor.matmul(bank[y_banks[half][t]][:], w[:, e, t * P:(t + 1) * P], x[:, e, c],
                                                            start=(e == 0 and n == 0), stop=(e == GE - 1 and n == 2))
                                if e == GE - 1:
                                    last.then_inc(*E.step(f"y{half}{t}"))

            @block.gpsimd
            def _(pool):
                pool.sem_inc(se, len(loop_e))
                nc.gpsimd.memset(y[:], 0.0).then_inc(zeroed, 1)

            @block.scalar
            def _(act):
                act.sem_inc(sa, len(loop_a) - 2)
                A.n = len(loop_a) - 2
                for e in range(2):
                    act.wait_ge(s_u[e], 16)
                    nc.scalar.activation(u_hi[:, e], ut[:, e], ACT.Copy).then_inc(*A.step(f"hi_u{e}"))
                with act.Fori(0, NGRP) as i:
                    for n in order:
                        e = int(n[1])
                        if n[0] == "v":
                            act.wait_ge(s_v[e % 2], i * 32 + 16 * (e // 2 + 1))
                            act.wait_ge(*E.after(f"y1{TT - 1}", i, 1))
                            nc.scalar.activation(v_hi[:, e], vt[:, e % 2], ACT.Copy).then_inc(*A.step(f"hi_v{e}"))
                        elif n[0] == "u":
                            act.wait_ge(s_u[e % 2], i * 32 + (32 if e >= 2 else 48))
                            act.wait_ge(*E.after(f"u{e ^ 2}", i))
                            nc.scalar.activation(u_hi[:, e % 2], ut[:, e % 2], ACT.Copy).then_inc(*A.step(f"hi_u{e}"))
                        else:
                            act.wait_ge(*(V.after(f"coef{e - 2}", i) if e >= 2 else V.after(f"coef{e + 2}", i, 1)))
                            act.wait_ge(*E.after(f"u{e}", i))
                            nc.scalar.activation(gel[:, e % 2, :], bank[a_banks[e]][:], ACT.Gelu).then_inc(*A.step(f"gelu{e}"))
                            act.wait_ge(*V.after(f"coef{e}", i))
                            nc.scalar.activation(c_hi[:, e], coef[:, e % 2], ACT.Copy).then_inc(*A.step(f"hi_c{e}"))
                act.wait_ge(*V.after(adds[-1], NGRP - 1))
                for t in range(TT):
                    nc.scalar.activation(vt[:, t % 2], y[:, t, :], ACT.Square, accum_out=ss[:, 0, t:t + 1]).then_inc(*A2.step(f"sq{t}"))
                    act.wait_ge(*A2.after(f"sq{t}"))
                nc.scalar.activation(ss[:, 1, :], ss[:, 0, :], ACT.Sqrt, bias=eps[:], scale=1.0 / D).then_inc(*A2.step("std"))
                for t in range(TT):
                    act.wait_ge(*V2.after(f"out{t}"))
                    act.dma_start(out[t * P:(t + 1) * P, :], y[:, t, :]).then_inc(stored, 16)
                act.wait_ge(stored, 16 * TT)

            @block.vector
            def _(dve):
                def rest(dst, src, hi):
                    return nc.vector.tensor_tensor(dst, src, hi.bitcast(F32), ALU.subtract)

                V.n = loop_v.index("lo_u0")
                dve.sem_inc(sv, V.n)
                for e in range(2):
                    dve.wait_ge(*u_split(A, "hi", e, 0))
                    rest(u_lo[:, e], ut[:, e], u_hi[:, e]).then_inc(*V.step(f"lo_u{e}"))
                dve.wait_ge(*u_split(V, "lo", 1, 0))
                V.n += len(adds)
                dve.sem_inc(sv, len(adds))
                dve.wait_ge(zeroed, 1)
                with dve.Fori(0, NGRP) as i:
                    for n in order:
                        e = int(n[1])
                        if n[0] == "v":
                            dve.wait_ge(*A.after(f"hi_v{e}", i))
                            rest(v_lo[:, e], vt[:, e % 2], v_hi[:, e]).then_inc(*V.step(f"lo_v{e}"))
                        elif n[0] == "u":
                            dve.wait_ge(*A.after(f"hi_u{e}", i))
                            rest(u_lo[:, e % 2], ut[:, e % 2], u_hi[:, e % 2]).then_inc(*V.step(f"lo_u{e}"))
                        else:
                            if e == 0:
                                dve.wait_ge(s_g, i * 16 + 16)
                            dve.wait_ge(*A.after(f"gelu{e}", i))
                            by_block = lambda x: x.rearrange("p (b t) -> p b t", t=TB)
                            nc.vector.tensor_tensor(by_block(coef[:, e % 2]), by_block(gel[:, e % 2]), gt[:, :, e, :], ALU.mult).then_inc(*V.step(f"coef{e}"))
                            dve.wait_ge(*A.after(f"hi_c{e}", i))
                            rest(c_lo[:, e], coef[:, e % 2], c_hi[:, e]).then_inc(*V.step(f"lo_c{e}"))
                    for half in range(2):
                        for t in range(TT):
                            dve.wait_ge(*E.after(f"y{half}{t}", i))
                            c = slice(half * 512, half * 512 + 512)
                            nc.vector.tensor_tensor(y[:, t, c], y[:, t, c], bank[y_banks[half][t]][:], ALU.add).then_inc(*V.step(f"add{half}{t}"))
                dve.wait_ge(*A2.after("std"))
                nc.vector.reciprocal(ss[:, 2, :], ss[:, 1, :]).then_inc(*V2.step("rstd"))
                dve.wait_ge(*V2.after("rstd"))
                for t in range(TT):
                    nc.vector.scalar_tensor_tensor(y[:, t, :], y[:, t, :], ss[:, 2, t:t + 1], row_ffn[:], ALU.mult, ALU.mult).then_inc(*V2.step(f"scaled{t}"))
                    dve.wait_ge(*V2.after(f"scaled{t}"))
                    nc.vector.tensor_tensor(y[:, t, :], y[:, t, :], x_tok[:, t, :], ALU.add).then_inc(*V2.step(f"out{t}"))


def lay_out(inputs):
    f = {k: np.asarray(v) for k, v in inputs.items()}

    def cols(w, c0, n):
        k = w.shape[0] // P
        return w[:, c0:c0 + n * P].reshape(k, P, n, P).transpose(2, 1, 0, 3)

    w_in = f["w_in_mix"][0]
    sc, qkv, z, ab = 0, 1536, 3072, 3584
    gates = 3600
    b_t, c_t, x_t = (cols(w_in, sc + 512 * n, 4) for n in range(3))
    sc_tiles = np.stack([c_t, x_t, b_t], 1).reshape(12, P, KT, P)
    g_sc, g_dn = cols(w_in, gates, KT), cols(w_in, gates + D, KT)
    merge = np.concatenate([g_sc, g_dn, cols(f["w_sc_out"][0], 0, KT), cols(f["w_dn_out"][0], 0, KT)], axis=2)
    _, wide, narrow = constants()
    r = {
        "x": f["x"][0],
        "c_col": f["c"][0].reshape(KT, P).T,
        "w_ada": f["w_ada"][0].reshape(KT, P, 24, 256).transpose(2, 1, 0, 3),
        "b_ada": f["b_ada"][0].reshape(MOD, P).T,
        "norms": np.stack([f[n][0].reshape(KT, P).T for n in ("norm_pre_mix", "norm_post_mix", "norm_pre_ffn", "norm_post_ffn")], 1),
        "w_proj": np.concatenate([sc_tiles, cols(w_in, qkv, 12), cols(w_in, z, 4)], 0),
        "w_ab": w_in[:, ab:ab + 16].reshape(KT, P, 16).transpose(1, 0, 2),
        "sc_w": f["sc_conv_w"][0].reshape(3, 4, P).transpose(2, 1, 0),
        "dn_w": f["dn_conv_w"][0].reshape(4, 12, P).transpose(2, 1, 0),
        "dt_bias": f["dn_dt_bias"][0][:, None],
        "a_log": f["dn_a_log"][0][:, None],
        "out_norm": np.concatenate([f["dn_out_norm"][0]] * 2)[:, None],
        "w_merge": merge,
        "w_mix": f["w_mix_out"][0].reshape(KT, P, D).transpose(1, 0, 2),
        "w_q": cols(f["peer_w_q"][0], 0, 16),
        "sub_keys": f["peer_sub_keys"][0].reshape(16, P, P).transpose(2, 0, 1),
        "peer_u": f["peer_u"].reshape(P, P, KT, P).transpose(1, 3, 2, 0),
        "peer_v": f["peer_v"].reshape(P, P, D).transpose(1, 0, 2),
        "wide": wide,
        "narrow": narrow,
    }
    return {k: np.ascontiguousarray(v) for k, v in r.items()}


SPILL = (P, T // TB, P, TB)


def kernel(**inputs):
    import concourse.bacc as _bacc
    from concourse.bass_utils import run_bass_kernel_spmd as _run

    nc = _bacc.Bacc("TRN2", target_bir_lowering=False, num_devices=1)
    laid = lay_out(inputs)
    aps = {n: nc.dram_tensor(f"in_{n}_dram", v.shape, mybir.dt.from_np(v.dtype), kind="ExternalInput").ap() for n, v in laid.items()}
    out = nc.dram_tensor("out_dram", (T, D), F32, kind="ExternalOutput").ap()
    spill = nc.dram_tensor("gate_scratch", SPILL, F32, kind="Internal").ap()
    program(nc, aps, out, spill)
    r = _run(nc, [{f"in_{n}_dram": v for n, v in laid.items()}], core_ids=[0])
    return r.results[0]["out_dram"].reshape(1, T, D)
```

```python
from contextlib import ExitStack

import numpy as np

import concourse.bass as bass
from concourse import mybir

F32 = mybir.dt.float32
F32R = mybir.dt.float32r
U32 = mybir.dt.uint32
ALU = mybir.AluOpType
ACT = mybir.ActivationFunctionType
AX = mybir.AxisListType

P = 128
T = 512
D = 1024
TT = T // P
KT = D // P
H, DK = 8, 64
HJ = H // 2
CH = 64
EPS = 1e-6
MOD = 6 * KT
SH1, SC1, GT1, SH2, SC2, GT2 = (KT * n for n in range(6))
N_SC, N_QKV, N_Z = 12, 12, 4
N_PROJ = N_SC + N_QKV + N_Z
NEG = -1e30
PH, TOPK, NKEYS = 8, 16, 128
TB = 32
U_HEAD, U_TAIL, S_TAIL = 4, 4, 4
N_RETR = PH * U_HEAD + U_TAIL
N_EARLY = N_RETR + T // TB + S_TAIL
EXP_TILES = NKEYS


class Steps:

    def __init__(self, sem, names, base=0):
        self.sem, self.base, self.at = sem, base, {n: i + 1 for i, n in enumerate(names)}
        assert len(self.at) == len(names)
        self.names, self.n = names, 0

    def after(self, name, it=0, back=0):
        value = self.base + self.at[name] - back * len(self.names)
        assert value > 0 or (back and not isinstance(it, int)), (name, value)
        return self.sem, it * len(self.names) + value

    def step(self, name):
        assert self.names[self.n % len(self.names)] == name, (name, self.names[self.n % len(self.names)])
        self.n += 1
        return self.sem, 1


def constants():
    i, j = np.arange(P)[:, None], np.arange(P)[None, :]
    chunk = i // CH == j // CH
    near = i // 16 == j // 16
    parts = {
        "ident": i == j,
        "headsum": i // DK == j // DK,
        "ones": np.ones((P, P)),
        "neg_near": -1.0 * (near & (j < i)),
        "neg_nearT": -1.0 * (near & (i < j)),
        "neg_farT": -1.0 * (chunk & ~near & (i < j)),
        "causal": np.where(chunk & (j <= i), 0.0, NEG),
        "causalT": np.where(chunk & (i <= j), 0.0, NEG),
        "iota": np.broadcast_to(j, (P, P)),
    }
    wide = np.concatenate([v.astype(np.float32) for v in parts.values()], axis=1)
    h = np.arange(H)[:, None]
    m = np.arange(P)[None, :]
    sel_head = np.stack([np.broadcast_to(h == n, (H, P)) for n in range(H)], 1)
    sel_pair = np.stack([h == 2 * n + m // DK for n in range(HJ)], 1)
    carry = np.broadcast_to(np.arange(T)[None, :] % CH != 0, (H, T))
    small = np.concatenate([a.reshape(H, -1).astype(np.float32) for a in (sel_head, sel_pair, carry)], 1)
    return list(parts), np.ascontiguousarray(wide), np.ascontiguousarray(small)


def program(nc, a, out, spill, acts):
    const_names = constants()[0]

    with ExitStack() as top:
        def sb(ctx, name, shape, dt=F32):
            return ctx.enter_context(nc.sbuf_tensor(name, shape, dt))

        def sem(ctx, name):
            return ctx.enter_context(nc.semaphore(name))

        bank = [top.enter_context(nc.psum_tensor(f"bank{i}", [P, 512], F32)) for i in range(8)]
        cst = sb(top, "cst", [P, len(const_names), P])
        C = {n: cst[:, i, :] for i, n in enumerate(const_names)}
        eps = sb(top, "eps", [P, 1])
        mod = sb(top, "mod", [P, MOD])
        norms = sb(top, "norms", [P, 4, KT])
        x_tok = sb(top, "x_tok", [P, TT, D])
        stat = sb(top, "stat", [P, 4, TT])

        row_ffn = sb(top, "row_ffn", [P, D])
        h_hi = sb(top, "h_hi", [P, KT, T], F32R)
        h_lo = sb(top, "h_lo", [P, KT, T], F32R)
        env = dict(locals())
        with ExitStack() as mix:
            env["zT"] = sb(mix, "zT", [P, HJ, T])
            env["scT"] = sb(mix, "scT", [P, HJ, T])
            with ExitStack() as delta:
                env["qkvT"] = sb(delta, "qkvT", [P, 12, T])
                env["small"] = small = sb(delta, "small", [H, 12 * P + T])
                env["sel_head"] = small[:, 0:8 * P].rearrange("h (n m) -> h n m", n=H)
                env["sel_pair"] = small[:, 8 * P:12 * P].rearrange("h (n m) -> h n m", n=HJ)
                env["carry"] = small[:, 12 * P:12 * P + T]
                env["abT"] = sb(delta, "abT", [H, 2, T])
                env["dt_bias"] = sb(delta, "dt_bias", [H, 1])
                env["a_log"] = sb(delta, "a_log", [H, 1])
                env["out_norm"] = sb(delta, "out_norm", [P, 1])
                project_stage(nc, a, env)
                delta_stage(nc, a, env)
            merge_stage(nc, a, env)
        with ExitStack() as pick:
            env["idxT"] = sb(pick, "idxT", [P, 2, T])
            env["gateT"] = sb(pick, "gateT", [P, T])
            retrieve_stage(nc, a, env, acts)
            scatter_stage(nc, a, env, spill, acts)
        expert_stage(nc, a, env, spill, acts, out)


def project_stage(nc, a, env):
    g = env
    bank, C, mod, norms, stat, eps = g["bank"], g["C"], g["mod"], g["norms"], g["stat"], g["eps"]
    x_tok, h_hi, h_lo, qkvT, zT, scT, abT = (g[n] for n in ("x_tok", "h_hi", "h_lo", "qkvT", "zT", "scT", "abT"))
    sb, sem = g["sb"], g["sem"]
    AR = 4
    NA, NA1 = MOD, SC1 + KT
    WR = 4
    NI = N_PROJ // WR
    RQ, RZ = N_SC // WR, NI - 1
    LAG = 2
    with ExitStack() as ctx:
        ada = sb(ctx, "ada", [P, AR, D])
        wring = sb(ctx, "wring", [P, WR, KT, P])
        w_hi = sb(ctx, "wring_hi", [P, 2, KT, P], F32R)
        w_lo = sb(ctx, "wring_lo", [P, 2, KT, P], F32R)
        w_ab = sb(ctx, "w_ab", [P, KT, 2 * H])
        raw = sb(ctx, "raw", [P, WR, 3 + T])
        h_raw = raw[:, 2:4, 3:3 + T]
        xn = sb(ctx, "xn", [P, TT * D])
        conv = xn[:, 0:3 * T].rearrange("p (n t) -> p n t", n=3)
        acc = xn[:, 3 * T:5 * T].rearrange("p (n t) -> p n t", n=2)
        upad = xn[:, 5 * T:6 * T + 2]
        sq = sb(ctx, "square", [P, 2, T])
        nrm = sb(ctx, "norm", [P, 2, T])
        c_row = sb(ctx, "c_row", [P, D])
        b_ada = sb(ctx, "b_ada", [P, MOD])
        scale1 = sb(ctx, "scale1", [P, KT])
        sc_w = sb(ctx, "sc_w", [P, HJ, 3])
        dn_w = sb(ctx, "dn_w", [P, 12, 4])

        s_c, s_const, s_x, s_small, s_wab = (sem(ctx, n) for n in ("c_landed", "const_landed", "x_landed", "small_landed", "wab_landed"))
        s_ada = [sem(ctx, f"ada_landed{i}") for i in range(AR)]
        s_w = [sem(ctx, f"w_landed{i}") for i in range(WR)]
        (ada_used, hi_ready, lo_ready, tile_done, raw_ready, raw_used, conv_done, silu_done, sq_done, ss_done, norm_done, inv_done,
         unit_done, conv_chain, last_v) = (sem(ctx, n) for n in (
             "ada_used", "w_hi_ready", "w_lo_ready", "tile_done", "raw_ready", "raw_used", "conv_done", "silu_done", "square_done",
             "square_sum_done", "norm_done", "norm_inverted", "unit_done", "conv_chain", "p_last"))
        V = Steps(sem(ctx, "p_vector"), ["pads", "eps"]
                  + ["rstd"] + [f"xn{t}" for t in range(TT)] + ["mod1", "scale_p", "scale1"] + [f"lo{k}" for k in range(KT)] + ["pads_u"])
        A = Steps(sem(ctx, "p_scalar"), ["c_silu"] + [f"sq{t}" for t in range(TT)] + ["std"] + [x for k in range(KT) for x in (f"h{k}", f"hi{k}")])
        E = Steps(sem(ctx, "p_tensor"), [f"xT{k}" for k in range(KT)])

        xT_ps = bank
        proj_ps, ss_ps, ab_ps = bank[0:4], bank[4:6], bank[6:8]

        with nc.Block() as block:
            @block.sync
            def _(sp):
                sp.dma_start(c_row[:], a["c_row"]).then_inc(s_c, 16)
                for t in range(TT):
                    sp.dma_start(x_tok[:, t, :], a["x"][t * P:(t + 1) * P, :]).then_inc(s_x, 16)
                sp.dma_start(g["cst"][:], a["wide"]).then_inc(s_const, 16)
                for dst, name in ((b_ada[:], "b_ada"), (norms[:], "norms"), (g["small"][:], "narrow"), (sc_w[:], "sc_w"),
                                  (dn_w[:], "dn_w"), (g["dt_bias"][:], "dt_bias"), (g["a_log"][:], "a_log"),
                                  (g["out_norm"][:], "out_norm")):
                    sp.dma_start(dst, a[name]).then_inc(s_small, 16)
                for n in range(NA1 + AR):
                    if n >= AR:
                        sp.wait_ge(ada_used, n - AR + 1)
                    sp.dma_start(ada[:, n % AR], a["w_ada"][n]).then_inc(s_ada[n % AR], 16)
                    if n in (NA1 - AR, NA1 - 1):
                        for m in range(2):
                            b = m if n < NA1 - 1 else 2 + m
                            sp.dma_start(wring[:, b], a["w_proj"][b]).then_inc(s_w[b], 16)
                sp.dma_start(w_ab[:], a["w_ab"]).then_inc(s_wab, 16)

                def round_loads(i, pieces):
                    for b in range(WR):
                        sp.wait_ge(lo_ready, i * WR + (b + 1 - WR))
                        sp.dma_start(wring[:, b], a["w_proj"][i * WR + b]).then_inc(s_w[b], 16)
                        for m in range(min(2, pieces - 2 * b)):
                            n = (2 * b + m) % AR
                            sp.wait_ge(ada_used, i * 8 + (NA1 - AR + 2 * b + m - AR + 1))
                            sp.dma_start(ada[:, n], a["w_ada"][i * 8 + (NA1 - AR + 2 * b + m)]).then_inc(s_ada[n], 16)

                with sp.Fori(1, 4) as i:
                    round_loads(i, 8)
                round_loads(4, 4)
                with sp.Fori(5, NI) as i:
                    round_loads(i, 0)

            def project(out, w, ready=None):
                for k in range(KT):
                    if ready:
                        ready(k)
                    for n, (ww, x) in enumerate(((w_hi, h_hi), (w_hi, h_lo), (w_lo, h_hi))):
                        last = nc.tensor.matmul(out, w(ww, k), x[:, k, :], start=(k == 0 and n == 0), stop=(k == KT - 1 and n == 2))
                return last

            @block.tensor
            def _(pe):
                pe.wait_ge(s_const, 16)
                pe.wait_ge(*V.after(f"xn{TT - 1}"))
                for k in range(KT):
                    for t in range(TT):
                        last = nc.tensor.transpose(xT_ps[k][:, t * P:(t + 1) * P], xn[:, t * D + k * P:t * D + (k + 1) * P], C["ident"])
                    last.then_inc(*E.step(f"xT{k}"))

                def tile(i, b):
                    pe.wait_ge(lo_ready, i * WR + (b + 1))
                    pe.wait_ge(raw_ready, i * WR + (b + 1))
                    project(proj_ps[b][:], lambda w, k: w[:, b % 2, k, :], h_part if isinstance(i, int) and i + b == 0 else None).then_inc(tile_done, 1)

                h_part = lambda k: pe.wait_ge(*V.after(f"lo{k}"))
                for b in range(WR):
                    tile(0, b)
                with pe.Fori(1, 4) as i:
                    for b in range(WR):
                        tile(i, b)
                with pe.Fori(4, RZ) as i:
                    for b in range(WR):
                        tile(i, b)
                        pe.wait_ge(sq_done, i * WR + (b + 1 - 4 * WR))
                        pe.wait_ge(norm_done, i * WR + (b + 1 - 4 * WR))
                        nc.tensor.matmul(ss_ps[b % 2][:], C["headsum"], sq[:, b % 2, :], start=True, stop=True).then_inc(ss_done, 1)
                for b in range(WR):
                    tile(RZ, b)
                pe.wait_ge(norm_done, LAG + 8)
                pe.wait_ge(lo_ready, N_PROJ + 1)
                for n in range(2):
                    ab = lambda w, k: w[:, 0].rearrange("p k m -> p (k m)")[:, 2 * H * k + n * H:2 * H * k + n * H + H]
                    project(ab_ps[n][0:H, :], ab).then_inc(tile_done, 1)

            @block.gpsimd
            def _(pool):
                pool.sem_inc(raw_ready, WR)
                for s in (silu_done, unit_done, ss_done, norm_done):
                    pool.sem_inc(s, LAG)

                def rest(b, slot, count):
                    pool.wait_ge(hi_ready, count)
                    nc.gpsimd.tensor_tensor(w_lo[:, slot], wring[:, b], w_hi[:, slot].bitcast(F32), ALU.subtract).then_inc(lo_ready, 1)

                def squares(i, b):
                    pool.wait_ge(silu_done, i * WR + (b + 1 + LAG - 4 * WR))
                    pool.wait_ge(ss_done, i * WR + (b + 1 - 4 * WR))
                    x = qkvT[:, bass.ds(i * WR + (b - 4 * WR), 1), :].rearrange("p n t -> p (n t)")
                    nc.gpsimd.tensor_tensor(sq[:, b % 2, :], x, x, ALU.mult).then_inc(sq_done, 1)

                for n in range(2):
                    rest(n, n, n + 1)
                with pool.Fori(0, 4) as i:
                    for b in range(WR):
                        rest((b + 2) % WR, b % 2, i * WR + (b + 3))
                with pool.Fori(4, RZ) as i:
                    for b in range(WR):
                        squares(i, b)
                        rest((b + 2) % WR, b % 2, i * WR + (b + 3))
                for b in range(2):
                    rest(b + 2, b % 2, RZ * WR + b + 3)
                pool.wait_ge(hi_ready, N_PROJ + 1)
                flat = lambda w: w.rearrange("p k m -> p (k m)")
                nc.gpsimd.tensor_tensor(flat(w_lo[:, 0])[:, 0:KT * 2 * H], flat(w_ab[:]), flat(w_hi[:, 0])[:, 0:KT * 2 * H].bitcast(F32), ALU.subtract).then_inc(lo_ready, 1)

            @block.scalar
            def _(act):
                act.wait_ge(s_c, 16)
                nc.scalar.activation(c_row[:], c_row[:], ACT.Silu).then_inc(*A.step("c_silu"))
                act.wait_ge(s_x, 16 * TT)
                for t in range(TT):
                    nc.scalar.activation(xn[:, t * D:(t + 1) * D], x_tok[:, t, :], ACT.Square, accum_out=stat[:, 0, t:t + 1]).then_inc(*A.step(f"sq{t}"))
                act.wait_ge(*A.after(f"sq{TT - 1}"))
                act.wait_ge(*V.after("eps"))
                nc.scalar.activation(stat[:, 1, :], stat[:, 0, :], ACT.Sqrt, bias=eps[:], scale=1.0 / D).then_inc(*A.step("std"))

                def split(b, slot, landed, done):
                    act.wait_ge(s_w[b], landed)
                    if done is not None:
                        act.wait_ge(tile_done, done)
                    nc.scalar.activation(w_hi[:, slot], wring[:, b], ACT.Copy).then_inc(hi_ready, 1)

                for n in range(2):
                    split(n, n, 16, None)
                act.wait_ge(*V.after("scale1"))
                for k in range(KT):
                    act.wait_ge(*E.after(f"xT{k}"))
                    if k >= 2:
                        act.wait_ge(*V.after(f"lo{k - 2}"))
                    nc.scalar.activation(h_raw[:, k % 2], xT_ps[k][:], ACT.Identity, bias=mod[:, SH1 + k:SH1 + k + 1],
                                         scale=scale1[:, k:k + 1]).then_inc(*A.step(f"h{k}"))
                    act.wait_ge(*A.after(f"h{k}"))
                    nc.scalar.activation(h_hi[:, k, :], h_raw[:, k % 2], ACT.Copy).then_inc(*A.step(f"hi{k}"))

                def take(i, b):
                    act.wait_ge(tile_done, i * WR + (b + 1))
                    if not (isinstance(i, int) and i == 0):
                        act.wait_ge(raw_used, i * WR + (b + 1 - WR))
                    nc.scalar.activation(raw[:, b, 3:3 + T], proj_ps[b][:], ACT.Copy).then_inc(raw_ready, 1)
                    split((b + 2) % WR, b % 2, i * 16 + (16 if b < 2 else 32), None)

                def silu(i, b):
                    act.wait_ge(conv_done, i * WR + (b + 1 - RQ * WR))
                    nc.scalar.activation(qkvT[:, i * WR + (b - RQ * WR), :], acc[:, b % 2, :], ACT.Silu).then_inc(silu_done, 1)

                act.wait_ge(*V.after("pads_u"))
                for b in range(WR):
                    take(0, b)
                with act.Fori(1, RQ) as i:
                    for b in range(WR):
                        take(i, b)
                with act.Fori(RQ, RQ + 1) as i:
                    for b in range(WR):
                        take(i, b)
                        silu(i, b)
                with act.Fori(4, RZ) as i:
                    for b in range(WR):
                        take(i, b)
                        act.wait_ge(ss_done, i * WR + (b + 1 + LAG - 4 * WR))
                        act.wait_ge(unit_done, i * WR + (b + 1 - 4 * WR))
                        nc.scalar.activation(nrm[:, b % 2, :], ss_ps[b % 2][:], ACT.Sqrt, bias=eps[:]).then_inc(norm_done, 1)
                        silu(i, b)
                for b in range(N_Z):
                    act.wait_ge(tile_done, RZ * WR + b + 1)
                    if b < 2:
                        split(b + 2, b % 2, 16 * NI, None)
                    elif b == 2:
                        act.wait_ge(s_wab, 16)
                        flat = lambda w: w.rearrange("p k m -> p (k m)")
                        nc.scalar.activation(flat(w_hi[:, 0])[:, 0:KT * 2 * H], flat(w_ab[:]), ACT.Copy).then_inc(hi_ready, 1)
                    nc.scalar.activation(zT[:, b, :], proj_ps[b][:], ACT.Silu).then_inc(raw_ready, 1)

            @block.vector
            def _(dve):
                nc.vector.memset(raw[:, :, 0:3], 0.0).then_inc(*V.step("pads"))
                nc.vector.memset(eps[:], EPS).then_inc(*V.step("eps"))

                def mod_column(n):
                    dve.wait_ge(s_ada[n % AR], 16 * (n // AR + 1))
                    nc.vector.scalar_tensor_tensor(ada[:, n % AR], ada[:, n % AR], 1.0, c_row[:], ALU.mult, ALU.mult,
                                                   accum_out=mod[:, n:n + 1]).then_inc(ada_used, 1)

                dve.wait_ge(*A.after("c_silu"))
                for n in range(AR):
                    mod_column(n)
                dve.wait_ge(*A.after("std"))
                nc.vector.reciprocal(stat[:, 2, :], stat[:, 1, :]).then_inc(*V.step("rstd"))
                dve.wait_ge(*V.after("rstd"))
                for t in range(TT):
                    nc.vector.tensor_scalar(xn[:, t * D:(t + 1) * D], x_tok[:, t, :], stat[:, 2, t:t + 1], None, ALU.mult).then_inc(*V.step(f"xn{t}"))
                for n in range(AR, NA1):
                    mod_column(n)
                dve.wait_ge(ada_used, NA1)
                dve.wait_ge(s_small, 16 * 8)
                nc.vector.tensor_tensor(mod[:, SH1:SC1 + KT], mod[:, SH1:SC1 + KT], b_ada[:, SH1:SC1 + KT], ALU.add).then_inc(*V.step("mod1"))
                dve.wait_ge(*V.after("mod1"))
                nc.vector.tensor_scalar(scale1[:], mod[:, SC1:SC1 + KT], 1.0, None, ALU.add).then_inc(*V.step("scale_p"))
                dve.wait_ge(*V.after("scale_p"))
                nc.vector.tensor_tensor(scale1[:], scale1[:], norms[:, 0, :], ALU.mult).then_inc(*V.step("scale1"))
                for k in range(KT):
                    dve.wait_ge(*A.after(f"hi{k}"))
                    nc.vector.tensor_tensor(h_lo[:, k, :], h_raw[:, k % 2], h_hi[:, k, :].bitcast(F32), ALU.subtract).then_inc(*V.step(f"lo{k}"))
                dve.wait_ge(*E.after(f"xT{KT - 1}"))
                nc.vector.memset(upad[:, 0:2], 0.0).then_inc(*V.step("pads_u"))

                n_chain = 0
                for j in range(N_SC // 3):
                    c, x, b = (3 * j + m for m in range(3))
                    for m in range(4):
                        mod_column(NA1 + 6 * j + m)
                    dve.wait_ge(raw_ready, WR + x + 1)
                    nc.vector.tensor_tensor(upad[:, 2:2 + T], raw[:, c % WR, 3:3 + T], raw[:, x % WR, 3:3 + T], ALU.mult).then_inc(raw_used, 2)
                    dve.wait_ge(raw_used, 3 * j + 2)
                    nc.vector.tensor_scalar(conv[:, 0, :], upad[:, 2:2 + T], sc_w[:, j, 2:3], None, ALU.mult).then_inc(conv_chain, 1)
                    for k in (1, 0):
                        n_chain += 1
                        dve.wait_ge(conv_chain, n_chain)
                        nc.vector.scalar_tensor_tensor(conv[:, 2 - k, :], upad[:, k:k + T], sc_w[:, j, k:k + 1], conv[:, 1 - k, :],
                                                       ALU.mult, ALU.add).then_inc(conv_chain, 1)
                    n_chain += 1
                    dve.wait_ge(conv_chain, n_chain)
                    for m in range(4, 6):
                        mod_column(NA1 + 6 * j + m)
                    dve.wait_ge(raw_ready, WR + b + 1)
                    nc.vector.tensor_tensor(scT[:, j, :], conv[:, 2, :], raw[:, b % WR, 3:3 + T], ALU.mult).then_inc(raw_used, 1)

                def convolve(i, b):
                    n = i * WR + (b - RQ * WR)
                    dve.wait_ge(raw_ready, i * WR + (WR + b + 1))
                    nc.vector.tensor_scalar(conv[:, 0, :], raw[:, b, 3:3 + T], dn_w[:, n, 3:4], None, ALU.mult).then_inc(conv_chain, 1)
                    for k in (2, 1):
                        dve.wait_ge(conv_chain, i * (3 * WR) + (n_chain - 3 * WR * RQ + 3 * b + 3 - k))
                        nc.vector.scalar_tensor_tensor(conv[:, 3 - k, :], raw[:, b, k:k + T], dn_w[:, n, k:k + 1], conv[:, 2 - k, :],
                                                       ALU.mult, ALU.add).then_inc(conv_chain, 1)
                    dve.wait_ge(conv_chain, i * (3 * WR) + (n_chain - 3 * WR * RQ + 3 * b + 3))
                    dve.wait_ge(silu_done, i * WR + (b + 1 - RQ * WR))
                    nc.vector.scalar_tensor_tensor(acc[:, b % 2, :], raw[:, b, 0:T], dn_w[:, n, 0:1], conv[:, 2, :],
                                                   ALU.mult, ALU.add).then_inc(conv_done, 1)
                    dve.wait_ge(conv_done, i * WR + (b + 1 - RQ * WR))
                    dve.sem_inc(raw_used, 1)

                for b in range(WR):
                    for m in range(2):
                        mod_column(NA1 + 6 * (N_SC // 3) + 2 * b + m)
                    convolve(RQ, b)
                with dve.Fori(4, RZ) as i:
                    for b in range(WR):
                        convolve(i, b)
                        m = i * WR + (b - 4 * WR)
                        dve.wait_ge(norm_done, i * WR + (b + 1 + LAG - 4 * WR))
                        nc.vector.reciprocal(nrm[:, b % 2, :], nrm[:, b % 2, :]).then_inc(inv_done, 1)
                        dve.wait_ge(inv_done, i * WR + (b + 1 - 4 * WR))
                        nc.vector.tensor_tensor(qkvT[:, m, :], nrm[:, b % 2, :], qkvT[:, m, :], ALU.mult).then_inc(unit_done, 1)
                for n in range(2):
                    dve.wait_ge(tile_done, N_PROJ + n + 1)
                    nc.vector.tensor_copy(abT[:, n, :], ab_ps[n][0:H, :]).then_inc(last_v, 1)
                dve.wait_ge(ada_used, NA)
                nc.vector.tensor_tensor(mod[:, GT1:MOD], mod[:, GT1:MOD], b_ada[:, GT1:MOD], ALU.add).then_inc(last_v, 1)


def delta_stage(nc, a, env):
    g_ = env
    bank, C, eps = g_["bank"], g_["C"], g_["eps"]
    qkvT, zT, abT = g_["qkvT"], g_["zT"], g_["abT"]
    sel_head, sel_pair, carry = g_["sel_head"], g_["sel_pair"], g_["carry"]
    sb, sem = g_["sb"], g_["sem"]
    G2 = range(2)
    with ExitStack() as ctx:
        ga = sb(ctx, "gate_work", [H, 4, T])
        rows = sb(ctx, "decay_rows", [H, 3, T])
        exp_a = sb(ctx, "exp_a", [H, 1])
        cols = sb(ctx, "decay_cols", [P, 3, TT, H])
        neg_g = sb(ctx, "neg_g", [P, TT, H])
        e_kd = sb(ctx, "e_kd", [P, TT, H])
        e_g = sb(ctx, "e_g", [P, TT, H])
        be_g = sb(ctx, "be_g", [P, TT, H])
        dec = sb(ctx, "decay", [P, 2, HJ, P])
        decT = sb(ctx, "decayT", [P, 2, HJ, P])
        kbT = sb(ctx, "kbT", [P, HJ, P])
        qgT = sb(ctx, "qgT", [P, HJ, P])
        egT = sb(ctx, "egT", [P, HJ, P])
        kdec = sb(ctx, "kdec", [P, H, DK])
        rw = sb(ctx, "rhs_w", [P, H, DK])
        rv = sb(ctx, "rhs_v", [P, H, DK])
        L, LT = (sb(ctx, n, [P, HJ, P]) for n in ("L", "LT"))
        aT = sb(ctx, "attnT", [P, 2, HJ, P])
        W = {(n, g): sb(ctx, f"{n}_{g}", [P, HJ, P]) for g in G2
             for n in ("A", "AT", "CT", "B", "BT", "PT", "QT")}
        u = sb(ctx, "u", [P, 2, HJ, DK])
        wT = sb(ctx, "wT", [P, HJ, P])
        qkv = sb(ctx, "qkv_tile", [P, 12, P])
        S = sb(ctx, "state", [P, HJ, DK])
        Sd = sb(ctx, "state_decayed", [P, HJ, DK])
        vn = sb(ctx, "v_new", [P, 2, HJ, DK])
        oS = sb(ctx, "o_state", [P, 2, HJ, DK])
        o = sb(ctx, "o", [P, 2, HJ, DK])
        on = sb(ctx, "o_normed", [P, HJ, 2, DK])
        ost = sb(ctx, "o_stat", [P, 3, H])

        pre_v = ["a_bias", "a_max", "a_neg", "a_min", "b_plus", "beta", "softplus", "g", "G", "G_left", "cols", "neg_g", "be_g", "S0"]
        pre_a = ["exp_b", "exp_a", "exp_x", "log", "e_kd", "e_g"]
        pre_e = ["cols"]
        loop_v = ["pre0", "preT0", "pre1", "preT1", "kb", "kdec", "rw", "rv", "qg"]
        for g in G2:
            loop_v += [f"L{g}", f"LT{g}", f"aT{g}"]
        levels_v = ["P1", "P2", "P3", "P4", "MT", "Q1", "TT"]
        loop_v += [f"{x}{g}" for x in levels_v for g in G2] + ["u0", "u1"]
        for c in G2:
            loop_v += [f"Sd{c}", f"vn{c}0", f"vn{c}1", f"S{c}", f"o{c}"]
        loop_v += ["osq", "oss", "ostd", "on", "oT"]
        loop_a = ["egT"] + [f"dec{g}{j}" for g in G2 for j in range(HJ)] + [f"decT{g}{j}" for g in G2 for j in range(HJ)]
        loop_a += [f"{x}{g}" for x in ["A2", "A2T", "A4", "A4T", "A8", "P", "M", "M2"] for g in G2] + ["wT"]
        loop_a += ["oi00", "oi01", "oi10", "oi11", "ostd"]
        loop_p = ["tile"] + [f"{x}{g}" for g in G2 for x in ("near", "nearT", "farT")]
        loop_e = ["grow0", "grow1", "betaT", "GT", "kX", "vX"] + [f"{x}{g}" for g in G2 for x in ("kk", "kkT", "qk")]
        loop_e += [f"{x}{g}" for x in ["A2", "A2T", "A4", "A4T", "PA2", "A8", "PA4", "PA8", "P", "M", "MT", "M2", "Q1", "TT"] for g in G2]
        loop_e += ["u0", "u1", "wT"]
        for c in G2:
            loop_e += [f"wS{c}0", f"wS{c}1", f"oi{c}0", f"oi{c}1", f"dS{c}", f"oa{c}"]
        loop_e += ["oT"]
        sv, sa, se, spl = (sem(ctx, f"dn_{n}") for n in ("vector", "scalar", "tensor", "pool"))
        V0, A0, E0 = Steps(sv, pre_v), Steps(sa, pre_a), Steps(se, pre_e)
        V, A, E = Steps(sv, loop_v, len(pre_v)), Steps(sa, loop_a, len(pre_a)), Steps(se, loop_e, len(pre_e))
        Q = Steps(spl, loop_p)
        held = sem(ctx, "held")

        def flat(t):
            return t.rearrange("p j m -> p (j m)")

        def mask(name):
            return C[name].unsqueeze(1).to_broadcast([P, HJ, P])

        def b4(n):
            return bank[n][:].rearrange("p (j m) -> p j m", j=HJ)

        with nc.Block() as block:
            @block.scalar
            def _(act):
                nc.scalar.activation(abT[:, 1, :], abT[:, 1, :], ACT.Exp, scale=-1.0).then_inc(*A0.step("exp_b"))
                nc.scalar.activation(exp_a[:], g_["a_log"][:], ACT.Exp).then_inc(*A0.step("exp_a"))
                act.wait_ge(*V0.after("a_min"))
                nc.scalar.activation(ga[:, 3, :], ga[:, 3, :], ACT.Exp).then_inc(*A0.step("exp_x"))
                act.wait_ge(*A0.after("exp_x"))
                nc.scalar.activation(ga[:, 3, :], ga[:, 3, :], ACT.Ln, bias=1.0).then_inc(*A0.step("log"))
                act.wait_ge(*V0.after("cols"))
                nc.scalar.activation(e_kd[:], cols[:, 2], ACT.Exp).then_inc(*A0.step("e_kd"))
                nc.scalar.activation(e_g[:], cols[:, 0], ACT.Exp).then_inc(*A0.step("e_g"))
                with act.Fori(0, TT) as tt:
                    act.wait_ge(*E.after("GT", tt))
                    nc.scalar.activation(flat(egT[:]), bank[3][:], ACT.Exp).then_inc(*A.step("egT"))
                    for d, v, bias, name in ((dec, "pre", cols[:, 0], "dec"), (decT, "preT", neg_g[:], "decT")):
                        for g in G2:
                            act.wait_ge(*V.after(f"{v}{g}", tt))
                            for j in range(HJ):
                                h = 2 * j + g
                                nc.scalar.activation(d[:, g, j, :], d[:, g, j, :], ACT.Exp, bias=bias[:, tt, h:h + 1]).then_inc(*A.step(f"{name}{g}{j}"))

                    def take(name, dst, src, g):
                        act.wait_ge(*E.after(f"{name}{g}", tt))
                        nc.scalar.activation(flat(dst[:]), bank[src][:], ACT.Copy).then_inc(*A.step(f"{name}{g}"))

                    b0 = (4, 7)
                    b1 = (5, 0)
                    for name, dst, bs in (("A2", "B", b0), ("A2T", "BT", b1), ("A4", "A", b0), ("A4T", "AT", b1), ("A8", "B", b0),
                                          ("P", "BT", b0), ("M", "A", b1), ("M2", "B", b0)):
                        for g in G2:
                            if name == "A4T":
                                act.wait_ge(*V.after(f"P1{g}", tt))
                            take(name, W[dst, g], bs[g], g)
                    act.wait_ge(*E.after("wT", tt))
                    nc.scalar.activation(flat(wT[:]), bank[2][:], ACT.Copy).then_inc(*A.step("wT"))
                    for c in G2:
                        r = slice(CH * c, CH * c + CH)
                        for g in G2:
                            act.wait_ge(*E.after(f"oi{c}{g}", tt))
                            nc.scalar.activation(oS[r, g], bank[5 + g][r, 0:HJ * DK], ACT.Copy).then_inc(*A.step(f"oi{c}{g}"))
                    act.wait_ge(*V.after("oss", tt))
                    nc.scalar.activation(ost[:, 1, :], ost[:, 0, :], ACT.Sqrt, bias=eps[:], scale=1.0 / DK).then_inc(*A.step("ostd"))

            @block.gpsimd
            def _(pool):
                with pool.Fori(0, TT) as tt:
                    pool.wait_ge(*V.after("oT", tt, 1))
                    nc.gpsimd.tensor_copy(qkv[:], qkvT[:, :, bass.ds(tt * P, P)]).then_inc(*Q.step("tile"))
                    for g in G2:
                        pool.wait_ge(*V.after(f"L{g}", tt))
                        nc.gpsimd.tensor_tensor(W["A", g][:], L[:], mask("neg_near"), ALU.mult).then_inc(*Q.step(f"near{g}"))
                        pool.wait_ge(*V.after(f"LT{g}", tt))
                        nc.gpsimd.tensor_tensor(W["AT", g][:], LT[:], mask("neg_nearT"), ALU.mult).then_inc(*Q.step(f"nearT{g}"))
                        nc.gpsimd.tensor_tensor(W["CT", g][:], LT[:], mask("neg_farT"), ALU.mult).then_inc(*Q.step(f"farT{g}"))

            @block.tensor
            def _(pe):
                pe.wait_ge(*V0.after("G_left"))
                for n in range(3):
                    for t in range(TT):
                        m = (n * TT + t) * H
                        last = nc.tensor.transpose(bank[2][:, m:m + H], rows[:, n, t * P:(t + 1) * P], C["ident"][0:H, 0:H])
                last.then_inc(*E0.step("cols"))
                pe.wait_ge(*V0.after("cols"))
                with pe.Fori(0, TT) as tt:
                    tok = bass.ds(tt * P, P)
                    pe.wait_ge(*V.after("oT", tt, 1))

                    def group(name, n, products, transpose=False):
                        for j in range(HJ):
                            lhs, rhs = products(j)
                            if transpose:
                                last = nc.tensor.transpose(bank[n][:, j * P:(j + 1) * P], lhs, C["ident"])
                            else:
                                last = nc.tensor.matmul(bank[n][:, j * P:(j + 1) * P], lhs, rhs, start=True, stop=True)
                        last.then_inc(*E.step(name))

                    for g in G2:
                        group(f"grow{g}", g, lambda j: (sel_head[:, 2 * j + g, :], rows[:, 0, tok]))
                    group("betaT", 2, lambda j: (sel_pair[:, j, :], rows[:, 1, tok]))
                    group("GT", 3, lambda j: (sel_pair[:, j, :], rows[:, 0, tok]))
                    pe.wait_ge(*Q.after("tile", tt))
                    group("kX", 4, lambda j: (qkv[:, HJ + j, :], None), transpose=True)
                    group("vX", 5, lambda j: (qkv[:, 2 * HJ + j, :], None), transpose=True)
                    pe.wait_ge(*V.after("kb", tt))
                    for g, banks in ((0, (6, 7, 0)), (1, (1, 2, 3))):
                        r = slice(DK * g, DK * g + DK)
                        if g == 1:
                            pe.wait_ge(*A.after("egT", tt))
                        group(f"kk{g}", banks[0], lambda j: (kbT[r, j, :], qkv[r, HJ + j, :]))
                        group(f"kkT{g}", banks[1], lambda j: (qkv[r, HJ + j, :], kbT[r, j, :]))
                        group(f"qk{g}", banks[2], lambda j: (qkv[r, HJ + j, :], qkv[r, j, :]))
                    b0, b1, b2 = (4, 7), (5, 0), (6, 1)

                    def level(name, banks, lhs, rhs, waits, transpose=False):
                        for g in G2:
                            for w in waits(g):
                                pe.wait_ge(*w)
                            group(f"{name}{g}", banks[g], lambda j: (W[lhs, g][:, j, :], rhs and W[rhs, g][:, j, :]), transpose)

                    VA, AA, PA = (lambda n: V.after(n, tt)), (lambda n: A.after(n, tt)), (lambda n: Q.after(n, tt))
                    level("A2", b0, "AT", "A", lambda g: [PA(f"nearT{g}"), VA("rv"), VA(f"LT{g}"), VA(f"aT{g}")])
                    level("A2T", b1, "A", "AT", lambda g: [])
                    level("A4", b0, "BT", "B", lambda g: [AA(f"A2{g}"), AA(f"A2T{g}")])
                    level("A4T", b1, "B", "BT", lambda g: [])
                    level("PA2", b2, "B", "PT", lambda g: [VA(f"P1{g}")])
                    level("A8", b0, "AT", "A", lambda g: [AA(f"A4{g}"), AA(f"A4T{g}")])
                    level("PA4", b2, "A", "PT", lambda g: [VA(f"P2{g}")])
                    level("PA8", b1, "B", "PT", lambda g: [AA(f"A8{g}"), VA(f"P3{g}")])
                    level("P", b0, "PT", None, lambda g: [VA(f"P4{g}")], transpose=True)
                    level("M", b1, "CT", "BT", lambda g: [PA(f"farT{g}"), AA(f"P{g}")])
                    level("MT", b2, "BT", "CT", lambda g: [])
                    level("M2", b0, "QT", "A", lambda g: [AA(f"M{g}"), VA(f"MT{g}")])
                    level("Q1", b1, "A", "PT", lambda g: [])
                    level("TT", b2, "B", "QT", lambda g: [AA(f"M2{g}"), VA(f"Q1{g}")])
                    for g in G2:
                        pe.wait_ge(*VA(f"TT{g}"))
                        for j in range(HJ):
                            last = nc.tensor.matmul(bank[b0[g]][:, j * DK:(j + 1) * DK], W["AT", g][:, j, :], rv[:, 2 * j + g, :], start=True, stop=True)
                        last.then_inc(*E.step(f"u{g}"))
                    for j in range(HJ):
                        for g in G2:
                            last = nc.tensor.matmul(bank[2][DK * g:DK * g + DK, j * P:(j + 1) * P], rw[:, 2 * j + g, :], W["AT", g][:, j, :], start=True, stop=True)
                    last.then_inc(*E.step("wT"))
                    for c in G2:
                        r = slice(CH * c, CH * c + CH)
                        if c == 0:
                            pe.wait_ge(*AA("wT"))
                            pe.wait_ge(*VA("u1"))
                        else:
                            pe.wait_ge(*VA("S0"))
                        pe.sem_inc(held, 1)
                        for g in G2:
                            q = slice(DK * g, DK * g + DK)
                            for j in range(HJ):
                                last = nc.tensor.matmul(bank[3 + g][r, j * DK:(j + 1) * DK], wT[q, j, r], S[q, j, :], start=True, stop=True)
                            last.then_inc(*E.step(f"wS{c}{g}"))
                        for g in G2:
                            q = slice(DK * g, DK * g + DK)
                            if c == 1:
                                pe.wait_ge(*AA(f"oi0{g}"))
                                pe.sem_inc(held, 1)
                            for j in range(HJ):
                                last = nc.tensor.matmul(bank[5 + g][r, j * DK:(j + 1) * DK], qgT[q, j, r], S[q, j, :], start=True, stop=True)
                            last.then_inc(*E.step(f"oi{c}{g}"))
                        pe.wait_ge(*VA(f"vn{c}1"))
                        pe.sem_inc(held, 1)
                        for j in range(HJ):
                            for g in G2:
                                last = nc.tensor.matmul(bank[0][DK * g:DK * g + DK, j * DK:(j + 1) * DK], kdec[r, 2 * j + g, :], vn[r, g, j, :], start=True, stop=True)
                        last.then_inc(*E.step(f"dS{c}"))
                        if c == 1:
                            pe.wait_ge(*VA("o0"))
                            pe.sem_inc(held, 1)
                        for g in G2:
                            for j in range(HJ):
                                m = (g * HJ + j) * DK
                                last = nc.tensor.matmul(bank[7][r, m:m + DK], aT[r, g, j, r], vn[r, g, j, :], start=True, stop=True)
                        last.then_inc(*E.step(f"oa{c}"))
                    pe.wait_ge(*VA("on"))
                    group("oT", 1, lambda j: (on[:, j].rearrange("p g d -> p (g d)"), None), transpose=True)

            @block.vector
            def _(dve):
                nc.vector.tensor_scalar(ga[:, 0, :], abT[:, 0, :], g_["dt_bias"][:], None, ALU.add).then_inc(*V0.step("a_bias"))
                dve.wait_ge(*V0.after("a_bias"))
                nc.vector.tensor_scalar(ga[:, 1, :], ga[:, 0, :], 0.0, None, ALU.max).then_inc(*V0.step("a_max"))
                nc.vector.tensor_scalar(ga[:, 2, :], ga[:, 0, :], -1.0, None, ALU.mult).then_inc(*V0.step("a_neg"))
                dve.wait_ge(*V0.after("a_neg"))
                nc.vector.tensor_tensor(ga[:, 3, :], ga[:, 0, :], ga[:, 2, :], ALU.min).then_inc(*V0.step("a_min"))
                dve.wait_ge(*A0.after("exp_b"))
                nc.vector.tensor_scalar(abT[:, 1, :], abT[:, 1, :], 1.0, None, ALU.add).then_inc(*V0.step("b_plus"))
                dve.wait_ge(*V0.after("b_plus"))
                nc.vector.reciprocal(rows[:, 1, :], abT[:, 1, :]).then_inc(*V0.step("beta"))
                dve.wait_ge(*A0.after("log"))
                nc.vector.tensor_tensor(ga[:, 0, :], ga[:, 1, :], ga[:, 3, :], ALU.add).then_inc(*V0.step("softplus"))
                dve.wait_ge(*V0.after("softplus"))
                nc.vector.tensor_scalar(ga[:, 2, :], ga[:, 0, :], exp_a[:], -1.0, ALU.mult, ALU.mult).then_inc(*V0.step("g"))
                dve.wait_ge(*V0.after("g"))
                nc.vector.tensor_tensor_scan(rows[:, 0, :], carry, ga[:, 2, :], 0.0, ALU.mult, ALU.add).then_inc(*V0.step("G"))
                dve.wait_ge(*V0.after("G"))
                by_chunk = rows[:, 0, :].rearrange("h (n c) -> h n c", c=CH)
                nc.vector.tensor_tensor(rows[:, 2, :].rearrange("h (n c) -> h n c", c=CH), by_chunk[:, :, CH - 1:CH].to_broadcast([H, T // CH, CH]),
                                        by_chunk, ALU.subtract).then_inc(*V0.step("G_left"))
                dve.wait_ge(*E0.after("cols"))
                nc.vector.tensor_copy(cols[:].rearrange("p a t h -> p (a t h)"), bank[2][:, 0:3 * TT * H]).then_inc(*V0.step("cols"))
                dve.wait_ge(*V0.after("cols"))
                nc.vector.tensor_scalar(neg_g[:], cols[:, 0], -1.0, None, ALU.mult).then_inc(*V0.step("neg_g"))
                dve.wait_ge(*A0.after("e_g"))
                nc.vector.tensor_tensor(be_g[:], e_g[:], cols[:, 1], ALU.mult).then_inc(*V0.step("be_g"))
                nc.vector.memset(S[:], 0.0).then_inc(*V0.step("S0"))

                with dve.Fori(0, TT) as tt:
                    tok = bass.ds(tt * P, P)
                    VA, AA, EA, PA = ((lambda n, s=s: s.after(n, tt)) for s in (V, A, E, Q))

                    def per_head(c):
                        return c[:, tt, :].unsqueeze(2).to_broadcast([P, H, DK])

                    for g in G2:
                        dve.wait_ge(*EA(f"grow{g}"))
                        nc.vector.scalar_tensor_tensor(dec[:, g], b4(g), -1.0, mask("causal"), ALU.mult, ALU.add).then_inc(*V.step(f"pre{g}"))
                        nc.vector.tensor_tensor(decT[:, g], b4(g), mask("causalT"), ALU.add).then_inc(*V.step(f"preT{g}"))
                    dve.wait_ge(*PA("tile"))
                    dve.wait_ge(*EA("betaT"))
                    nc.vector.tensor_tensor(kbT[:], qkv[:, HJ:2 * HJ, :], b4(2), ALU.mult).then_inc(*V.step("kb"))
                    dve.wait_ge(*EA("kX"))
                    heads = bank[4][:].rearrange("p (h d) -> p h d", h=H)
                    nc.vector.tensor_tensor(kdec[:], heads, per_head(e_kd), ALU.mult).then_inc(*V.step("kdec"))
                    nc.vector.tensor_tensor(rw[:], heads, per_head(be_g), ALU.mult).then_inc(*V.step("rw"))
                    dve.wait_ge(*EA("vX"))
                    nc.vector.tensor_tensor(rv[:], bank[5][:].rearrange("p (h d) -> p h d", h=H), per_head(cols[:, 1]), ALU.mult).then_inc(*V.step("rv"))
                    dve.wait_ge(*AA("egT"))
                    nc.vector.scalar_tensor_tensor(qgT[:], qkv[:, 0:HJ, :], DK ** -0.5, egT[:], ALU.mult, ALU.mult).then_inc(*V.step("qg"))
                    for g, banks in ((0, (6, 7, 0)), (1, (1, 2, 3))):
                        dve.wait_ge(*AA(f"decT{g}{HJ - 1}"))
                        dve.wait_ge(*EA(f"kk{g}"))
                        if g:
                            dve.wait_ge(*PA("near0"))
                        nc.vector.tensor_tensor(L[:], b4(banks[0]), dec[:, g], ALU.mult).then_inc(*V.step(f"L{g}"))
                        dve.wait_ge(*EA(f"kkT{g}"))
                        if g:
                            dve.wait_ge(*PA("farT0"))
                        nc.vector.tensor_tensor(LT[:], b4(banks[1]), decT[:, g], ALU.mult).then_inc(*V.step(f"LT{g}"))
                        dve.wait_ge(*EA(f"qk{g}"))
                        nc.vector.scalar_tensor_tensor(aT[:, g], b4(banks[2]), DK ** -0.5, decT[:, g], ALU.mult, ALU.mult).then_inc(*V.step(f"aT{g}"))
                    b1, b2 = (5, 0), (6, 1)

                    def plus(name, dst, add, banks, product):
                        for g in G2:
                            dve.wait_ge(*EA(f"{product}{g}"))
                            nc.vector.tensor_tensor(flat(W[dst, g][:]), flat(W[add, g][:]), bank[banks[g]][:], ALU.add).then_inc(*V.step(f"{name}{g}"))

                    for g in G2:
                        dve.wait_ge(*PA(f"nearT{g}"))
                        nc.vector.tensor_tensor(W["PT", g][:], W["AT", g][:], mask("ident"), ALU.add).then_inc(*V.step(f"P1{g}"))
                    dve.wait_ge(*VA("P11"))
                    plus("P2", "PT", "PT", b2, "PA2")
                    dve.wait_ge(*VA("P21"))
                    plus("P3", "PT", "PT", b2, "PA4")
                    dve.wait_ge(*VA("P31"))
                    plus("P4", "PT", "PT", b1, "PA8")
                    for g in G2:
                        dve.wait_ge(*EA(f"MT{g}"))
                        nc.vector.tensor_copy(flat(W["QT", g][:]), bank[b2[g]][:]).then_inc(*V.step(f"MT{g}"))
                    for g in G2:
                        dve.wait_ge(*EA(f"M2{g}"))
                        dve.wait_ge(*EA(f"Q1{g}"))
                        nc.vector.tensor_tensor(flat(W["QT", g][:]), flat(W["PT", g][:]), bank[b1[g]][:], ALU.add).then_inc(*V.step(f"Q1{g}"))
                    dve.wait_ge(*VA("Q11"))
                    plus("TT", "AT", "QT", b2, "TT")
                    for g in G2:
                        dve.wait_ge(*EA(f"u{g}"))
                        nc.vector.tensor_copy(u[:, g].rearrange("p j d -> p (j d)"), bank[(4, 7)[g]][:, 0:HJ * DK]).then_inc(*V.step(f"u{g}"))
                    for c in G2:
                        r = slice(CH * c, CH * c + CH)
                        last = CH * c + CH - 1
                        nc.vector.tensor_tensor(Sd[:], S[:], egT[:, :, last:last + 1].to_broadcast([P, HJ, DK]), ALU.mult).then_inc(*V.step(f"Sd{c}"))
                        for g in G2:
                            dve.wait_ge(*EA(f"wS{c}{g}"))
                            nc.vector.tensor_tensor(vn[r, g], u[r, g], bank[3 + g][r, 0:HJ * DK].rearrange("p (j d) -> p j d", j=HJ),
                                                    ALU.subtract).then_inc(*V.step(f"vn{c}{g}"))
                        dve.wait_ge(*EA(f"dS{c}"))
                        nc.vector.tensor_tensor(S[:], Sd[:], bank[0][:, 0:HJ * DK].rearrange("p (j d) -> p j d", j=HJ), ALU.add).then_inc(*V.step(f"S{c}"))
                        dve.wait_ge(*EA(f"oa{c}"))
                        dve.wait_ge(*AA(f"oi{c}1"))
                        nc.vector.tensor_tensor(o[r], oS[r], bank[7][r, :].rearrange("p (g j d) -> p g j d", g=2, j=HJ), ALU.add).then_inc(*V.step(f"o{c}"))
                        dve.wait_ge(*VA(f"S{c}"))
                    dve.wait_ge(*VA("o1"))
                    o8 = o[:].rearrange("p g j d -> p (g j) d")
                    sq8 = oS[:].rearrange("p g j d -> p (g j) d")
                    nc.vector.tensor_tensor(sq8, o8, o8, ALU.mult).then_inc(*V.step("osq"))
                    dve.wait_ge(*VA("osq"))
                    nc.vector.tensor_reduce(ost[:, 0, :], sq8, AX.X, ALU.add).then_inc(*V.step("oss"))
                    dve.wait_ge(*AA("ostd"))
                    nc.vector.reciprocal(ost[:, 2, :], ost[:, 1, :]).then_inc(*V.step("ostd"))
                    dve.wait_ge(*VA("ostd"))
                    nc.vector.tensor_tensor(on[:].rearrange("p j g d -> p g j d"), o[:],
                                            ost[:, 2, :].rearrange("p (g j) -> p g j", g=2).unsqueeze(3).to_broadcast([P, 2, HJ, DK]),
                                            ALU.mult).then_inc(*V.step("on"))
                    dve.wait_ge(*EA("oT"))
                    nc.vector.scalar_tensor_tensor(zT[:, :, tok], b4(1), g_["out_norm"][:], zT[:, :, tok], ALU.mult, ALU.mult).then_inc(*V.step("oT"))


def merge_stage(nc, a, env):
    g_ = env
    bank, C, mod, norms, stat, eps = g_["bank"], g_["C"], g_["mod"], g_["norms"], g_["stat"], g_["eps"]
    x_tok, h_hi, h_lo, scT, oT = g_["x_tok"], g_["h_hi"], g_["h_lo"], g_["scT"], g_["zT"]
    row_ffn = g_["row_ffn"]
    sb, sem = g_["sb"], g_["sem"]
    NM, NW = 3 * KT, 4 * KT
    with ExitStack() as ctx:
        row_mix = sb(ctx, "row_mix", [P, D])
        wm = sb(ctx, "merge_w", [P, 2, KT, P])
        w_hi = sb(ctx, "merge_w_hi", [P, 2, KT, P], F32R)
        w_lo = sb(ctx, "merge_w_lo", [P, 2, KT, P], F32R)
        br_hi = sb(ctx, "branches_hi", [P, 2, HJ, T], F32R)
        br_lo = sb(ctx, "branches_lo", [P, 2, HJ, T], F32R)
        work = sb(ctx, "merge_work", [P, TT, D])
        sg, part = (work[:, 2 * n:2 * n + 2, :].rearrange("p b (n t) -> p b n t", n=2) for n in range(2))
        xn = tmp = work
        m_hi = sb(ctx, "merged_hi", [P, KT, T], F32R)
        m_lo = sb(ctx, "merged_lo", [P, KT, T], F32R)
        diag = sb(ctx, "diag", [P, KT, P])
        gate = sb(ctx, "gate", [P, 2, KT])
        ss = sb(ctx, "y_squares", [P, TT, 2])
        s_m = [sem(ctx, f"merge_landed{i}") for i in range(2)]
        hi_ready, lo_ready, piece_done, sg_ready, br_ready = (sem(ctx, n) for n in (
            "mg_hi_ready", "mg_lo_ready", "mg_piece_done", "mg_sigmoid_ready", "mg_branch_hi"))
        pre_v = ["gate0", "diag0", "gate1", "diag1", "br_lo0", "br_lo1"]
        loop_v = [f"{x}{b}" for b in range(2) for x in ("sc", "dn", "sum", "hi", "lo")]
        n_loop = KT // 2
        post_v = [x for t in range(TT + 1) for x in ([f"ss{t}", f"rstd{t}", f"y0_{t}", f"y1_{t}", f"x{t}"] if t < TT else [])
                  + ([f"rstd2_{t - 1}"] if t else [])]
        post_a = [x for t in range(TT + 1) for x in ([f"sq0_{t}", f"sq1_{t}", f"std{t}"] if t < TT else [])
                  + ([f"sqx{t - 1}", f"std2_{t - 1}"] if t else [])]
        sv, sa, se = (sem(ctx, f"mg_{n}") for n in ("vector", "scalar", "tensor"))
        V0, A0, E0 = Steps(sv, pre_v), Steps(sa, [f"row{n}" for n in range(4)]), Steps(se, [f"row{n}" for n in range(4)])
        V = Steps(sv, loop_v, len(pre_v) + len(loop_v))
        V2, A2 = Steps(sv, post_v, len(pre_v) + (1 + n_loop) * len(loop_v)), Steps(sa, post_a, 4)
        E2 = Steps(se, [f"y{half}_{t}" for t in range(TT) for half in range(2)], 4)
        PARTS = ((0, 0), (0, 1), (1, 0))

        with nc.Block() as block:
            @block.sync
            def _(sp):
                for b in range(2):
                    sp.dma_start(wm[:, b], a["w_merge"][b]).then_inc(s_m[b], 16)
                with sp.Fori(1, NW // 2) as i:
                    for b in range(2):
                        sp.wait_ge(lo_ready, i * 2 + (b - 1))
                        sp.dma_start(wm[:, b], a["w_merge"][i * 2 + b]).then_inc(s_m[b], 16)

            @block.tensor
            def _(pe):
                for n in range(2):
                    pe.wait_ge(*V0.after(f"diag{n}"))
                    for half in range(2):
                        for k in range(HJ):
                            last = nc.tensor.matmul(bank[4 + 2 * n + half][:, k * P:(k + 1) * P], C["ones"], diag[:, HJ * half + k, :], start=True, stop=True)
                        last.then_inc(*E0.step(f"row{2 * n + half}"))
                w = (w_hi, w_lo)

                def products(out, slot, k0, x):
                    kn = x[0].shape[1]
                    for k in range(kn):
                        for n, (l, r) in enumerate(PARTS):
                            last = nc.tensor.matmul(out, w[l][:, slot, k0 + k, :], x[r][:, k, :], start=(k == 0 and n == 0), stop=(k == kn - 1 and n == 2))
                    return last

                with pe.Fori(0, n_loop) as i:
                    for b in range(2):
                        pe.wait_ge(*V.after(f"dn{b}", i, 1))
                        if b == 1:
                            pe.wait_ge(*A0.after("row3"))
                        for n in range(3):
                            m = 3 * b + n
                            pe.wait_ge(lo_ready, i * 6 + (m + 1))
                            if n < 2:
                                last = products(bank[4 * b + n][:], m % 2, 0, (h_hi[:], h_lo[:]))
                            else:
                                pe.wait_ge(*V0.after("br_lo1"))
                                for q in range(2):
                                    last = products(bank[4 * b + 2 + q][:], m % 2, HJ * q, (br_hi[:, q], br_lo[:, q]))
                            last.then_inc(piece_done, 1)

                def mix(k, slot, t, half, start, stop):
                    for n, (l, r) in enumerate(PARTS):
                        last = nc.tensor.matmul(bank[2 * t + half][:], (m_hi, m_lo)[l][:, k, t * P:(t + 1) * P],
                                                w[r][:, slot, 4 * half:4 * half + 4, :].rearrange("p k m -> p (k m)"),
                                                start=(start and n == 0), stop=(stop and n == 2))
                    return last

                outs = [(t, half) for t in range(TT) for half in range(2)]
                for k in range(KT - 2):
                    pe.wait_ge(lo_ready, NM + k + 1)
                    for t, half in outs:
                        if k == 0 and (t, half) in ((0, 0), (TT // 2, 0)):
                            pe.wait_ge(*V.after(f"lo{t // (TT // 2)}", n_loop - 1))
                        last = mix(k, k % 2, t, half, k == 0, False)
                    last.then_inc(piece_done, 1)
                pe.wait_ge(lo_ready, NW)
                for t, half in outs:
                    mix(KT - 2, 0, t, half, False, False)
                    mix(KT - 1, 1, t, half, False, True).then_inc(*E2.step(f"y{half}_{t}"))

            @block.gpsimd
            def _(pool):
                with pool.Fori(0, NW // 2) as i:
                    for b in range(2):
                        pool.wait_ge(hi_ready, i * 2 + (b + 1))
                        nc.gpsimd.tensor_tensor(w_lo[:, b], wm[:, b], w_hi[:, b].bitcast(F32), ALU.subtract).then_inc(lo_ready, 1)

            @block.scalar
            def _(act):
                def split(b, landed):
                    act.wait_ge(s_m[b], landed)
                    nc.scalar.activation(w_hi[:, b], wm[:, b], ACT.Copy).then_inc(hi_ready, 1)

                for b in range(2):
                    split(b, 16)
                for n, x in enumerate((scT, oT)):
                    nc.scalar.activation(br_hi[:, n], x[:], ACT.Copy).then_inc(br_ready, 1)
                for n in range(4):
                    act.wait_ge(*E0.after(f"row{n}"))
                    dst = (row_mix, row_ffn)[n // 2]
                    nc.scalar.activation(dst[:, 512 * (n % 2):512 * (n % 2) + 512], bank[4 + n][:], ACT.Copy).then_inc(*A0.step(f"row{n}"))
                with act.Fori(0, n_loop) as i:
                    for m in range(6):
                        b, n = m // 3, m % 3
                        act.wait_ge(piece_done, i * 6 + (m + 1))
                        split(m % 2, i * 48 + 16 * (m // 2 + 2))
                        if n < 2:
                            act.wait_ge(*V.after(f"dn{b}", i, 1))
                            nc.scalar.activation(sg[:, b, n, :], bank[4 * b + n][:], ACT.Sigmoid).then_inc(sg_ready, 1)
                with act.Fori(0, KT // 2 - 1) as i:
                    for b in range(2):
                        act.wait_ge(piece_done, i * 2 + (NM + b + 1))
                        split(b, i * 16 + 8 * NM + 32)
                act.wait_ge(*V.after("sum1", n_loop - 1))
                for t in range(TT + 1):
                    if t < TT:
                        for half in range(2):
                            act.wait_ge(*E2.after(f"y{half}_{t}"))
                            nc.scalar.activation(tmp[:, t, half * 512:half * 512 + 512], bank[2 * t + half][:], ACT.Square,
                                                 accum_out=ss[:, t, half:half + 1]).then_inc(*A2.step(f"sq{half}_{t}"))
                        act.wait_ge(*V2.after(f"ss{t}"))
                        nc.scalar.activation(stat[:, 1, t:t + 1], stat[:, 0, t:t + 1], ACT.Sqrt, bias=eps[:], scale=1.0 / D).then_inc(*A2.step(f"std{t}"))
                    if t:
                        q = t - 1
                        act.wait_ge(*V2.after(f"x{q}"))
                        nc.scalar.activation(xn[:, q, :], x_tok[:, q, :], ACT.Square, accum_out=stat[:, 2, q:t]).then_inc(*A2.step(f"sqx{q}"))
                        act.wait_ge(*A2.after(f"sqx{q}"))
                        nc.scalar.activation(stat[:, 3, q:t], stat[:, 2, q:t], ACT.Sqrt, bias=eps[:], scale=1.0 / D).then_inc(*A2.step(f"std2_{q}"))

            @block.vector
            def _(dve):
                for n, (col, norm) in enumerate(((GT1, 1), (GT2, 3))):
                    if n:
                        dve.wait_ge(*E0.after("row1"))
                    nc.vector.tensor_tensor(gate[:, n, :], mod[:, col:col + KT], norms[:, norm, :], ALU.mult).then_inc(*V0.step(f"gate{n}"))
                    dve.wait_ge(*V0.after(f"gate{n}"))
                    nc.vector.tensor_tensor(diag[:], C["ident"].unsqueeze(1).to_broadcast([P, KT, P]),
                                            gate[:, n, :].unsqueeze(2).to_broadcast([P, KT, P]), ALU.mult).then_inc(*V0.step(f"diag{n}"))
                for n, x in enumerate((scT, oT)):
                    dve.wait_ge(br_ready, n + 1)
                    nc.vector.tensor_tensor(br_lo[:, n], x[:], br_hi[:, n].bitcast(F32), ALU.subtract).then_inc(*V0.step(f"br_lo{n}"))
                dve.wait_ge(*V0.after("br_lo1"))
                dve.sem_inc(sv, len(loop_v))
                with dve.Fori(0, n_loop) as i:
                    for b in range(2):
                        m = part[:, b, 0, :]
                        for n, x in enumerate(("sc", "dn")):
                            dve.wait_ge(sg_ready, i * 4 + (2 * b + n + 1))
                            dve.wait_ge(piece_done, i * 6 + (3 * b + 3))
                            nc.vector.tensor_tensor(part[:, b, n, :], sg[:, b, n, :], bank[4 * b + 2 + n][:], ALU.mult).then_inc(*V.step(f"{x}{b}"))
                        dve.wait_ge(*V.after(f"dn{b}", i))
                        nc.vector.tensor_tensor(m, m, part[:, b, 1, :], ALU.add).then_inc(*V.step(f"sum{b}"))
                        dve.wait_ge(*V.after(f"sum{b}", i))
                        hi = m_hi[:, bass.ds(i * 2 + b, 1), :].rearrange("p k t -> p (k t)")
                        nc.vector.tensor_copy(hi, m).then_inc(*V.step(f"hi{b}"))
                        dve.wait_ge(*V.after(f"hi{b}", i))
                        nc.vector.tensor_tensor(m_lo[:, bass.ds(i * 2 + b, 1), :].rearrange("p k t -> p (k t)"), m, hi.bitcast(F32),
                                                ALU.subtract).then_inc(*V.step(f"lo{b}"))
                for t in range(TT + 1):
                    if t < TT:
                        dve.wait_ge(*A2.after(f"sq1_{t}"))
                        nc.vector.tensor_tensor(stat[:, 0, t:t + 1], ss[:, t, 0:1], ss[:, t, 1:2], ALU.add).then_inc(*V2.step(f"ss{t}"))
                        dve.wait_ge(*A2.after(f"std{t}"))
                        nc.vector.reciprocal(stat[:, 0, t:t + 1], stat[:, 1, t:t + 1]).then_inc(*V2.step(f"rstd{t}"))
                        dve.wait_ge(*V2.after(f"rstd{t}"))
                        for half in range(2):
                            nc.vector.scalar_tensor_tensor(tmp[:, t, half * 512:half * 512 + 512], bank[2 * t + half][:], stat[:, 0, t:t + 1],
                                                           row_mix[:, half * 512:half * 512 + 512], ALU.mult, ALU.mult).then_inc(*V2.step(f"y{half}_{t}"))
                        dve.wait_ge(*V2.after(f"y1_{t}"))
                        nc.vector.tensor_tensor(x_tok[:, t, :], x_tok[:, t, :], tmp[:, t, :], ALU.add).then_inc(*V2.step(f"x{t}"))
                    if t:
                        dve.wait_ge(*A2.after(f"std2_{t - 1}"))
                        nc.vector.reciprocal(stat[:, 2, t - 1:t], stat[:, 3, t - 1:t]).then_inc(*V2.step(f"rstd2_{t - 1}"))


def retrieve_stage(nc, a, env, acts):
    g_ = env
    bank, C, mod, norms, stat, x_tok, h_hi, h_lo = (g_[n] for n in ("bank", "C", "mod", "norms", "stat", "x_tok", "h_hi", "h_lo"))
    idxT, gateT = g_["idxT"], g_["gateT"]
    sb, sem = g_["sb"], g_["sem"]
    K2 = TOPK * TOPK
    with ExitStack() as ctx:
        xn = sb(ctx, "xn2", [P, TT, D])
        h_raw = sb(ctx, "h_raw", [P, 2, T])
        scale2 = sb(ctx, "scale2", [P, KT])
        w = sb(ctx, "piece", [P, 2, KT, P])
        w_hi = sb(ctx, "piece_hi", [P, 2, KT, P], F32R)
        w_lo = sb(ctx, "piece_lo", [P, 2, KT, P], F32R)
        gel = sb(ctx, "gelu_early", [P, 2, T])
        keys = sb(ctx, "sub_keys", [P, 2 * PH, NKEYS])
        qT = sb(ctx, "queryT", [P, 2, T])
        s = sb(ctx, "scores", [P, 2, TT, NKEYS])
        v = sb(ctx, "top_half", [P, 2, TT, TOPK])
        iu = sb(ctx, "top_half_at", [P, 2, TT, TOPK], U32)
        fi = sb(ctx, "top_half_key", [P, 2, TT, TOPK])
        cand = sb(ctx, "candidates", [P, TT, K2])
        ts = sb(ctx, "top", [P, TT, TOPK])
        pos = sb(ctx, "top_at", [P, TT, TOPK], U32)
        ab = sb(ctx, "top_ab", [P, 2, TT, TOPK], U32)
        abf = sb(ctx, "top_ab_f", [P, 2, TT, TOPK])
        hot = sb(ctx, "rank_hot", [P, 2, TT, K2])
        score = sb(ctx, "top_all", [P, TT, PH, TOPK])
        sel = sb(ctx, "key_all", [P, 2, TT, PH, TOPK])
        gates = sb(ctx, "gates", [P, TT, PH, TOPK])
        gsum = sb(ctx, "gate_sum", [P, 2, TT, PH])
        s_w = [sem(ctx, f"piece_landed{i}") for i in range(2)]
        stored = [sem(ctx, f"gelu_stored{i}") for i in range(2)]
        hi_ready, lo_ready, piece_done, gelu_done = (sem(ctx, f"rt_{n}") for n in ("hi_ready", "lo_ready", "piece_done", "gelu_done"))
        NP = 2 + U_HEAD
        s_k = sem(ctx, "keys_landed")
        loop_e = ["s0", "s1"]
        loop_a = ["q0", "q1", "s0", "s1"]
        pre_e = [f"xT{k}" for k in range(KT)]
        pre_a = [x for k in range(KT) for x in (f"h{k}", f"hi{k}")]
        pre_v = ["scale_p", "scale2"] + [f"xn{t}" for t in range(TT)] + [f"lo{k}" for k in range(KT)]
        R4 = range(TT)
        loop_v = [f"{x}{p}{t}" for p in range(2) for x in ("max", "at", "rest", "max2_", "at2_") for t in R4]
        loop_v += ["key"] + [f"{x}{t}" for x in ("cand", "cmax", "cat", "crest", "cmax2_", "cat2_") for t in R4]
        loop_v += ["score", "shift", "mask", "ab_f", "hot0", "hot1", "pick0", "pick1", "sel0", "sel1"]
        se, sa, sv = (sem(ctx, f"rt_{n}") for n in ("tensor", "scalar", "vector"))
        E0, A0, V0 = Steps(se, pre_e), Steps(sa, pre_a), Steps(sv, pre_v)
        E, A = Steps(se, loop_e, len(pre_e)), Steps(sa, loop_a, len(pre_a))
        V = Steps(sv, loop_v, len(pre_v) + len(loop_v))
        post_v = ["gsub", "gsum", "grec", "gates", "idx0", "idx1", "gT"]
        V2 = Steps(sv, post_v, len(pre_v) + (1 + PH) * len(loop_v))
        A2 = Steps(sa, ["gexp"], len(pre_a) + PH * len(loop_a))
        E2 = Steps(se, ["idx0", "idx1", "gate"], len(pre_e) + PH * len(loop_e))
        held = sem(ctx, "rt_held")

        with nc.Block() as block:
            @block.sync
            def _(sp):
                def source(h, n):
                    return a["w_q"][h * 2 + n] if n < 2 else a["peer_u"][h * U_HEAD + (n - 2)]

                for n in range(2):
                    sp.dma_start(w[:, n], source(0, n)).then_inc(s_w[n], 16)
                sp.dma_start(keys[:], a["sub_keys"]).then_inc(s_k, 16)
                for n in range(2, NP):
                    sp.wait_ge(lo_ready, n - 1)
                    sp.dma_start(w[:, n % 2], source(0, n)).then_inc(s_w[n % 2], 16)
                with sp.Fori(1, PH) as h:
                    for n in range(NP):
                        sp.wait_ge(lo_ready, h * NP + (n - 1))
                        sp.dma_start(w[:, n % 2], source(h, n)).then_inc(s_w[n % 2], 16)
                for n in range(U_TAIL):
                    sp.wait_ge(lo_ready, PH * NP + n - 1)
                    sp.dma_start(w[:, n % 2], a["peer_u"][PH * U_HEAD + n]).then_inc(s_w[n % 2], 16)

            @block.tensor
            def _(pe):
                for k in range(KT):
                    if k == 0:
                        pe.wait_ge(*V0.after(f"xn{TT - 1}"))
                    for t in R4:
                        last = nc.tensor.transpose(bank[k][:, t * P:(t + 1) * P], xn[:, t, k * P:(k + 1) * P], C["ident"])
                    last.then_inc(*E0.step(f"xT{k}"))
                pe.wait_ge(s_k, 16)

                def product(h, n, out):
                    pe.wait_ge(lo_ready, h * NP + (n + 1))
                    for k in range(KT):
                        if n == 0:
                            pe.wait_ge(*V0.after(f"lo{k}"))
                        for m, (ww, x) in enumerate(((w_hi, h_hi), (w_hi, h_lo), (w_lo, h_hi))):
                            last = nc.tensor.matmul(out, ww[:, n % 2, k, :], x[:, k, :], start=(k == 0 and m == 0), stop=(k == KT - 1 and m == 2))
                    last.then_inc(piece_done, 1)

                def early(h, m):
                    pe.wait_ge(gelu_done, h * U_HEAD + (m + 1))
                    product(h, m + 2, bank[4 + m % 2][:])

                with pe.Fori(0, PH) as h:
                    for p in range(2):
                        product(h, p, bank[p][:])
                    early(h, 0)
                    for p in range(2):
                        pe.wait_ge(*A.after(f"q{p}", h))
                        for t in R4:
                            last = nc.tensor.matmul(bank[2 + p][:, t * P:(t + 1) * P], qT[:, p, t * P:(t + 1) * P], keys[:, 2 * h + p, :], start=True, stop=True)
                        last.then_inc(*E.step(f"s{p}"))
                    for m in range(1, U_HEAD):
                        early(h, m)
                for m in range(U_TAIL):
                    pe.wait_ge(gelu_done, PH * U_HEAD + m + 1)
                    product(PH, m, bank[4 + m % 2][:])
                for n in range(3):
                    pe.wait_ge(*(V.after("sel1", PH - 1) if n < 2 else V2.after("gates")))
                    for t in R4:
                        src = (sel[:, n, t] if n < 2 else gates[:, t]).rearrange("p h k -> p (h k)")
                        last = nc.tensor.transpose(bank[n][:, t * P:(t + 1) * P], src, C["ident"])
                    last.then_inc(*E2.step(("idx0", "idx1", "gate")[n]))

            @block.scalar
            def _(act):
                act.sem_inc(gelu_done, 2)
                for q in stored:
                    act.sem_inc(q, 16)

                def split(slot, landed):
                    act.wait_ge(s_w[slot], landed)
                    nc.scalar.activation(w_hi[:, slot], w[:, slot], ACT.Copy).then_inc(hi_ready, 1)

                for n in range(2):
                    split(n, 16)
                act.wait_ge(*V0.after("scale2"))
                for k in range(KT):
                    act.wait_ge(*E0.after(f"xT{k}"))
                    if k >= 2:
                        act.wait_ge(*V0.after(f"lo{k - 2}"))
                    nc.scalar.activation(h_raw[:, k % 2], bank[k][:], ACT.Identity, bias=mod[:, SH2 + k:SH2 + k + 1],
                                         scale=scale2[:, k:k + 1]).then_inc(*A0.step(f"h{k}"))
                    act.wait_ge(*A0.after(f"h{k}"))
                    nc.scalar.activation(h_hi[:, k, :], h_raw[:, k % 2], ACT.Copy).then_inc(*A0.step(f"hi{k}"))

                def early(h, m):
                    act.wait_ge(stored[m % 2], h * (8 * U_HEAD) + (16 * (m // 2) + 16))
                    nc.scalar.activation(gel[:, m % 2, :], bank[4 + m % 2][:], ACT.Gelu).then_inc(gelu_done, 1)
                    act.wait_ge(gelu_done, h * U_HEAD + (m + 3))
                    act.dma_start(acts[h * U_HEAD + m], gel[:, m % 2, :]).then_inc(stored[m % 2], 16)

                with act.Fori(0, PH) as h:
                    for n in range(NP):
                        act.wait_ge(piece_done, h * NP + (n + 1))
                        split(n % 2, h * (8 * NP) + (16 * (n // 2) + 32))
                        if n < 2:
                            nc.scalar.activation(qT[:, n, :], bank[n][:], ACT.Copy).then_inc(*A.step(f"q{n}"))
                        else:
                            early(h, n - 2)
                        if n == 2:
                            for p in range(2):
                                act.wait_ge(*V.after(f"at2_{p}{TT - 1}", h, 1))
                                act.wait_ge(*E.after(f"s{p}", h))
                                nc.scalar.activation(s[:, p].rearrange("p t n -> p (t n)"), bank[2 + p][:], ACT.Copy).then_inc(*A.step(f"s{p}"))
                for m in range(U_TAIL):
                    act.wait_ge(piece_done, PH * NP + m + 1)
                    if m + 2 < U_TAIL:
                        split(m % 2, 8 * PH * NP + 16 * (m // 2) + 32)
                    if m == U_TAIL - 2:
                        act.wait_ge(*V2.after("gsub"))
                        nc.scalar.activation(gates[:], gates[:], ACT.Exp).then_inc(*A2.step("gexp"))
                    early(PH, m)
                for q in stored:
                    act.wait_ge(q, 8 * N_RETR + 16)

            @block.gpsimd
            def _(pool):
                def rest(slot, count):
                    pool.wait_ge(hi_ready, count)
                    nc.gpsimd.tensor_tensor(w_lo[:, slot], w[:, slot], w_hi[:, slot].bitcast(F32), ALU.subtract).then_inc(lo_ready, 1)

                with pool.Fori(0, (PH * NP + U_TAIL) // 2) as i:
                    for n in range(2):
                        rest(n, i * 2 + (n + 1))

            @block.vector
            def _(dve):
                nc.vector.tensor_scalar(scale2[:], mod[:, SC2:SC2 + KT], 1.0, None, ALU.add).then_inc(*V0.step("scale_p"))
                dve.wait_ge(*V0.after("scale_p"))
                nc.vector.tensor_tensor(scale2[:], scale2[:], norms[:, 2, :], ALU.mult).then_inc(*V0.step("scale2"))
                for t in R4:
                    nc.vector.tensor_scalar(xn[:, t, :], x_tok[:, t, :], stat[:, 2, t:t + 1], None, ALU.mult).then_inc(*V0.step(f"xn{t}"))
                for k in range(KT):
                    dve.wait_ge(*A0.after(f"hi{k}"))
                    nc.vector.tensor_tensor(h_lo[:, k, :], h_raw[:, k % 2], h_hi[:, k, :].bitcast(F32), ALU.subtract).then_inc(*V0.step(f"lo{k}"))
                dve.wait_ge(*V0.after(f"lo{KT - 1}"))
                dve.sem_inc(sv, len(loop_v))
                with dve.Fori(0, PH) as h:
                    VA = lambda n: V.after(n, h)

                    def ready(*w):
                        for x in w:
                            dve.wait_ge(*x)
                        dve.sem_inc(held, 1)

                    for p in range(2):
                        ready(A.after(f"s{p}", h))
                        for t in R4:
                            nc.vector.max(v[:, p, t, 0:8], s[:, p, t]).then_inc(*V.step(f"max{p}{t}"))
                        ready(VA(f"max{p}{TT - 1}"))
                        for t in R4:
                            nc.vector.max_index(iu[:, p, t, 0:8], v[:, p, t, 0:8], s[:, p, t]).then_inc(*V.step(f"at{p}{t}"))
                        for t in R4:
                            nc.vector.match_replace(s[:, p, t], v[:, p, t, 0:8], s[:, p, t], -3e38).then_inc(*V.step(f"rest{p}{t}"))
                        ready(VA(f"rest{p}{TT - 1}"))
                        for t in R4:
                            nc.vector.max(v[:, p, t, 8:16], s[:, p, t]).then_inc(*V.step(f"max2_{p}{t}"))
                        ready(VA(f"max2_{p}{TT - 1}"))
                        for t in R4:
                            nc.vector.max_index(iu[:, p, t, 8:16], v[:, p, t, 8:16], s[:, p, t]).then_inc(*V.step(f"at2_{p}{t}"))
                    dve.wait_ge(*VA(f"at2_1{TT - 1}"))
                    nc.vector.tensor_copy(fi[:], iu[:]).then_inc(*V.step("key"))
                    for t in R4:
                        nc.vector.tensor_tensor(cand[:, t].rearrange("p (x y) -> p x y", x=TOPK), v[:, 0, t].unsqueeze(2).to_broadcast([P, TOPK, TOPK]),
                                                v[:, 1, t].unsqueeze(1).to_broadcast([P, TOPK, TOPK]), ALU.add).then_inc(*V.step(f"cand{t}"))
                    ready(VA(f"cand{TT - 1}"))
                    for t in R4:
                        nc.vector.max(ts[:, t, 0:8], cand[:, t]).then_inc(*V.step(f"cmax{t}"))
                    ready(VA(f"cmax{TT - 1}"))
                    for t in R4:
                        nc.vector.max_index(pos[:, t, 0:8], ts[:, t, 0:8], cand[:, t]).then_inc(*V.step(f"cat{t}"))
                    for t in R4:
                        nc.vector.match_replace(cand[:, t], ts[:, t, 0:8], cand[:, t], -3e38).then_inc(*V.step(f"crest{t}"))
                    ready(VA(f"crest{TT - 1}"))
                    for t in R4:
                        nc.vector.max(ts[:, t, 8:16], cand[:, t]).then_inc(*V.step(f"cmax2_{t}"))
                    ready(VA(f"cmax2_{TT - 1}"))
                    for t in R4:
                        nc.vector.max_index(pos[:, t, 8:16], ts[:, t, 8:16], cand[:, t]).then_inc(*V.step(f"cat2_{t}"))
                    nc.vector.tensor_copy(score[:, :, h, :], ts[:]).then_inc(*V.step("score"))
                    dve.wait_ge(*VA(f"cat2_{TT - 1}"))
                    nc.vector.tensor_scalar(ab[:, 0], pos[:], 4, None, ALU.logical_shift_right).then_inc(*V.step("shift"))
                    nc.vector.tensor_scalar(ab[:, 1], pos[:], TOPK - 1, None, ALU.bitwise_and).then_inc(*V.step("mask"))
                    dve.wait_ge(*VA("mask"))
                    nc.vector.tensor_copy(abf[:], ab[:]).then_inc(*V.step("ab_f"))
                    dve.wait_ge(*VA("ab_f"))
                    for n in range(2):
                        nc.vector.tensor_tensor(hot[:, n].rearrange("p t (k r) -> p (t k) r", r=TOPK),
                                                abf[:, n].rearrange("p t k -> p (t k)").unsqueeze(2).to_broadcast([P, TT * TOPK, TOPK]),
                                                C["iota"][:, 0:TOPK].unsqueeze(1).to_broadcast([P, TT * TOPK, TOPK]), ALU.is_equal).then_inc(*V.step(f"hot{n}"))
                    by_rank = lambda x: x.rearrange("p t (k r) -> p t k r", r=TOPK)
                    for n in range(2):
                        dve.wait_ge(*VA(f"hot{n}"))
                        nc.vector.tensor_tensor(by_rank(hot[:, n]), by_rank(hot[:, n]), fi[:, n].unsqueeze(2).to_broadcast([P, TT, TOPK, TOPK]),
                                                ALU.mult).then_inc(*V.step(f"pick{n}"))
                    for n in range(2):
                        dve.wait_ge(*VA(f"pick{n}"))
                        nc.vector.tensor_reduce(sel[:, n, :, h, :], by_rank(hot[:, n]), AX.X, ALU.add).then_inc(*V.step(f"sel{n}"))
                dve.wait_ge(*V.after("sel1", PH - 1))
                th = lambda x: x.rearrange("p t h k -> p (t h) k")
                nc.vector.tensor_tensor(th(gates[:]), th(score[:]), th(score[:])[:, :, 0:1].to_broadcast([P, TT * PH, TOPK]), ALU.subtract).then_inc(*V2.step("gsub"))
                dve.wait_ge(*A2.after("gexp"))
                nc.vector.tensor_reduce(gsum[:, 0].rearrange("p t h -> p (t h)"), th(gates[:]), AX.X, ALU.add).then_inc(*V2.step("gsum"))
                dve.wait_ge(*V2.after("gsum"))
                nc.vector.reciprocal(gsum[:, 1], gsum[:, 0]).then_inc(*V2.step("grec"))
                dve.wait_ge(*V2.after("grec"))
                nc.vector.tensor_tensor(th(gates[:]), th(gates[:]), gsum[:, 1].rearrange("p t h -> p (t h)").unsqueeze(2).to_broadcast([P, TT * PH, TOPK]),
                                        ALU.mult).then_inc(*V2.step("gates"))
                for n in range(2):
                    dve.wait_ge(*E2.after(f"idx{n}"))
                    nc.vector.tensor_copy(idxT[:, n, :], bank[n][:]).then_inc(*V2.step(f"idx{n}"))
                dve.wait_ge(*E2.after("gate"))
                nc.vector.tensor_copy(gateT[:], bank[2][:]).then_inc(*V2.step("gT"))


def scatter_stage(nc, a, env, spill, acts):
    g_ = env
    bank, C, idxT, gateT, h_hi, h_lo = (g_[n] for n in ("bank", "C", "idxT", "gateT", "h_hi", "h_lo"))
    sb, sem = g_["sb"], g_["sem"]
    UT = 8
    UB, SLOTS = TB // UT, 2
    NU = UB * SLOTS
    NR = T // (NU * UT)
    R = 4
    with ExitStack() as ctx:
        hot1 = sb(ctx, "hot_i1", [P, R, UT, P])
        hot2 = sb(ctx, "gated_i2", [P, R, UT, P])
        block_g = sb(ctx, "gate_block", [P, SLOTS, P, TB])
        w = sb(ctx, "u_early", [P, 2, KT, P])
        w_hi = sb(ctx, "u_early_hi", [P, 2, KT, P], F32R)
        w_lo = sb(ctx, "u_early_lo", [P, 2, KT, P], F32R)
        gel = sb(ctx, "gelu_early2", [P, 2, T])
        s_w = [sem(ctx, f"u_early_landed{i}") for i in range(2)]
        s_gel = [sem(ctx, f"gelu2_stored{i}") for i in range(2)]
        hi_ready, lo_ready, piece_done, gelu_done = (sem(ctx, f"sc_{n}") for n in ("hi_ready", "lo_ready", "piece_done", "gelu_done"))
        units = [f"unit{u}" for u in range(NU)]
        sv, se, sa = (sem(ctx, n) for n in ("hot_ready", "dense", "copied"))
        stored = [sem(ctx, f"stored{i}") for i in range(SLOTS)]
        V, E, A = Steps(sv, units), Steps(se, units, NU), Steps(sa, units, NU)

        with nc.Block() as block:
            @block.vector
            def _(dve):
                with dve.Fori(0, NR) as i:
                    for u in range(NU):
                        dve.wait_ge(*(E.after(f"unit{u - R}", i) if u >= R else E.after(f"unit{NU + u - R}", i, 1)))
                        nc.vector.tensor_tensor(hot1[:, u % R], C["iota"].unsqueeze(1).to_broadcast([P, UT, P]),
                                                idxT[:, 0, bass.ds(i * (NU * UT) + u * UT, UT)].unsqueeze(2).to_broadcast([P, UT, P]), ALU.is_equal)
                        for t in range(UT):
                            at = bass.ds(i * (NU * UT) + (u * UT + t), 1)
                            last = nc.vector.tensor_scalar(hot2[:, u % R, t, :], C["iota"], idxT[:, 1, at], gateT[:, at], ALU.is_equal, ALU.mult)
                        last.then_inc(*V.step(f"unit{u}"))

            @block.gpsimd
            def _(pool):
                pool.sem_inc(se, NU)
                pool.sem_inc(sa, NU)
                for s in stored + s_gel:
                    pool.sem_inc(s, 16)
                pool.sem_inc(gelu_done, SLOTS)
                with pool.Fori(0, NR + S_TAIL // SLOTS) as i:
                    for b in range(SLOTS):
                        pool.wait_ge(hi_ready, i * SLOTS + (b + 1))
                        nc.gpsimd.tensor_tensor(w_lo[:, b], w[:, b], w_hi[:, b].bitcast(F32), ALU.subtract).then_inc(lo_ready, 1)

            @block.tensor
            def _(pe):
                def early(i, b):
                    pe.wait_ge(lo_ready, i * SLOTS + (b + 1))
                    pe.wait_ge(gelu_done, i * SLOTS + (b + 1))
                    for k in range(KT):
                        for m, (ww, x) in enumerate(((w_hi, h_hi), (w_hi, h_lo), (w_lo, h_hi))):
                            last = nc.tensor.matmul(bank[4 + b][:], ww[:, b, k, :], x[:, k, :], start=(k == 0 and m == 0), stop=(k == KT - 1 and m == 2))
                    last.then_inc(piece_done, 1)

                with pe.Fori(0, NR) as i:
                    for u in range(NU):
                        pe.wait_ge(*(A.after(f"unit{u - 2}", i) if u >= 2 else A.after(f"unit{NU + u - 2}", i, 1)))
                        pe.wait_ge(*V.after(f"unit{u}", i))
                        for t in range(UT):
                            last = nc.tensor.matmul(bank[2 * (u % 2) + t // 4][:, t % 4 * P:(t % 4 + 1) * P], hot1[:, u % R, t, :], hot2[:, u % R, t, :],
                                                    start=True, stop=True)
                        last.then_inc(*E.step(f"unit{u}"))
                        if u % UB == UB - 1:
                            early(i, u // UB)
                for m in range(S_TAIL):
                    early(NR + m // SLOTS, m % SLOTS)

            @block.scalar
            def _(act):
                def split(i, b):
                    act.wait_ge(s_w[b], i * 16 + 16)
                    nc.scalar.activation(w_hi[:, b], w[:, b], ACT.Copy).then_inc(hi_ready, 1)

                def early(i, b, more):
                    act.wait_ge(piece_done, i * SLOTS + (b + 1))
                    if more:
                        split(i + 1, b)
                    act.wait_ge(s_gel[b], i * 16 + 16)
                    nc.scalar.activation(gel[:, b, :], bank[4 + b][:], ACT.Gelu).then_inc(gelu_done, 1)
                    act.wait_ge(gelu_done, i * SLOTS + (b + 1 + SLOTS))
                    act.dma_start(acts[i * SLOTS + (N_RETR + b)], gel[:, b, :]).then_inc(s_gel[b], 16)

                for b in range(SLOTS):
                    split(0, b)
                with act.Fori(0, NR) as i:
                    for u in range(NU):
                        slot = u // UB
                        if u % UB == 0:
                            act.wait_ge(stored[slot], i * 16 + 16)
                        act.wait_ge(*E.after(f"unit{u}", i))
                        for b in range(2):
                            t = u % UB * UT + 4 * b
                            last = nc.scalar.activation(block_g[:, slot, :, t:t + 4], bank[2 * (u % 2) + b][:].rearrange("p (t n) -> p n t", t=4), ACT.Copy)
                        last.then_inc(*A.step(f"unit{u}"))
                        if u % UB == UB - 1:
                            early(i, slot, True)
                for m in range(S_TAIL):
                    early(NR + m // SLOTS, m % SLOTS, m + SLOTS < S_TAIL)
                for s in s_gel:
                    act.wait_ge(s, 16 * (NR + S_TAIL // SLOTS + 1))

            @block.sync
            def _(sp):
                for b in range(SLOTS):
                    sp.dma_start(w[:, b], a["peer_u"][N_RETR + b]).then_inc(s_w[b], 16)
                with sp.Fori(0, NR) as i:
                    for slot in range(SLOTS):
                        sp.wait_ge(lo_ready, i * SLOTS + (slot + 1))
                        sp.dma_start(w[:, slot], a["peer_u"][i * SLOTS + (N_RETR + SLOTS + slot)]).then_inc(s_w[slot], 16)
                        sp.wait_ge(*A.after(f"unit{slot * UB + UB - 1}", i))
                        sp.dma_start(spill[:, bass.ds(i * SLOTS + slot, 1)], block_g[:, slot:slot + 1]).then_inc(stored[slot], 16)
                for m in range(SLOTS, S_TAIL):
                    sp.wait_ge(lo_ready, NR * SLOTS + m - SLOTS + 1)
                    sp.dma_start(w[:, m % SLOTS], a["peer_u"][N_RETR + NR * SLOTS + m]).then_inc(s_w[m % SLOTS], 16)
                for s in stored:
                    sp.wait_ge(s, 16 * (NR + 1))


def expert_stage(nc, a, env, spill, acts, out):
    g_ = env
    bank, eps, x_tok, h_hi, h_lo, row_ffn = (g_[n] for n in ("bank", "eps", "x_tok", "h_hi", "h_lo", "row_ffn"))
    sb, sem = g_["sb"], g_["sem"]
    GE = 4
    NG1 = N_EARLY // GE
    NGRP = EXP_TILES // GE - NG1
    with ExitStack() as ctx:
        ut = sb(ctx, "u_tile", [P, 2, KT, P])
        u_hi = sb(ctx, "u_hi", [P, 2, KT, P], F32R)
        u_lo = sb(ctx, "u_lo", [P, 2, KT, P], F32R)
        vt = sb(ctx, "v_tile", [P, GE, D])
        v_hi = sb(ctx, "v_hi", [P, GE, D], F32R)
        v_lo = sb(ctx, "v_lo", [P, GE, D], F32R)
        gt = sb(ctx, "gate_tiles", [P, T // TB, GE, TB])
        gel = sb(ctx, "gelu", [P, GE, T])
        coef = sb(ctx, "coef", [P, 2, T])
        c_hi = sb(ctx, "coef_hi", [P, GE, T], F32R)
        c_lo = sb(ctx, "coef_lo", [P, GE, T], F32R)
        y = sb(ctx, "y", [P, TT, D])
        ss = sb(ctx, "y_sq", [P, 4, TT])
        s_u = [sem(ctx, f"u_landed{i}") for i in range(2)]
        s_v = [sem(ctx, f"v_landed{i}") for i in range(GE)]
        s_g, s_g0 = sem(ctx, "gates_landed"), sem(ctx, "first_gates_landed")
        s_gel = [sem(ctx, f"gelu_landed{i}") for i in range(GE)]
        early_e = [f"y0{t}" for t in range(TT)] + [f"half1_{e}" for e in range(GE - 1)] + [f"y1{t}" for t in range(TT)]
        early_a = [f"hi_{x}{e}" for e in range(GE) for x in "vc"]
        prep = [[f"coef{e}", f"lo_c{e}"] for e in range(GE)]
        early_v = sum(prep[:-1], []) + [f"add1{t}" for t in range(TT)] + prep[-1] + [f"add0{t}" for t in range(TT)]
        be, ba, bv = (sem(ctx, f"ex0_{n}") for n in ("tensor", "scalar", "vector"))
        v_lo_ready = sem(ctx, "v_lo_ready")
        L_E, L_V = len(early_e), len(early_v)
        E1, A1, V1 = Steps(be, early_e, L_E), Steps(ba, early_a), Steps(bv, early_v, L_V)
        zeroed, stored = sem(ctx, "y_zeroed"), sem(ctx, "out_stored")
        loop_e = [f"u{e}" for e in range(GE)] + [f"y{half}{t}" for half in range(2) for t in range(TT)]
        order = ["v0", "v1", "u2", "c0", "v2", "u3", "c1", "v3", "c2", "c3", "u0", "u1"]
        loop_a = [x for n in order for x in ([f"gelu{n[1]}", f"hi_c{n[1]}"] if n[0] == "c" else [f"hi_{n}"])]
        loop_v = [x for n in order for x in ([f"coef{n[1]}", f"lo_c{n[1]}"] if n[0] == "c" else [f"lo_{n}"])]
        adds = [f"add{half}{t}" for half in range(2) for t in range(TT)]
        loop_v += adds
        se, sa, sv = (sem(ctx, f"ex_{n}") for n in ("tensor", "scalar", "vector"))
        E, A, V = Steps(se, loop_e, len(loop_e)), Steps(sa, loop_a, len(loop_a)), Steps(sv, loop_v, len(loop_v))
        A2 = Steps(sa, [f"sq{half}{t}" for half in range(2) for t in range(TT)] + ["std"], (1 + NGRP) * len(loop_a))
        V2 = Steps(sv, ["row0", "row1", "ss", "row2", "row3", "rstd"] + [f"out{t}" for t in range(TT)], (1 + NGRP) * len(loop_v))
        lower_row = sem(ctx, "y_lower_row")
        a_banks, y_banks = (2, 3, 4, 5), ((2, 3, 4, 5), (6, 7, 0, 1))

        with nc.Block() as block:
            def u_split(S, part, e, i):
                return S.after(f"{part}_u{e}", i, 1 if e < 2 else 0)

            @block.sync
            def _(sp):
                for e in range(GE):
                    sp.dma_start(vt[:, e], a["peer_v"][e]).then_inc(s_v[e], 16)
                    sp.dma_start(gel[:, e, :], acts[e]).then_inc(s_gel[e], 16)
                    if e < 2:
                        part = slice(e, e + 1 if e == 0 else GE)
                        sp.dma_start(gt[:, :, part, :], spill[:, :, part, :]).then_inc(s_g if e else s_g0, 16)
                with sp.Fori(1, NG1) as i:
                    for e in range(GE):
                        sp.wait_ge(v_lo_ready, i * GE + (e + 1 - GE))
                        sp.dma_start(vt[:, e], a["peer_v"][i * GE + e]).then_inc(s_v[e], 16)
                        sp.wait_ge(*V1.after(f"coef{e}", i, 1))
                        sp.dma_start(gel[:, e, :], acts[i * GE + e]).then_inc(s_gel[e], 16)
                    sp.dma_start(gt[:], spill[:, :, bass.ds(i * GE, GE), :]).then_inc(s_g, 16)

                for n in range(2):
                    sp.dma_start(ut[:, n], a["peer_u"][N_EARLY + n]).then_inc(s_u[n], 16)
                with sp.Fori(0, NGRP) as i:
                    sp.wait_ge(*V.after(f"coef{GE - 1}", i, 1))
                    sp.dma_start(gt[:], spill[:, :, bass.ds(i * GE + N_EARLY, GE), :]).then_inc(s_g, 16)
                    for e in range(GE):
                        sp.wait_ge(*V.after(f"lo_v{e}", i, 1))
                        sp.dma_start(vt[:, e], a["peer_v"][i * GE + (N_EARLY + e)]).then_inc(s_v[e], 16)
                        sp.wait_ge(*u_split(V, "lo", e, i))
                        sp.dma_start(ut[:, e % 2], a["peer_u"][(i * GE + (N_EARLY + e + 2)) % EXP_TILES]).then_inc(s_u[e % 2], 16)

            @block.tensor
            def _(pe):
                def y_products(half, e, t):
                    c = slice(half * 512, half * 512 + 512)
                    for n, (w, x) in enumerate(((c_hi, v_hi), (c_hi, v_lo), (c_lo, v_hi))):
                        last = nc.tensor.matmul(bank[y_banks[half][t]][:], w[:, e, t * P:(t + 1) * P], x[:, e, c],
                                                start=(e == 0 and n == 0), stop=(e == GE - 1 and n == 2))
                    return last

                with pe.Fori(0, NG1) as i:
                    for half in range(2):
                        for e in range(GE):
                            if half == 0:
                                pe.wait_ge(v_lo_ready, i * GE + (e + 1))
                                pe.wait_ge(*V1.after(f"lo_c{e}", i))
                            for t in range(TT):
                                if e == 0:
                                    pe.wait_ge(*(V1.after(f"add0{t}", i, 1) if half == 0 else V1.after(f"add1{t}", i)))
                                last = y_products(half, e, t)
                                if e == GE - 1:
                                    last.then_inc(*E1.step(f"y{half}{t}"))
                            if half == 1 and e < GE - 1:
                                last.then_inc(*E1.step(f"half1_{e}"))

                with pe.Fori(0, NGRP) as i:
                    for e in range(GE):
                        pe.wait_ge(*u_split(V, "lo", e, i))
                        pe.wait_ge(*V.after(f"add0{e}", i, 1))
                        for k in range(KT):
                            for n, (w, x) in enumerate(((u_hi, h_hi), (u_hi, h_lo), (u_lo, h_hi))):
                                last = nc.tensor.matmul(bank[a_banks[e]][:], w[:, e % 2, k, :], x[:, k, :], start=(k == 0 and n == 0), stop=(k == KT - 1 and n == 2))
                        last.then_inc(*E.step(f"u{e}"))
                    for half in range(2):
                        for e in range(GE):
                            if half == 0:
                                pe.wait_ge(*V.after(f"lo_v{e}", i))
                                pe.wait_ge(*V.after(f"lo_c{e}", i))
                            for t in range(TT):
                                if e == 0:
                                    pe.wait_ge(*(A.after(f"gelu{t}", i) if half == 0 else V.after(f"add1{t}", i, 1)))
                                last = y_products(half, e, t)
                                if e == GE - 1:
                                    last.then_inc(*E.step(f"y{half}{t}"))

            @block.gpsimd
            def _(pool):
                pool.sem_inc(be, L_E)
                with pool.Fori(0, NG1) as i:
                    for e in range(GE):
                        pool.wait_ge(*A1.after(f"hi_v{e}", i))
                        nc.gpsimd.tensor_tensor(v_lo[:, e], vt[:, e], v_hi[:, e].bitcast(F32), ALU.subtract).then_inc(v_lo_ready, 1)
                for t in range(TT):
                    pool.wait_ge(*A2.after(f"sq0{t}"))
                    nc.gpsimd.tensor_tensor(y[:, t, 0:512], y[:, t, 0:512], row_ffn[:, 0:512], ALU.mult).then_inc(lower_row, 1)

            @block.scalar
            def _(act):
                with act.Fori(0, NG1) as i:
                    for e in range(GE):
                        act.wait_ge(s_v[e], i * 16 + 16)
                        act.wait_ge(*E1.after(f"half1_{e}" if e < GE - 1 else f"y1{TT - 1}", i, 1))
                        nc.scalar.activation(v_hi[:, e], vt[:, e], ACT.Copy).then_inc(*A1.step(f"hi_v{e}"))
                        act.wait_ge(*V1.after(f"coef{e}", i))
                        nc.scalar.activation(c_hi[:, e], coef[:, e % 2], ACT.Copy).then_inc(*A1.step(f"hi_c{e}"))

                act.sem_inc(sa, len(loop_a) - 2)
                A.n = len(loop_a) - 2
                for e in range(2):
                    act.wait_ge(s_u[e], 16)
                    nc.scalar.activation(u_hi[:, e], ut[:, e], ACT.Copy).then_inc(*A.step(f"hi_u{e}"))
                with act.Fori(0, NGRP) as i:
                    for n in order:
                        e = int(n[1])
                        if n[0] == "v":
                            act.wait_ge(s_v[e], i * 16 + 16 * (NG1 + 1))
                            act.wait_ge(*E.after(f"y1{TT - 1}", i, 1))
                            nc.scalar.activation(v_hi[:, e], vt[:, e], ACT.Copy).then_inc(*A.step(f"hi_v{e}"))
                        elif n[0] == "u":
                            act.wait_ge(s_u[e % 2], i * 32 + (32 if e >= 2 else 48))
                            act.wait_ge(*E.after(f"u{e ^ 2}", i))
                            nc.scalar.activation(u_hi[:, e % 2], ut[:, e % 2], ACT.Copy).then_inc(*A.step(f"hi_u{e}"))
                        else:
                            act.wait_ge(*V.after(f"coef{e}", i, 1))
                            act.wait_ge(*E.after(f"u{e}", i))
                            nc.scalar.activation(gel[:, e, :], bank[a_banks[e]][:], ACT.Gelu).then_inc(*A.step(f"gelu{e}"))
                            act.wait_ge(*V.after(f"coef{e}", i))
                            nc.scalar.activation(c_hi[:, e], coef[:, e % 2], ACT.Copy).then_inc(*A.step(f"hi_c{e}"))
                for half in range(2):
                    for t in range(TT):
                        act.wait_ge(*V.after(f"add{half}{t}", NGRP - 1))
                        nc.scalar.activation(gel[:, t, :], y[:, t, half * 512:half * 512 + 512], ACT.Square,
                                             accum_out=ss[:, half, t:t + 1]).then_inc(*A2.step(f"sq{half}{t}"))
                        act.wait_ge(*A2.after(f"sq{half}{t}"))
                act.wait_ge(*V2.after("ss"))
                nc.scalar.activation(ss[:, 3, :], ss[:, 2, :], ACT.Sqrt, bias=eps[:], scale=1.0 / D).then_inc(*A2.step("std"))
                for t in range(TT):
                    act.wait_ge(*V2.after(f"out{t}"))
                    act.dma_start(out[t * P:(t + 1) * P, :], y[:, t, :]).then_inc(stored, 16)
                act.wait_ge(stored, 16 * TT)

            @block.vector
            def _(dve):
                def rest(dst, src, hi):
                    return nc.vector.tensor_tensor(dst, src, hi.bitcast(F32), ALU.subtract)

                by_block = lambda x: x.rearrange("p (b t) -> p b t", t=TB)

                def coefficients(e):
                    return nc.vector.tensor_tensor(by_block(coef[:, e % 2]), by_block(gel[:, e]), gt[:, :, e, :], ALU.mult)

                def add(half, t):
                    c = slice(half * 512, half * 512 + 512)
                    return nc.vector.tensor_tensor(y[:, t, c], y[:, t, c], bank[y_banks[half][t]][:], ALU.add)

                def early_group(i, first=False):
                    for e in range(GE):
                        if e == GE - 1:
                            if first:
                                dve.wait_ge(*V1.after(f"lo_c{e - 1}", 0))
                                V1.n += TT
                                dve.sem_inc(bv, TT)
                            else:
                                early_adds(i, 1)
                        if first and e == 0:
                            dve.wait_ge(s_g0, 16)
                        elif e == (1 if first else 0):
                            dve.wait_ge(s_g, i * 16 + 16)
                        dve.wait_ge(s_gel[e], i * 16 + 16)
                        coefficients(e).then_inc(*V1.step(f"coef{e}"))
                        dve.wait_ge(*A1.after(f"hi_c{e}", i))
                        rest(c_lo[:, e], coef[:, e % 2], c_hi[:, e]).then_inc(*V1.step(f"lo_c{e}"))
                    early_adds(i, 0)

                def early_adds(i, half):
                    for t in range(TT):
                        dve.wait_ge(*(E1.after(f"y0{t}", i) if half == 0 else E1.after(f"y1{t}", i, 1)))
                        add(half, t).then_inc(*V1.step(f"add{half}{t}"))

                nc.vector.memset(y[:], 0.0).then_inc(zeroed, 1)
                dve.sem_inc(bv, L_V)
                dve.wait_ge(zeroed, 1)
                early_group(0, first=True)
                with dve.Fori(1, NG1) as i:
                    early_group(i)

                dve.wait_ge(*V1.after(f"add0{TT - 1}", NG1 - 1))
                dve.wait_ge(v_lo_ready, NG1 * GE)
                V.n = loop_v.index("lo_u0")
                dve.sem_inc(sv, V.n)
                for e in range(2):
                    dve.wait_ge(*u_split(A, "hi", e, 0))
                    rest(u_lo[:, e], ut[:, e], u_hi[:, e]).then_inc(*V.step(f"lo_u{e}"))
                V1.n += (GE - 1) * 2
                dve.sem_inc(bv, (GE - 1) * 2)
                early_adds(NG1, 1)
                dve.wait_ge(*u_split(V, "lo", 1, 0))
                dve.wait_ge(*V1.after(f"add1{TT - 1}", NG1))
                dve.sem_inc(se, len(loop_e))
                V.n += len(adds)
                dve.sem_inc(sv, len(adds))
                with dve.Fori(0, NGRP) as i:
                    for n in order:
                        e = int(n[1])
                        if n[0] == "v":
                            dve.wait_ge(*A.after(f"hi_v{e}", i))
                            rest(v_lo[:, e], vt[:, e], v_hi[:, e]).then_inc(*V.step(f"lo_v{e}"))
                        elif n[0] == "u":
                            dve.wait_ge(*A.after(f"hi_u{e}", i))
                            rest(u_lo[:, e % 2], ut[:, e % 2], u_hi[:, e % 2]).then_inc(*V.step(f"lo_u{e}"))
                        else:
                            if e == 0:
                                dve.wait_ge(s_g, i * 16 + 16 * (NG1 + 1))
                            dve.wait_ge(*A.after(f"gelu{e}", i))
                            coefficients(e).then_inc(*V.step(f"coef{e}"))
                            dve.wait_ge(*A.after(f"hi_c{e}", i))
                            rest(c_lo[:, e], coef[:, e % 2], c_hi[:, e]).then_inc(*V.step(f"lo_c{e}"))
                    for half in range(2):
                        for t in range(TT):
                            dve.wait_ge(*E.after(f"y{half}{t}", i))
                            add(half, t).then_inc(*V.step(f"add{half}{t}"))
                def by_row(t):
                    dve.wait_ge(*A2.after(f"sq1{t}"))
                    nc.vector.tensor_tensor(y[:, t, 512:D], y[:, t, 512:D], row_ffn[:, 512:D], ALU.mult).then_inc(*V2.step(f"row{t}"))

                for t in range(2):
                    by_row(t)
                dve.wait_ge(*A2.after(f"sq1{TT - 1}"))
                nc.vector.tensor_tensor(ss[:, 2, :], ss[:, 0, :], ss[:, 1, :], ALU.add).then_inc(*V2.step("ss"))
                for t in range(2, TT):
                    by_row(t)
                dve.wait_ge(*A2.after("std"))
                nc.vector.reciprocal(ss[:, 0, :], ss[:, 3, :]).then_inc(*V2.step("rstd"))
                dve.wait_ge(*V2.after("rstd"))
                for t in range(TT):
                    dve.wait_ge(lower_row, t + 1)
                    nc.vector.scalar_tensor_tensor(y[:, t, :], y[:, t, :], ss[:, 0, t:t + 1], x_tok[:, t, :], ALU.mult, ALU.add).then_inc(*V2.step(f"out{t}"))


def lay_out(inputs):
    f = {k: np.asarray(v) for k, v in inputs.items()}

    def cols(w, c0, n):
        k = w.shape[0] // P
        return w[:, c0:c0 + n * P].reshape(k, P, n, P).transpose(2, 1, 0, 3)

    w_in = f["w_in_mix"][0]
    sc, qkv, z, ab = 0, 1536, 3072, 3584
    gates = 3600
    b_t, c_t, x_t = (cols(w_in, sc + 512 * n, 4) for n in range(3))
    sc_tiles = np.stack([c_t, x_t, b_t], 1).reshape(12, P, KT, P)
    g_sc, g_dn = cols(w_in, gates, KT), cols(w_in, gates + D, KT)
    branches = np.concatenate([cols(f["w_sc_out"][0], 0, KT), cols(f["w_dn_out"][0], 0, KT)], axis=2)
    merge = np.stack([g_sc, g_dn, branches], 1).reshape(3 * KT, P, KT, P)
    _, wide, narrow = constants()
    r = {
        "x": f["x"][0],
        "c_row": np.broadcast_to(f["c"], (P, D)),
        "w_ada": f["w_ada"][0].T.reshape(MOD, P, D),
        "b_ada": f["b_ada"][0].reshape(MOD, P).T,
        "norms": np.stack([f[n][0].reshape(KT, P).T for n in ("norm_pre_mix", "norm_post_mix", "norm_pre_ffn", "norm_post_ffn")], 1),
        "w_proj": np.concatenate([sc_tiles, cols(w_in, qkv, 12), cols(w_in, z, 4)], 0),
        "w_ab": w_in[:, ab:ab + 16].reshape(KT, P, 16).transpose(1, 0, 2),
        "sc_w": f["sc_conv_w"][0].reshape(3, 4, P).transpose(2, 1, 0),
        "dn_w": f["dn_conv_w"][0].reshape(4, 12, P).transpose(2, 1, 0),
        "dt_bias": f["dn_dt_bias"][0][:, None],
        "a_log": f["dn_a_log"][0][:, None],
        "out_norm": np.concatenate([f["dn_out_norm"][0]] * 2)[:, None],
        "w_merge": np.concatenate([merge, f["w_mix_out"][0].reshape(KT, P, KT, P)], 0),
        "w_q": cols(f["peer_w_q"][0], 0, 16),
        "sub_keys": f["peer_sub_keys"][0].reshape(16, P, P).transpose(2, 0, 1),
        "peer_u": f["peer_u"].reshape(P, P, KT, P).transpose(1, 3, 2, 0),
        "peer_v": f["peer_v"].reshape(P, P, D).transpose(1, 0, 2),
        "wide": wide,
        "narrow": narrow,
    }
    return {k: np.ascontiguousarray(v) for k, v in r.items()}


SPILL = (P, T // TB, P, TB)
ACTS = (N_EARLY, P, T)


def kernel(**inputs):
    import concourse.bacc as _bacc
    from concourse.bass_utils import run_bass_kernel_spmd as _run

    nc = _bacc.Bacc("TRN2", target_bir_lowering=False, num_devices=1)
    laid = lay_out(inputs)
    aps = {n: nc.dram_tensor(f"in_{n}_dram", v.shape, mybir.dt.from_np(v.dtype), kind="ExternalInput").ap() for n, v in laid.items()}
    out = nc.dram_tensor("out_dram", (T, D), F32, kind="ExternalOutput").ap()
    spill = nc.dram_tensor("gate_scratch", SPILL, F32, kind="Internal").ap()
    acts = nc.dram_tensor("gelu_scratch", ACTS, F32, kind="Internal").ap()
    program(nc, aps, out, spill, acts)
    r = _run(nc, [{f"in_{n}_dram": v for n, v in laid.items()}], core_ids=[0])
    return r.results[0]["out_dram"].reshape(1, T, D)
```
